# Optimizing a Trainium2 kernel written in Bass

```python
import jax, jax.numpy as jnp
from jax import lax
import numpy as np

D_MODEL = 1024
BATCH = 1
SEQ = 512
DEPTH = 2

HEAD_DIM = 64
GROUP_HEADS = 4
GROUP_WIDTH = GROUP_HEADS * HEAD_DIM
N_GROUPS = 4
MIX_WIDTH = N_GROUPS * GROUP_WIDTH
MLA_Q_RANK = 256
MLA_KV_RANK = 128
MLA_NOPE = 64
MLA_ROPE = 32
MLA_QK = MLA_NOPE + MLA_ROPE
MLA_V = 64
ROPE_BASE = 10000.0
Q_BLOCK = 128
MLSTM_CONV = 4
MLSTM_CHUNK = 64
FGATE_BIAS_LO = 3.0
FGATE_BIAS_HI = 6.0
SPATIAL_CHUNK = 128
CONV_WIDTH = 31
PEER_HEADS = 8
PEER_KEYS = 128
PEER_EXPERTS = PEER_KEYS * PEER_KEYS
PEER_TOPK = 16
PEER_QDIM = 128
PEER_HALF = PEER_QDIM // 2
PEER_TOKEN_BLOCK = 128
EPS = 1e-6

SPLIT_SIZES = (MLA_Q_RANK, MLA_KV_RANK, MLA_ROPE,
               GROUP_WIDTH, GROUP_WIDTH, GROUP_WIDTH, GROUP_HEADS, GROUP_HEADS,
               GROUP_WIDTH, GROUP_WIDTH,
               GROUP_WIDTH, GROUP_WIDTH)
PROJ_WIDTH = sum(SPLIT_SIZES)

kernel_name = 'hybrid_mla_mlstm_gmlp_conv_peer'

def _split_points():
    pts, acc = [], 0
    for s in SPLIT_SIZES[:-1]:
        acc += s
        pts.append(acc)
    return pts

def rmsnorm(x, g):
    xf = x.astype(jnp.float32)
    y = xf * lax.rsqrt(jnp.mean(xf * xf, axis=-1, keepdims=True) + EPS)
    return (y * g.astype(jnp.float32)).astype(x.dtype)

def layernorm(x, g, b):
    xf = x.astype(jnp.float32)
    mu = jnp.mean(xf, axis=-1, keepdims=True)
    var = jnp.mean(jnp.square(xf - mu), axis=-1, keepdims=True)
    y = (xf - mu) * lax.rsqrt(var + EPS) * g.astype(jnp.float32) + b.astype(jnp.float32)
    return y.astype(x.dtype)

def apply_rope(x, cos, sin):
    x1, x2 = x[..., :MLA_ROPE // 2], x[..., MLA_ROPE // 2:]
    return jnp.concatenate([x1 * cos - x2 * sin, x1 * sin + x2 * cos], axis=-1)

def causal_dwconv(x, w, b):
    k = w.shape[0]
    y = lax.conv_general_dilated(x, w[:, None, :].astype(x.dtype), window_strides=(1,),
                                 padding=((k - 1, 0),),
                                 dimension_numbers=('NWC', 'WIO', 'NWC'),
                                 feature_group_count=x.shape[-1])
    return y + b.astype(x.dtype)

def mla_mixer(cq, ckv, kr, cos, sin, cq_g, ckv_g, w_uq, w_ukv, qn_g, kn_g):
    bsz, s, _ = cq.shape
    q = (rmsnorm(cq, cq_g) @ w_uq).reshape(bsz, s, GROUP_HEADS, MLA_QK)
    kv = (rmsnorm(ckv, ckv_g) @ w_ukv).reshape(bsz, s, GROUP_HEADS, MLA_NOPE + MLA_V)
    k_nope, v = kv[..., :MLA_NOPE], kv[..., MLA_NOPE:]
    k_rope = jnp.broadcast_to(kr[:, :, None, :], (bsz, s, GROUP_HEADS, MLA_ROPE))
    k = jnp.concatenate([k_nope, k_rope], axis=-1)
    q = rmsnorm(q, qn_g)
    k = rmsnorm(k, kn_g)
    q = jnp.concatenate([q[..., :MLA_NOPE], apply_rope(q[..., MLA_NOPE:], cos, sin)], axis=-1)
    k = jnp.concatenate([k[..., :MLA_NOPE], apply_rope(k[..., MLA_NOPE:], cos, sin)], axis=-1)
    q = q.transpose(0, 2, 1, 3)
    k = k.transpose(0, 2, 1, 3)
    v = v.transpose(0, 2, 1, 3)
    nb = s // Q_BLOCK
    qb = jnp.moveaxis(q.reshape(bsz, GROUP_HEADS, nb, Q_BLOCK, MLA_QK), 2, 0)
    key_pos = jnp.arange(s)
    scale = MLA_QK ** -0.5

    def block(args):
        qi, start = args
        sc = jnp.einsum('bhqd,bhkd->bhqk', qi, k).astype(jnp.float32) * scale
        qpos = start + jnp.arange(Q_BLOCK)
        sc = jnp.where(key_pos[None, :] <= qpos[:, None], sc, -jnp.inf)
        p = jax.nn.softmax(sc, axis=-1).astype(v.dtype)
        return jnp.einsum('bhqk,bhkd->bhqd', p, v)

    out = lax.map(block, (qb, jnp.arange(nb) * Q_BLOCK))
    return out.transpose(1, 0, 3, 2, 4).reshape(bsz, s, GROUP_HEADS * MLA_V)

def mlstm_mixer(xqk, xv, xo, ig_pre, fg_pre, conv_w, conv_b, w_q, w_k, b_i, b_f, hn_g):
    bsz, s, _ = xqk.shape
    xc = jax.nn.silu(causal_dwconv(xqk, conv_w, conv_b)).reshape(bsz, s, GROUP_HEADS, HEAD_DIM)
    q = jnp.einsum('bshd,hde->bhse', xc, w_q).astype(jnp.float32)
    k = jnp.einsum('bshd,hde->bhse', xc, w_k).astype(jnp.float32) * (HEAD_DIM ** -0.5)
    v = xv.reshape(bsz, s, GROUP_HEADS, HEAD_DIM).transpose(0, 2, 1, 3).astype(jnp.float32)
    ig = (ig_pre + b_i).astype(jnp.float32).transpose(0, 2, 1)
    lf = jax.nn.log_sigmoid((fg_pre + b_f).astype(jnp.float32)).transpose(0, 2, 1)
    nc = s // MLSTM_CHUNK

    def chunks(t):
        return jnp.moveaxis(t.reshape(bsz, GROUP_HEADS, nc, MLSTM_CHUNK, *t.shape[3:]), 2, 0)

    tri = jnp.tril(jnp.ones((MLSTM_CHUNK, MLSTM_CHUNK), dtype=bool))

    def step(carry, inp):
        c_st, n_st, m_st = carry
        qc, kc, vc, ic, fc = inp
        bcum = jnp.cumsum(fc, axis=-1)
        dmat = jnp.where(tri, bcum[..., :, None] - bcum[..., None, :] + ic[..., None, :], -jnp.inf)
        m_inter = bcum + m_st[..., None]
        m_t = jnp.maximum(jnp.max(dmat, axis=-1), m_inter)
        w = jnp.exp(dmat - m_t[..., None]) * jnp.einsum('bhtd,bhsd->bhts', qc, kc)
        inter = jnp.exp(m_inter - m_t)
        num = jnp.einsum('bhts,bhsd->bhtd', w, vc) + inter[..., None] * jnp.einsum('bhvk,bhtk->bhtv', c_st, qc)
        den = jnp.sum(w, axis=-1) + inter * jnp.einsum('bhk,bhtk->bht', n_st, qc)
        h = num / jnp.maximum(jnp.abs(den), jnp.exp(-m_t))[..., None]
        b_last = bcum[..., -1]
        g = b_last[..., None] - bcum + ic
        m_new = jnp.maximum(b_last + m_st, jnp.max(g, axis=-1))
        decay = jnp.exp(b_last + m_st - m_new)
        wg = jnp.exp(g - m_new[..., None])
        c_new = decay[..., None, None] * c_st + jnp.einsum('bhs,bhsv,bhsk->bhvk', wg, vc, kc)
        n_new = decay[..., None] * n_st + jnp.einsum('bhs,bhsk->bhk', wg, kc)
        return (c_new, n_new, m_new), h

    init = (jnp.zeros((bsz, GROUP_HEADS, HEAD_DIM, HEAD_DIM), jnp.float32),
            jnp.zeros((bsz, GROUP_HEADS, HEAD_DIM), jnp.float32),
            jnp.zeros((bsz, GROUP_HEADS), jnp.float32))
    _, hs = lax.scan(step, init, (chunks(q), chunks(k), chunks(v), chunks(ig), chunks(lf)))
    h = jnp.moveaxis(hs, 0, 2).reshape(bsz, GROUP_HEADS, s, HEAD_DIM).transpose(0, 2, 1, 3)
    h = rmsnorm(h, hn_g).reshape(bsz, s, GROUP_WIDTH)
    return (jax.nn.sigmoid(xo.astype(jnp.float32)) * h).astype(xqk.dtype)

def spatial_gating_mixer(xu, xv, ln_g, ln_b, w_s, b_s):
    bsz, s, _ = xu.shape
    u = jax.nn.gelu(xu)
    v = layernorm(jax.nn.gelu(xv), ln_g, ln_b)
    nc = s // SPATIAL_CHUNK
    v = v.reshape(bsz, nc, SPATIAL_CHUNK, GROUP_HEADS, HEAD_DIM)
    tri = jnp.tril(jnp.ones((SPATIAL_CHUNK, SPATIAL_CHUNK), dtype=bool))
    ws = jnp.where(tri[None], w_s, 0.0).astype(v.dtype)
    sg = jnp.einsum('gts,bcsgd->bctgd', ws, v) + b_s.T[None, None, :, :, None].astype(v.dtype)
    return u * sg.reshape(bsz, s, GROUP_WIDTH)

def conv_module_mixer(xa, xb, dw_w, dw_b, cn_g, cn_b):
    bsz, s, _ = xa.shape
    y = causal_dwconv(xa * jax.nn.sigmoid(xb), dw_w, dw_b)
    y = layernorm(y.reshape(bsz, s, GROUP_HEADS, HEAD_DIM), cn_g, cn_b)
    return jax.nn.silu(y).reshape(bsz, s, GROUP_WIDTH)

def peer_ffn(x, w_pq, sub_keys, u_emb, v_emb):
    bsz, s, d = x.shape
    t = bsz * s
    xt = x.reshape(t, d)
    q = (xt @ w_pq).reshape(t, PEER_HEADS, 2, PEER_HALF)
    sc = jnp.einsum('thpd,hpnd->thpn', q, sub_keys).astype(jnp.float32)
    s1, i1 = lax.top_k(sc[:, :, 0], PEER_TOPK)
    s2, i2 = lax.top_k(sc[:, :, 1], PEER_TOPK)
    cand = (s1[..., :, None] + s2[..., None, :]).reshape(t, PEER_HEADS, PEER_TOPK * PEER_TOPK)
    top_s, top_i = lax.top_k(cand, PEER_TOPK)
    e1 = jnp.take_along_axis(i1, top_i // PEER_TOPK, axis=-1)
    e2 = jnp.take_along_axis(i2, top_i % PEER_TOPK, axis=-1)
    experts = (e1 * PEER_KEYS + e2).reshape(t, PEER_HEADS * PEER_TOPK)
    gates = jax.nn.softmax(top_s, axis=-1).reshape(t, PEER_HEADS * PEER_TOPK)
    nb = t // PEER_TOKEN_BLOCK

    def block(args):
        xb, eb, gb = args
        a = jnp.einsum('tkd,td->tk', u_emb[eb], xb).astype(jnp.float32)
        act = (jax.nn.gelu(a) * gb).astype(xb.dtype)
        return jnp.einsum('tk,tkd->td', act, v_emb[eb])

    out = lax.map(block, (xt.reshape(nb, PEER_TOKEN_BLOCK, d),
                          experts.reshape(nb, PEER_TOKEN_BLOCK, PEER_HEADS * PEER_TOPK),
                          gates.reshape(nb, PEER_TOKEN_BLOCK, PEER_HEADS * PEER_TOPK)))
    return out.reshape(bsz, s, d)

def setup_inputs(seed: int = 0) -> dict:
    key = jax.random.key(seed)
    ks = jax.random.split(key, 40)

    def nrm(k, shape, scale):
        return jax.random.normal(k, shape, jnp.float32) * scale

    def gain(k, shape):
        return 1.0 + 0.05 * jax.random.normal(k, shape, jnp.float32)

    L = DEPTH
    x = jax.random.normal(ks[0], (BATCH, SEQ, D_MODEL), jnp.float32)
    offset = jax.random.randint(ks[1], (BATCH, 1), 0, 4096, dtype=jnp.int32)
    positions = (offset + jnp.arange(SEQ, dtype=jnp.int32)[None, :]).astype(jnp.int32)
    b_f = (jnp.linspace(FGATE_BIAS_LO, FGATE_BIAS_HI, GROUP_HEADS, dtype=jnp.float32)[None, :]
           + 0.1 * jax.random.normal(ks[16], (L, GROUP_HEADS), jnp.float32))
    return {
        'x': x,
        'positions': positions,
        'norm1_g': gain(ks[2], (L, D_MODEL)),
        'w_in': nrm(ks[3], (L, D_MODEL, PROJ_WIDTH), D_MODEL ** -0.5),
        'a_cq_g': gain(ks[4], (L, MLA_Q_RANK)),
        'a_ckv_g': gain(ks[5], (L, MLA_KV_RANK)),
        'a_w_uq': nrm(ks[6], (L, MLA_Q_RANK, GROUP_HEADS * MLA_QK), MLA_Q_RANK ** -0.5),
        'a_w_ukv': nrm(ks[7], (L, MLA_KV_RANK, GROUP_HEADS * (MLA_NOPE + MLA_V)), MLA_KV_RANK ** -0.5),
        'a_qn_g': gain(ks[8], (L, MLA_QK)),
        'a_kn_g': gain(ks[9], (L, MLA_QK)),
        'b_conv_w': nrm(ks[10], (L, MLSTM_CONV, GROUP_WIDTH), MLSTM_CONV ** -0.5),
        'b_conv_b': nrm(ks[11], (L, GROUP_WIDTH), 0.02),
        'b_w_q': nrm(ks[12], (L, GROUP_HEADS, HEAD_DIM, HEAD_DIM), HEAD_DIM ** -0.5),
        'b_w_k': nrm(ks[13], (L, GROUP_HEADS, HEAD_DIM, HEAD_DIM), HEAD_DIM ** -0.5),
        'b_b_i': nrm(ks[14], (L, GROUP_HEADS), 0.1),
        'b_b_f': b_f,
        'b_hn_g': gain(ks[15], (L, GROUP_HEADS, HEAD_DIM)),
        'c_ln_g': gain(ks[17], (L, GROUP_WIDTH)),
        'c_ln_b': nrm(ks[18], (L, GROUP_WIDTH), 0.02),
        'c_w_s': nrm(ks[19], (L, GROUP_HEADS, SPATIAL_CHUNK, SPATIAL_CHUNK), SPATIAL_CHUNK ** -0.5),
        'c_b_s': 1.0 + nrm(ks[20], (L, GROUP_HEADS, SPATIAL_CHUNK), 0.02),
        'd_dw_w': nrm(ks[21], (L, CONV_WIDTH, GROUP_WIDTH), CONV_WIDTH ** -0.5),
        'd_dw_b': nrm(ks[22], (L, GROUP_WIDTH), 0.02),
        'd_cn_g': gain(ks[23], (L, GROUP_HEADS, HEAD_DIM)),
        'd_cn_b': nrm(ks[24], (L, GROUP_HEADS, HEAD_DIM), 0.02),
        'w_out': nrm(ks[25], (L, MIX_WIDTH, D_MODEL), MIX_WIDTH ** -0.5),
        'norm2_g': gain(ks[26], (L, D_MODEL)),
        'p_w_q': nrm(ks[27], (L, D_MODEL, PEER_HEADS * PEER_QDIM), D_MODEL ** -0.5),
        'p_sub_keys': nrm(ks[28], (L, PEER_HEADS, 2, PEER_KEYS, PEER_HALF), PEER_HALF ** -0.5),
        'p_u': nrm(ks[29], (L, PEER_EXPERTS, D_MODEL), D_MODEL ** -0.5),
        'p_v': nrm(ks[30], (L, PEER_EXPERTS, D_MODEL), PEER_HEADS ** -0.5),
    }

def reference(x, positions, norm1_g, w_in, a_cq_g, a_ckv_g, a_w_uq, a_w_ukv, a_qn_g, a_kn_g,
              b_conv_w, b_conv_b, b_w_q, b_w_k, b_b_i, b_b_f, b_hn_g,
              c_ln_g, c_ln_b, c_w_s, c_b_s, d_dw_w, d_dw_b, d_cn_g, d_cn_b,
              w_out, norm2_g, p_w_q, p_sub_keys, p_u, p_v):
    inv_freq = ROPE_BASE ** (-jnp.arange(0, MLA_ROPE, 2, dtype=jnp.float32) / MLA_ROPE)
    ang = positions.astype(jnp.float32)[..., None] * inv_freq
    cos = jnp.cos(ang)[:, :, None, :].astype(x.dtype)
    sin = jnp.sin(ang)[:, :, None, :].astype(x.dtype)
    split_pts = _split_points()
    for l in range(DEPTH):
        hn = rmsnorm(x, norm1_g[l])
        proj = hn @ w_in[l]
        (a_cq, a_ckv, a_kr, b_qk, b_v, b_o, b_i, b_f,
         c_u, c_v, d_a, d_b) = jnp.split(proj, split_pts, axis=-1)
        out_a = mla_mixer(a_cq, a_ckv, a_kr, cos, sin, a_cq_g[l], a_ckv_g[l],
                          a_w_uq[l], a_w_ukv[l], a_qn_g[l], a_kn_g[l])
        out_b = mlstm_mixer(b_qk, b_v, b_o, b_i, b_f, b_conv_w[l], b_conv_b[l],
                            b_w_q[l], b_w_k[l], b_b_i[l], b_b_f[l], b_hn_g[l])
        out_c = spatial_gating_mixer(c_u, c_v, c_ln_g[l], c_ln_b[l], c_w_s[l], c_b_s[l])
        out_d = conv_module_mixer(d_a, d_b, d_dw_w[l], d_dw_b[l], d_cn_g[l], d_cn_b[l])
        mix = jnp.concatenate([out_a, out_b, out_c, out_d], axis=-1)
        x = x + mix @ w_out[l]
        x = x + peer_ffn(rmsnorm(x, norm2_g[l]), p_w_q[l], p_sub_keys[l], p_u[l], p_v[l])
    return x


_drawn_inputs = setup_inputs


def setup_inputs(seed=0):
    import zlib

    import numpy as np

    out = dict(_drawn_inputs(seed))
    spreads = {}
    factors = {'a_cq_g': 3.194, 'a_qn_g': 3.027, 'a_kn_g': 2.893, 'b_b_i': 64.0, 'c_ln_b': 2.995}
    for name, (base, spread) in spreads.items():
        noise = np.random.default_rng([zlib.crc32(name.encode()), seed]).standard_normal(out[name].shape)
        drawn = base * np.exp(spread * noise) if base else spread * noise
        out[name] = __import__('jax').numpy.asarray(drawn.astype(out[name].dtype))
    for name, factor in factors.items():
        out[name] = (out[name] * factor).astype(out[name].dtype)
    return out
```

```python
from contextlib import ExitStack

import numpy as np

import concourse.bass as bass
from concourse import mybir

F32 = mybir.dt.float32
I32 = mybir.dt.int32
U32 = mybir.dt.uint32
ALU = mybir.AluOpType
ACT = mybir.ActivationFunctionType
AX = mybir.AxisListType
ds = bass.ds

P = 128
D = 1024
SEQ = 512
DEPTH = 2
BLOCKS = SEQ // P
UNITS = DEPTH * BLOCKS
KC = D // P
HEADS = 4
HD = 64
GW = HEADS * HD
NOPE, ROPE = 64, 32
QK = NOPE + ROPE
HR = ROPE // 2
QR, KVR = 256, 128
KB = 4
KD = 31
PH = 8
KEYS = 128
TOPK = 16
SLOTS = PH * TOPK
EXPERTS = KEYS * KEYS
EPS = 1e-6
LOWEST = -3.4028234663852886e38

A0, A1 = 0, QR + KVR + ROPE
Q0, Q1 = A1, A1 + GW
B0, B1 = Q1, Q1 + 2 * GW + 2 * HEADS
C0, C1 = B1, B1 + 2 * GW
D0, D1 = C1, C1 + 2 * GW
IN_CHUNKS = [(0, 128), (128, 256), (256, A1), (Q0, Q1), (B0, B0 + 256), (B0 + 256, B1),
             (C0, C0 + 256), (C0 + 256, C1), (D0, D0 + 256), (D0 + 256, D1)]
WIDTHS = [b - a for a, b in IN_CHUNKS] + [256] * 8
AFTER_A, AFTER_Q, AFTER_B, AFTER_C, AFTER_D, AFTER_OUT = 3, 4, 6, 8, 10, 14
NW = len(WIDTHS)
WSLOTS = 3
WMAX = KC * max(WIDTHS)

ROWS = [("g1", D), ("g2", D), ("qkg", 2 * QK), ("cg", GW), ("cb", GW), ("dg", GW), ("db", GW),
        ("hg", GW), ("gb", 2 * HEADS)]
ROW_AT, _n = {}, 0
for _name, _w in ROWS:
    ROW_AT[_name] = (_n, _n + _w)
    _n += _w
ROW_W = _n
COLS = [("lat", 3), ("bw", 2 * KB), ("bb", 2), ("dw", 2 * KD), ("db", 2), ("bs", HEADS)]
COL_AT, _n = {}, 0
for _name, _w in COLS:
    COL_AT[_name] = (_n, _n + _w)
    _n += _w
COL_W = _n
MATS = [("uq", 2 * HEADS * QK), ("ukv", 2 * GW), ("ws", HEADS * P), ("sk", PH * KEYS)]
MAT_AT, _n = {}, 0
for _name, _w in MATS:
    MAT_AT[_name] = (_n, _n + _w)
    _n += _w
MAT_W = _n

ARENA = A1 + 384 + 3 * P + 8 * QK + HEADS * P + SEQ
GROUP = 4
RING = 8
PAIRS = SLOTS // RING
NRS = 7
DVE_LINKS = 135
ACT_LINKS = 8


def nth(u, per, n):
    return u * per + n


def build(nc, x, positions, w_all, rows, cols, mats, bq, bk, uv, out):
    ctx = ExitStack()
    with ctx:
        def sb(name, shape, dt=F32):
            return ctx.enter_context(nc.sbuf_tensor(name, shape, dt))

        def sem(name):
            return ctx.enter_context(nc.semaphore(name))

        xs = sb("xs", [P, BLOCKS * D])
        h = sb("h", [P, D])
        xn = sb("xn", [P, D])
        xT = sb("xT", [P, D])
        mix = sb("mix", [P, D])
        wr = sb("wr", [P, WSLOTS * WMAX])
        prow = sb("prow", [P, ROW_W])
        pcol = sb("pcol", [P, COL_W])
        pmat = sb("pmat", [P, MAT_W])
        wqd = sb("wqd", [P, 2 * P])
        wkd = sb("wkd", [P, 2 * P])
        ident = sb("ident", [P, P])
        tri = sb("tri", [P, P])
        key_no = sb("key_no", [P, SEQ])
        qpos_i = sb("qpos_i", [P, UNITS], I32)
        qpos = sb("qpos", [P, UNITS])
        carry = sb("carry", [P, UNITS + 1])
        lbase = sb("lbase", [P, UNITS])
        n16 = sb("n16", [P, TOPK])
        sel = sb("sel", [HEADS, HEADS * P])
        pair_sel = sb("pair_sel", [HEADS, 2 * P])
        ones4 = sb("ones4", [HEADS, P])
        one_col = sb("one_col", [P, 1])
        pos_i = sb("pos_i", [P, BLOCKS], I32)
        pos_f = sb("pos_f", [P, BLOCKS])
        freq = sb("freq", [P, HR])
        cs = sb("cs", [P, BLOCKS * ROPE])
        csb = sb("csb", [P, ROPE])
        ms = sb("ms", [P, 4])
        var = sb("var", [P, 24])
        rs = sb("rs", [P, 24])
        rt = sb("rt", [P, 24])
        pB = sb("pB", [P, B1 - B0])
        pC = sb("pC", [P, 2 * GW])
        KT = sb("KT", [QK, HEADS * SEQ])
        V = sb("V", [P, BLOCKS * GW])
        zrow = sb("zrow", [1, P])
        yt = sb("yt", [P, GW])
        big = sb("big", [P, HEADS * SEQ])
        arena = sb("arena", [P, ARENA])

        def views(tensor, *parts):
            at = 0
            for width, parts_, dt in parts:
                v = tensor[0:parts_, at:at + width]
                yield v if dt is F32 else v.bitcast(dt)
                at += width

        pA, lat, latT, qk, qT, mask = views(
            arena, (A1 - A0, P, F32), (QR + KVR, P, F32), (3 * P, P, F32), (8 * QK, P, F32), (HEADS * P, QK, F32),
            (SEQ, P, F32))
        qk_sq, rp = views(big, (8 * QK, P, F32), (4 * 8 * HR, P, F32))
        gr, wgv, nd, t1, hh, yd, exo = views(
            arena, (8 * P, HEADS, F32), (HEADS * (HD + 1), P, F32), (HEADS * (HD + 1), P, F32),
            (HEADS * (HD + 1), P, F32), (GW, P, F32), (2 * P, P, F32), (GW, P, F32))
        Dm, qkTb, ktok, yb, eb, xcT = views(
            big, (HEADS * P, P, F32), (4 * P, P, F32), (GW, P, F32), (2 * P, P, F32), (2 * P, P, F32), (2 * P, P, F32))
        n_ = 2 * PH * TOPK
        (s_top, i_top, if_top, swk, c_top, ci_top, c_hi, c_lo, f_hi, f_lo, e1, e2, eg) = views(
            arena, (n_, P, F32), (n_, P, U32), (n_, P, F32), (TOPK * TOPK, P, F32), (SLOTS, P, F32), (SLOTS, P, U32),
            (SLOTS, P, U32), (SLOTS, P, U32), *[(SLOTS, P, F32)] * 5)
        key_i, ang, ang_n, ang_c = views(big, (SEQ, P, I32), *[(BLOCKS * HR, P, F32)] * 3)
        ebd = yt
        mx = sb("mx", [P, HEADS])
        psum_p = sb("psum_p", [P, HEADS])
        rsum_p = sb("rsum_p", [P, HEADS])
        cbuf = sb("cbuf", [P, 2 * (KB - 1 + P)])
        gl = sb("gl", [P, 5 * 2 * HEADS])
        m_st = sb("m_st", [HEADS, 1])
        gc = sb("gc", [P, 24])
        v1 = sb("v1", [P, HEADS * (HD + 1)])
        den = sb("den", [P, HEADS])
        Cst = sb("Cst", [P, 2 * (HD + 1)])
        bn = sb("bn", [P, HEADS * 6])
        mv = sb("mv", [P, HEADS * 2])
        vn = sb("vn", [P, GW])
        glu = sb("glu", [P, 2 * (KD - 1 + P)])
        gs = sb("gs", [P, PH])
        xp = sb("xp", [P, D])
        gates = sb("gates", [P, SLOTS])
        eidx = sb("eidx", [P, SLOTS], I32)
        idxb = sb("idxb", [P, RING], I32)
        ring = sb("ring", [P, RING * 2 * D])
        dots = sb("dots", [P, RING])
        gel = sb("gel", [P, RING])
        acts = sb("acts", [P, RING])
        diag = sb("diag", [P, RING * P])
        acc = ctx.enter_context(nc.psum_tensor("acc", [P, D], F32))
        ps = ctx.enter_context(nc.psum_tensor("ps", [P, 6 * 512], F32))

        def bank(n, a=0, b=512, p0=0, p1=P):
            return ps[p0:p1, n * 512 + a:n * 512 + b]

        def row(name):
            a, b = ROW_AT[name]
            return prow[:, a:b]

        def col(name, i=None):
            a, b = COL_AT[name]
            return pcol[:, a:b] if i is None else pcol[:, a + i:a + i + 1]

        def mat(name):
            a, b = MAT_AT[name]
            return pmat[:, a:b]

        def wchunk(c):
            s = c % WSLOTS
            return wr[:, s * WMAX:s * WMAX + KC * WIDTHS[c]].rearrange("p (k n) -> p k n", k=KC)

        x_in = sem("x_in")
        tables = sem("tables")
        tables_f = sem("tables_f")
        pos_in = sem("pos_in")
        ang_ready = sem("ang_ready")
        rope_ready = sem("rope_ready")
        params_in = sem("params_in")
        w_in = [sem(f"w_in{s}") for s in range(WSLOTS)]
        chunk_done = sem("chunk_done")
        dve_link = sem("dve_link")
        act_link = sem("act_link")
        pool_link = sem("pool_link")
        h_ready = sem("h_ready")
        ms_ready = sem("ms_ready")
        var_ready = sem("var_ready")
        rs_ready = sem("rs_ready")
        xn_ready = sem("xn_ready")
        xT_ps = sem("xT_ps")
        xT_ready = sem("xT_ready")
        pA_ready = sem("pA_ready")
        pB_ready = sem("pB_ready")
        pC_ready = sem("pC_ready")
        cbuf_ready = sem("cbuf_ready")
        ebd_ready = sem("ebd_ready")
        glu_ready = sem("glu_ready")
        lat_ready = sem("lat_ready")
        latT_ps = sem("latT_ps")
        latT_ready = sem("latT_ready")
        qkv_ps = sem("qkv_ps")
        qk_evac = sem("qk_evac")
        qk_ready = sem("qk_ready")
        qkT_ps = sem("qkT_ps")
        qkT_ready = sem("qkT_ready")
        S_ps = sem("S_ps")
        mx_ready = sem("mx_ready")
        P_ready = sem("P_ready")
        PT_ps = sem("PT_ps")
        PT_ready = sem("PT_ready")
        o_ps = sem("o_ps")
        oA_done = sem("oA_done")
        yb_ready = sem("yb_ready")
        eb_ready = sem("eb_ready")
        xcT_ready = sem("xcT_ready")
        negz_ready = sem("negz_ready")
        softplus_ready = sem("softplus_ready")
        gates_ready = sem("gates_ready")
        gT_ps = sem("gT_ps")
        rows_ready = sem("rows_ready")
        EN_ready = sem("EN_ready")
        col_ps = sem("col_ps")
        y_ready = sem("y_ready")
        D_ready = sem("D_ready")
        qkb_ps = sem("qkb_ps")
        qkb_ready = sem("qkb_ready")
        SI_ps = sem("SI_ps")
        Wt_ready = sem("Wt_ready")
        wgv_ready = sem("wgv_ready")
        num_ps = sem("num_ps")
        st_ps = sem("st_ps")
        vn_ready = sem("vn_ready")
        sg_ps = sem("sg_ps")
        yd_ready = sem("yd_ready")
        ydT_ps = sem("ydT_ps")
        yt_ready = sem("yt_ready")
        eyt_ready = sem("eyt_ready")
        mix_ready = sem("mix_ready")
        h2_ready = sem("h2_ready")
        qpT_ready = sem("qpT_ready")
        sc_ps = sem("sc_ps")
        scs_ready = sem("scs_ready")
        top_ready = sem("top_ready")
        eg_ready = sem("eg_ready")
        handover = sem("handover")
        row_in = [sem(f"row_in{s}") for s in range(RING)]
        row_used = sem("row_used")
        pool_gate = sem("pool_gate")
        dve_hold = sem("dve_hold")
        pe_hold = sem("pe_hold")
        sp_hold = sem("sp_hold")
        idx_ready = sem("idx_ready")
        dot_done = sem("dot_done")
        gelu_done = sem("gelu_done")
        act_done = sem("act_done")
        diag_ready = sem("diag_ready")
        experts_ps = sem("experts_ps")
        x_done = sem("x_done")
        out_done = sem("out_done")

        TURNS = [1, 2, 1, 2, 3, 1, 2, 2, 2]
        assert sum(TURNS) == PAIRS

        def interleave(eng, stages, turn, handoff, hold=None):
            for f in stages:
                f(0)
            handoff(0)
            with eng.Fori(1, UNITS) as u:
                before = u - 1
                at = 0
                for f, n in zip(stages, TURNS):
                    f(u)
                    if hold:
                        hold()
                    if n == 1:
                        turn(before, at)
                    else:
                        with eng.Fori(at, at + n) as j:
                            turn(before, j)
                    at += n
                handoff(u)
            with eng.Fori(0, PAIRS) as j:
                turn(UNITS - 1, j)
            handoff(UNITS)

        block = ctx.enter_context(nc.Block())

        @block.sync
        def _(sp):
            sp.dma_start(pos_i[:, :], positions.rearrange("a (b p) -> p (a b)", p=P),
                         allow_slow_non_contiguous=True).then_inc(pos_in, 16)
            sp.dma_start(xs[:, :].rearrange("p (b d) -> p b d", b=BLOCKS),
                         x.rearrange("a (b p) d -> p (a b) d", p=P)).then_inc(x_in, 16)

            def loads(u):
                layer = u // BLOCKS
                if u is not 0:
                    sp.wait_ge(sc_ps, u)
                    sp.sem_inc(sp_hold, 1)
                    sp.wait_ge(xn_ready, u * 2)
                    sp.sem_inc(sp_hold, 1)
                else:
                    sp.wait_ge(tables, 2)
                one = ds(layer, 1)
                sp.dma_start(prow[:, :], rows[one, :].to_broadcast([P, ROW_W])).then_inc(params_in, 16)
                sp.dma_start(pcol[:, :], cols[one, :, :].rearrange("a p n -> (a p) n")).then_inc(params_in, 16)
                sp.dma_start(pmat[:, :], mats[one, :, :].rearrange("a p n -> (a p) n")).then_inc(params_in, 16)
                for tile, src in ((wqd, bq), (wkd, bk)):
                    for half in range(2):
                        p0 = half * HD
                        dst = tile[p0:p0 + HD, :].rearrange("p (j n) -> p j n", j=2)[:, :, p0:p0 + HD]
                        sp.dma_start(dst, src[one, half, :, :].rearrange("a p (j n) -> (a p) j n", j=2)) \
                            .then_inc(params_in, 16)
                for c in range(NW):
                    if u is not 0 or c >= WSLOTS:
                        sp.wait_ge(chunk_done, nth(u, NW, c + 1 - WSLOTS))
                        sp.sem_inc(sp_hold, 1)
                    n = KC * WIDTHS[c]
                    s = c % WSLOTS
                    at = sum(KC * P * w for w in WIDTHS[:c])
                    src = w_all[one, at:at + P * n].rearrange("a (p n) -> (a p) n", p=P)
                    sp.dma_start(wr[:, s * WMAX:s * WMAX + n], src).then_inc(w_in[s], 16)

            loads(0)
            with sp.Fori(1, UNITS) as u:
                loads(u)
            o = out.rearrange("a (b p) d -> p (a b) d", p=P)
            xv = xs[:, :].rearrange("p (b d) -> p b d", b=BLOCKS)
            sp.wait_ge(x_done, UNITS - 1)
            sp.dma_start(o[:, 0:BLOCKS - 1, :], xv[:, 0:BLOCKS - 1, :]).then_inc(out_done, 16)
            sp.wait_ge(x_done, UNITS)
            sp.dma_start(o[:, BLOCKS - 1, :], xv[:, BLOCKS - 1, :]).then_inc(out_done, 16)
            sp.wait_ge(out_done, 32)

        @block.gpsimd
        def _(pool):
            nc.gpsimd.memset(wqd[:, :], 0.0).then_inc(tables, 1)
            nc.gpsimd.memset(wkd[:, :], 0.0).then_inc(tables, 1)
            nc.gpsimd.memset(ident[:, :], 0.0)
            nc.gpsimd.memset(tri[:, :], 1.0)
            nc.gpsimd.memset(sel[:, :], 0.0)
            nc.gpsimd.memset(pair_sel[:, :], 0.0)
            nc.gpsimd.memset(carry[:, :], 1.0)
            nc.gpsimd.memset(lbase[:, 0:BLOCKS], 0.0)
            nc.gpsimd.memset(lbase[:, BLOCKS:UNITS], float(EXPERTS)).then_inc(pool_link, 1)
            pool.wait_ge(pool_link, 1)
            for b in range(0, UNITS + 1, BLOCKS):
                nc.gpsimd.memset(carry[:, b:b + 1], 0.0)
            nc.gpsimd.affine_select(out=ident[:, :], in_=ident[:, :], compare_op=ALU.not_equal, fill=1.0, base=0,
                                    pattern=[[-1, P]], channel_multiplier=1)
            nc.gpsimd.affine_select(out=tri[:, :], in_=tri[:, :], compare_op=ALU.is_ge, fill=0.0, base=0,
                                    pattern=[[1, P]], channel_multiplier=-1)
            for t, n in ((sel, P), (pair_sel, HD)):
                v = t[:, :].rearrange("p (h n) -> p h n", h=HEADS)
                nc.gpsimd.affine_select(out=v, in_=v, compare_op=ALU.not_equal, fill=1.0, base=0,
                                        pattern=[[-1, HEADS], [0, n]], channel_multiplier=1)
            nc.gpsimd.iota(key_i[:, :], pattern=[[1, SEQ]], base=0, channel_multiplier=0)
            nc.gpsimd.iota(qpos_i[:, :], pattern=[[0, DEPTH], [P, BLOCKS]], base=0, channel_multiplier=1)
            for j in range(HR):
                f = np.float32(10000.0) ** (np.float32(-2 * j) / np.float32(ROPE))
                nc.gpsimd.memset(freq[:, j:j + 1], float(f))
            nc.gpsimd.memset(ones4[:, :], 1.0)
            nc.gpsimd.memset(zrow[:, :], 0.0)
            nc.gpsimd.memset(one_col[:, :], 1.0)
            for t in (KT, V, cbuf, glu, Cst, m_st):
                nc.gpsimd.memset(t[:, :], 0.0)
            nc.gpsimd.memset(v1[:, :], 1.0).then_inc(tables, 1)

            def turn(u, j):
                for q in range(RING // GROUP):
                    at = j * RING + q * GROUP
                    pool.wait_ge(row_used, nth(u, SLOTS, at + GROUP))
                    pool.sem_inc(pool_gate, 1)
                    nc.gpsimd.tensor_copy(idxb[:, q * GROUP:(q + 1) * GROUP],
                                          eidx[:, ds(at, GROUP)]).then_inc(idx_ready, 1)
                    pool.wait_ge(idx_ready, nth(u, SLOTS // GROUP, j * (RING // GROUP) + q + 1))
                    for g in range(GROUP):
                        s = q * GROUP + g
                        pool.wait_ge(row_used, nth(u, SLOTS, at + g + 1))
                        pool.sem_inc(pool_gate, 1)
                        nc.gpsimd.indirect_dma_start(
                            out=ring[:, s * 2 * D:(s + 1) * 2 * D], out_offset=None, in_=uv[:, :],
                            in_offset=bass.IndirectOffsetOnAxis(ap=idxb[:, s:s + 1], axis=0),
                        ).then_inc(row_in[s], 16)

            def nothing(u):
                pass

            def handoff(u):
                if u is not UNITS:
                    pool.wait_ge(handover, nth(u, 2, 2))
                    pool.sem_inc(pool_gate, 1)

            interleave(pool, [nothing] * len(TURNS), turn, handoff)

        @block.scalar
        def _(act):
            links = [0]
            sc = nc.scalar

            def link(u, ins):
                links[0] += 1
                ins.then_inc(act_link, 1)
                act.wait_ge(act_link, nth(u, ACT_LINKS, links[0]))

            def rsqrt(u, k, a, b):
                act.wait_ge(var_ready, nth(u, NRS, k))
                link(u, sc.activation(rs[:, a:b], var[:, a:b], ACT.Ln))
                sc.activation(rs[:, a:b], rs[:, a:b], ACT.Exp, scale=-0.5).then_inc(rs_ready, 1)

            def evac_xT(u, k):
                for n in range(2):
                    act.wait_ge(xT_ps, nth(u, 6, 2 * k + n + 1))
                    sc.activation(xT[:, n * 512:(n + 1) * 512], bank(n), ACT.Copy).then_inc(xT_ready, 1)

            def tables_stage():
                act.wait_ge(ang_ready, 1)
                c4 = cs[:, :].rearrange("p (b c f) -> p b c f", b=BLOCKS, c=2)
                sc.activation(c4[:, :, 0, :], ang_c[:, :].rearrange("p (b f) -> p b f", b=BLOCKS), ACT.Sin)
                sc.activation(c4[:, :, 1, :], ang[:, :].rearrange("p (b f) -> p b f", b=BLOCKS),
                              ACT.Sin).then_inc(rope_ready, 1)

            def norm1(u):
                links[0] = 0
                act.wait_ge(h_ready, nth(u, 1, 1))
                sc.activation(mix[:, :], h[:, :], ACT.Square, scale=float(D ** -0.5),
                              accum_out=ms[:, 0:1]).then_inc(ms_ready, 1)
                rsqrt(u, 1, 0, 1)
                evac_xT(u, 0)

            def project(u):
                act.wait_ge(chunk_done, nth(u, NW, AFTER_A))
                sc.activation(pA[:, :], bank(2, 0, A1 - A0), ACT.Copy).then_inc(pA_ready, 1)
                sc.activation(mix[:, 0:QR], bank(2, 0, QR), ACT.Square, scale=float(QR ** -0.5),
                              accum_out=ms[:, 1:2])
                sc.activation(mix[:, QR:QR + KVR], bank(2, QR, QR + KVR), ACT.Square, scale=float(KVR ** -0.5),
                              accum_out=ms[:, 2:3]).then_inc(ms_ready, 1)
                act.wait_ge(chunk_done, nth(u, NW, AFTER_Q))
                if u is not 0:
                    act.wait_ge(xcT_ready, u)
                sc.activation(cbuf[:, :].rearrange("p (j t) -> p j t", j=2)[:, :, KB - 1:],
                              bank(3, 0, 2 * P).rearrange("p (j t) -> p j t", j=2), ACT.Copy).then_inc(cbuf_ready, 1)
                act.wait_ge(chunk_done, nth(u, NW, AFTER_B))
                sc.activation(pB[:, 0:512], bank(4), ACT.Copy)
                sc.activation(pB[:, 512:520], bank(3, 256, 264), ACT.Copy).then_inc(pB_ready, 1)
                act.wait_ge(chunk_done, nth(u, NW, AFTER_D))
                sc.activation(ebd[:, :], bank(0, 256, 512), ACT.Exp, scale=-1.0).then_inc(ebd_ready, 1)
                rsqrt(u, 2, 1, 3)
                act.wait_ge(chunk_done, nth(u, NW, AFTER_C))
                sc.activation(pC[:, :], bank(5), ACT.Gelu_apprx_tanh).then_inc(pC_ready, 1)
                act.wait_ge(latT_ps, nth(u, 1, 1))
                for k in range(3):
                    last = sc.activation(latT[:, k * P:(k + 1) * P], bank(1, k * P, (k + 1) * P), ACT.Copy,
                                         scale=col("lat", k))
                last.then_inc(latT_ready, 1)

            def qkv(u):
                qk3 = qk[:, :].rearrange("p (h d) -> p h d", h=8)
                act.wait_ge(qkv_ps, nth(u, 2, 1))
                sc.activation(qk[:, 0:HEADS * QK], bank(2, 0, HEADS * QK), ACT.Copy)
                act.wait_ge(qkv_ps, nth(u, 2, 2))
                kv3 = bank(1).rearrange("p (h d) -> p h d", h=HEADS)
                sc.activation(qk3[:, HEADS:8, 0:NOPE], kv3[:, :, 0:NOPE], ACT.Copy).then_inc(qk_evac, 1)
                sc.activation(V[:, ds((u % BLOCKS) * GW, GW)].rearrange("p (h d) -> p h d", h=HEADS),
                              kv3[:, :, NOPE:], ACT.Copy)
                rsqrt(u, 3, 3, 11)
                act.wait_ge(qkT_ps, nth(u, 2, 1))
                sc.activation(qT[:, :], bank(2, 0, 512, 0, QK), ACT.Copy).then_inc(qkT_ready, 1)
                act.wait_ge(qkT_ps, nth(u, 2, 2))
                sc.activation(KT[:, :].rearrange("p (h t) -> p h t", h=HEADS)[:, :, ds((u % BLOCKS) * P, P)],
                              bank(1, 0, 512, 0, QK).rearrange("p (h t) -> p h t", h=HEADS),
                              ACT.Copy).then_inc(qkT_ready, 1)

            def attend(u):
                act.wait_ge(mx_ready, nth(u, 1, 1))
                for hd in range(HEADS):
                    sc.activation(big[:, hd * SEQ:(hd + 1) * SEQ], big[:, hd * SEQ:(hd + 1) * SEQ], ACT.Exp,
                                  bias=mx[:, hd:hd + 1], scale=float(QK ** -0.5),
                                  accum_out=psum_p[:, hd:hd + 1]).then_inc(P_ready, 1)
                for hd in range(HEADS):
                    act.wait_ge(PT_ps, nth(u, HEADS, hd + 1))
                    sc.activation(big[:, hd * SEQ:(hd + 1) * SEQ], bank(2 + hd), ACT.Copy).then_inc(PT_ready, 1)

            def mlstm_in(u):
                act.wait_ge(yb_ready, nth(u, 1, 1))
                act.wait_ge(pB_ready, nth(u, 1, 1))
                sc.activation(exo[:, :], pB[:, GW:2 * GW], ACT.Exp, scale=-1.0)
                sc.activation(eb[:, :], yb[:, :], ACT.Exp, scale=-1.0).then_inc(eb_ready, 1)
                act.wait_ge(negz_ready, nth(u, 1, 1))
                link(u, sc.activation(gl[:, 24:28], gl[:, 16:20], ACT.Exp))
                sc.activation(gl[:, 28:32], gl[:, 24:28], ACT.Ln, bias=one_col[:, 0:1]).then_inc(softplus_ready, 1)
                act.wait_ge(rows_ready, nth(u, 1, 1))
                sc.activation(gr[:, 6 * P:7 * P], gr[:, 4 * P:5 * P], ACT.Exp, bias=m_st[:, 0:1], scale=-1.0)
                sc.activation(gr[:, 7 * P:8 * P], gr[:, 5 * P:6 * P], ACT.Exp, scale=-1.0).then_inc(EN_ready, 1)
                act.wait_ge(qkb_ps, nth(u, 1, 1))
                sc.activation(qkTb[:, 0:2 * P], bank(3, 0, 2 * P), ACT.Copy)
                sc.activation(qkTb[:, 2 * P:4 * P], bank(3, 2 * P, 4 * P), ACT.Copy, scale=float(HD ** -0.5))
                sc.activation(ktok[:, :], bank(4, 0, GW), ACT.Copy, scale=float(HD ** -0.5)).then_inc(qkb_ready, 1)

            def mlstm_out(u):
                act.wait_ge(y_ready, nth(u, 1, 1))
                sc.activation(Dm[:, :], Dm[:, :], ACT.Exp, scale=-1.0).then_inc(D_ready, 1)
                rsqrt(u, 4, 11, 15)

            def spatial(u):
                rsqrt(u, 5, 15, 16)

            def convmod(u):
                rsqrt(u, 6, 16, 20)
                act.wait_ge(yt_ready, nth(u, 1, 1))
                sc.activation(vn[:, :], yt[:, :], ACT.Exp, scale=-1.0).then_inc(eyt_ready, 1)

            def mix_out(u):
                evac_xT(u, 1)
                act.wait_ge(h2_ready, nth(u, 1, 1))
                sc.activation(mix[:, :], h[:, :], ACT.Square, scale=float(D ** -0.5),
                              accum_out=ms[:, 3:4]).then_inc(ms_ready, 1)
                rsqrt(u, 7, 20, 21)
                evac_xT(u, 2)

            def route(u):
                for n in range(2):
                    act.wait_ge(chunk_done, nth(u, NW, AFTER_OUT + 2 * n + 2))
                    sc.activation(mix[:, n * 512:(n + 1) * 512], bank(4 + n), ACT.Copy).then_inc(qpT_ready, 1)
                act.wait_ge(sc_ps, nth(u, 1, 1))
                for n in range(4):
                    sc.activation(big[:, n * 512:(n + 1) * 512], bank(2 + n), ACT.Copy).then_inc(scs_ready, 1)
                act.wait_ge(top_ready, nth(u, 1, 1))
                sc.activation(eg[:, :], eg[:, :], ACT.Exp).then_inc(eg_ready, 1)
                assert links[0] == ACT_LINKS, links

            def turn(u, j):
                for q in range(RING // GROUP):
                    at = j * RING + q * GROUP
                    k = j * (RING // GROUP) + q + 1
                    act.wait_ge(dot_done, nth(u, SLOTS, at + GROUP))
                    sc.activation(gel[:, q * GROUP:(q + 1) * GROUP], dots[:, q * GROUP:(q + 1) * GROUP],
                                  ACT.Gelu_apprx_tanh).then_inc(gelu_done, 1)
                    act.wait_ge(act_done, nth(u, SLOTS // GROUP, k))
                    for g in range(GROUP):
                        s = q * GROUP + g
                        sc.activation(diag[:, s * P:(s + 1) * P], ident[:, :], ACT.Copy,
                                      scale=acts[:, s:s + 1]).then_inc(diag_ready, 1)

            act.wait_ge(tables, 3)
            tables_stage()
            interleave(act, [norm1, project, qkv, attend, mlstm_in, mlstm_out, spatial, convmod,
                             lambda u: (mix_out(u), route(u))], turn, lambda u: None)

        @block.tensor
        def _(pe):
            T = nc.tensor

            def transposes(src, u, k):
                for n in range(2):
                    for i in range(4):
                        c = n * 4 + i
                        last = T.transpose(bank(n, i * P, (i + 1) * P), src[:, c * P:(c + 1) * P], ident[:, :])
                    last.then_inc(xT_ps, 1)

            def wait_w(u, c):
                s = c % WSLOTS
                per = NW // WSLOTS
                pe.wait_ge(w_in[s], nth(u, 16 * per, 16 * (c // WSLOTS + 1)))

            def tokens_by(c, n0, n1, dst):
                w = wchunk(c)
                for k in range(KC):
                    last = T.matmul(dst, xT[:, k * P:(k + 1) * P], w[:, k, n0:n1], start=(k == 0), stop=(k == KC - 1))
                return last

            def channels_by(c, b, a, blocks=2):
                w = wchunk(c)
                for i in range(blocks):
                    for k in range(KC):
                        last = T.matmul(bank(b, a + i * P, a + (i + 1) * P), w[:, k, i * P:(i + 1) * P],
                                        xT[:, k * P:(k + 1) * P], start=(k == 0), stop=(k == KC - 1))
                return last

            def norm1(u):
                pe.wait_ge(xn_ready, nth(u, 2, 1))
                transposes(xn, u, 0)
                pe.wait_ge(xT_ready, nth(u, 6, 2))

            def project(u):
                at = 0
                for c in range(AFTER_A):
                    wait_w(u, c)
                    tokens_by(c, 0, WIDTHS[c], bank(2, at, at + WIDTHS[c])).then_inc(chunk_done, 1)
                    at += WIDTHS[c]
                wait_w(u, 3)
                channels_by(3, 3, 0).then_inc(chunk_done, 1)
                wait_w(u, 4)
                tokens_by(4, 0, 256, bank(4, 0, 256)).then_inc(chunk_done, 1)
                wait_w(u, 5)
                tokens_by(5, 0, 256, bank(4, 256, 512))
                pe.wait_ge(cbuf_ready, nth(u, 1, 1))
                tokens_by(5, 256, 256 + 2 * HEADS, bank(3, 256, 256 + 2 * HEADS)).then_inc(chunk_done, 1)
                for n in range(2):
                    wait_w(u, AFTER_B + n)
                    tokens_by(AFTER_B + n, 0, 256, bank(5, n * 256, (n + 1) * 256)).then_inc(chunk_done, 1)
                for n in range(2):
                    wait_w(u, AFTER_C + n)
                    channels_by(AFTER_C + n, 0, n * 256).then_inc(chunk_done, 1)
                pe.wait_ge(lat_ready, nth(u, 1, 1))
                for k in range(3):
                    last = T.transpose(bank(1, k * P, (k + 1) * P), lat[:, k * P:(k + 1) * P], ident[:, :])
                last.then_inc(latT_ps, 1)

            def qkv(u):
                pe.wait_ge(latT_ready, nth(u, 1, 1))
                for k in range(2):
                    last = T.matmul(bank(2, 0, HEADS * QK), latT[:, k * P:(k + 1) * P],
                                    mat("uq")[:, k * HEADS * QK:(k + 1) * HEADS * QK], start=(k == 0), stop=(k == 1))
                last.then_inc(qkv_ps, 1)
                T.matmul(bank(1), latT[:, 2 * P:3 * P], mat("ukv"), start=True, stop=True).then_inc(qkv_ps, 1)
                pe.wait_ge(qk_ready, nth(u, 1, 1))
                for n in range(2):
                    for hd in range(HEADS):
                        c = n * HEADS + hd
                        last = T.transpose(bank(2 - n, hd * P, (hd + 1) * P, 0, QK), qk[:, c * QK:(c + 1) * QK],
                                           ident[:, :])
                    last.then_inc(qkT_ps, 1)

            def attend(u):
                pe.wait_ge(qkT_ready, nth(u, 2, 2))
                pe.wait_ge(pC_ready, nth(u, 1, 1))
                for hd in range(HEADS):
                    last = T.matmul(bank(2 + hd), qT[:, hd * P:(hd + 1) * P], KT[:, hd * SEQ:(hd + 1) * SEQ],
                                    start=True, stop=True)
                last.then_inc(S_ps, 1)
                for hd in range(HEADS):
                    pe.wait_ge(P_ready, nth(u, HEADS, hd + 1))
                    for k in range(BLOCKS):
                        last = T.transpose(bank(2 + hd, k * P, (k + 1) * P),
                                           big[:, hd * SEQ + k * P:hd * SEQ + (k + 1) * P], ident[:, :])
                    last.then_inc(PT_ps, 1)
                for hd in range(HEADS):
                    pe.wait_ge(PT_ready, nth(u, HEADS, hd + 1))
                    for k in range(BLOCKS):
                        last = T.matmul(bank(1, hd * HD, (hd + 1) * HD),
                                        big[:, hd * SEQ + k * P:hd * SEQ + (k + 1) * P],
                                        V[:, k * GW + hd * HD:k * GW + (hd + 1) * HD],
                                        start=(k == 0), stop=(k == BLOCKS - 1))
                last.then_inc(o_ps, 1)

            def mlstm_in(u):
                pe.wait_ge(xcT_ready, nth(u, 1, 1))
                for j in range(2):
                    T.matmul(bank(3, j * P, (j + 1) * P), wqd[:, j * P:(j + 1) * P], xcT[:, j * P:(j + 1) * P],
                             start=True, stop=True)
                    T.matmul(bank(3, (2 + j) * P, (3 + j) * P), wkd[:, j * P:(j + 1) * P],
                             xcT[:, j * P:(j + 1) * P], start=True, stop=True)
                    last = T.matmul(bank(4, j * P, (j + 1) * P), xcT[:, j * P:(j + 1) * P],
                                    wkd[:, j * P:(j + 1) * P], start=True, stop=True)
                last.then_inc(qkb_ps, 1)
                pe.wait_ge(gates_ready, nth(u, 1, 1))
                T.transpose(bank(0, 0, P, 0, HEADS), gl[:, 8:12], ident[:, :])
                T.transpose(bank(0, P, 2 * P, 0, HEADS), gl[:, 36:40], ident[:, :]).then_inc(gT_ps, 1)
                pe.wait_ge(EN_ready, nth(u, 1, 1))
                pe.sem_inc(pe_hold, 1)
                for i, r in enumerate((3, 6, 7)):
                    T.transpose(bank(0, 4 * i, 4 * i + 4), gr[:, r * P:(r + 1) * P], ident[0:HEADS, 0:HEADS])
                for j in range(2):
                    T.matmul(bank(0, 16 + j, 17 + j), pair_sel[:, j * P:(j + 1) * P], gr[:, 7 * P - 1:7 * P],
                             start=True, stop=True)
                for hd in range(HEADS):
                    last = T.matmul(bank(2, hd * P, (hd + 1) * P), sel[:, hd * P:(hd + 1) * P],
                                    gr[:, 4 * P:5 * P], start=True, stop=True)
                last.then_inc(col_ps, 1)

            def mlstm_out(u):
                pe.wait_ge(qkb_ready, nth(u, 1, 1))
                pe.wait_ge(y_ready, nth(u, 1, 1))
                v = HD + 1
                for hd in range(HEADS):
                    j, p0 = hd // 2, hd % 2 * HD
                    T.matmul(bank((5, 3)[hd % 2], j * P, (j + 1) * P), qkTb[p0:p0 + HD, (2 + j) * P:(3 + j) * P],
                             qkTb[p0:p0 + HD, j * P:(j + 1) * P], start=True, stop=True)
                    last = T.matmul(bank((4, 2)[hd % 2], j * v, (j + 1) * v), qkTb[p0:p0 + HD, j * P:(j + 1) * P],
                                    Cst[p0:p0 + HD, j * v:(j + 1) * v], start=True, stop=True)
                last.then_inc(SI_ps, 1)
                pe.wait_ge(Wt_ready, nth(u, 1, 1))
                for hd in range(HEADS):
                    last = T.matmul(bank(0, hd * v, (hd + 1) * v), Dm[:, hd * P:(hd + 1) * P],
                                    v1[:, hd * v:(hd + 1) * v], start=True, stop=True)
                last.then_inc(num_ps, 1)
                pe.wait_ge(wgv_ready, nth(u, 1, 1))
                for j in range(2):
                    last = T.matmul(bank(1, j * 2 * v, (j + 1) * 2 * v), ktok[:, j * P:(j + 1) * P],
                                    wgv[:, j * 2 * v:(j + 1) * 2 * v], start=True, stop=True)
                last.then_inc(st_ps, 1)

            def spatial(u):
                pe.wait_ge(vn_ready, nth(u, 1, 1))
                for hd in range(HEADS):
                    last = T.matmul(bank(5, hd * HD, (hd + 1) * HD), mat("ws")[:, hd * P:(hd + 1) * P],
                                    vn[:, hd * HD:(hd + 1) * HD], start=True, stop=True)
                last.then_inc(sg_ps, 1)

            def convmod(u):
                pe.wait_ge(yd_ready, nth(u, 1, 1))
                for j in range(2):
                    last = T.transpose(bank(4, j * P, (j + 1) * P), yd[:, j * P:(j + 1) * P], ident[:, :])
                last.then_inc(ydT_ps, 1)

            def mix_out(u):
                pe.wait_ge(mix_ready, nth(u, 1, 1))
                transposes(mix, u, 1)
                pe.wait_ge(xT_ready, nth(u, 6, 4))
                for n in range(4):
                    wait_w(u, AFTER_D + n)
                    tokens_by(AFTER_D + n, 0, 256, bank(2 + n // 2, n % 2 * 256, n % 2 * 256 + 256)) \
                        .then_inc(chunk_done, 1)
                pe.wait_ge(xn_ready, nth(u, 2, 2))
                transposes(xn, u, 2)
                pe.wait_ge(xT_ready, nth(u, 6, 6))

            def route(u):
                for n in range(4):
                    wait_w(u, AFTER_OUT + n)
                    channels_by(AFTER_OUT + n, 4 + n // 2, n % 2 * 256).then_inc(chunk_done, 1)
                pe.wait_ge(qpT_ready, nth(u, 2, 2))
                for hd in range(PH):
                    for half in range(2):
                        p0 = half * HD
                        i = half * PH + hd
                        last = T.matmul(bank(2 + i // 4, i % 4 * P, (i % 4 + 1) * P),
                                        mix[p0:p0 + HD, hd * P:(hd + 1) * P],
                                        mat("sk")[p0:p0 + HD, hd * KEYS:(hd + 1) * KEYS], start=True, stop=True)
                last.then_inc(sc_ps, 1)

            def turn(u, j):
                for s in range(RING):
                    pe.wait_ge(diag_ready, nth(u, SLOTS, j * RING + s + 1))
                    for n in range(2):
                        a = s * 2 * D + D + n * 512
                        last = T.matmul(acc[:, n * 512:(n + 1) * 512], diag[:, s * P:(s + 1) * P],
                                        ring[:, a:a + 512], start=False, stop=False, skip_group_check=True)
                    last.then_inc(row_used, 1)

            def handoff(u):
                if u is not 0:
                    T.matmul(acc[:, 0:1], zrow[:, 0:P], zrow[:, 0:1], start=False, stop=False,
                             skip_group_check=True).then_inc(experts_ps, 1)
                if u is not UNITS:
                    pe.wait_ge(handover, nth(u, 2, 2))
                    for n in range(2):
                        T.matmul(acc[:, n * 512:(n + 1) * 512], zrow[:, 0:P], key_no[0:1, :], start=True, stop=False,
                                 skip_group_check=True)

            pe.sem_inc(row_used, RING)
            pe.wait_ge(tables, 3)
            interleave(pe, [norm1, project, qkv, attend, mlstm_in, mlstm_out, spatial, convmod,
                            lambda u: (mix_out(u), route(u))], turn, handoff)

        @block.vector
        def _(dve):
            V_ = nc.vector
            links, of_setup = [0], [0]

            def link(u, ins, held=False):
                links[0] += 1
                ins.then_inc(dve_link, 1)
                dve.wait_ge(dve_link, nth(u, DVE_LINKS, of_setup[0] + links[0]))
                if held:
                    hold()

            def hold():
                dve.sem_inc(dve_hold, 1)

            def rsqrt(u, k, a, b):
                dve.wait_ge(rs_ready, nth(u, NRS, k))
                v, r, t = var[:, a:b], rs[:, a:b], rt[:, a:b]
                link(u, V_.tensor_tensor(t, r, r, ALU.mult))
                link(u, V_.tensor_tensor(t, t, v, ALU.mult))
                link(u, V_.tensor_scalar(t, t, -0.5, 1.5, ALU.mult, ALU.add))
                link(u, V_.tensor_tensor(r, r, t, ALU.mult))

            def sigmoid_mul(u, dst, e, other):
                link(u, V_.tensor_scalar(e, e, 1.0, None, ALU.add))
                link(u, V_.reciprocal(e, e))
                return V_.tensor_tensor(dst, other, e, ALU.mult)

            def heads(ap, n=HEADS):
                return ap.rearrange("p (h d) -> p h d", h=n)

            def over(ap, n, d):
                return ap.unsqueeze(2).to_broadcast([P, n, d])

            def setup():
                dve.wait_ge(tables, 3)
                V_.tensor_copy(key_no[:, :], key_i[:, :])
                V_.tensor_copy(n16[:, :], key_i[:, 0:TOPK])
                V_.tensor_copy(qpos[:, :], qpos_i[:, :]).then_inc(tables_f, 1)
                dve.wait_ge(pos_in, 16)
                link(0, V_.tensor_copy(pos_f[:, :], pos_i[:, :]))
                two_pi = 2.0 * np.pi
                p1 = 6.28125
                p2 = float(np.round((two_pi - p1) * 2.0 ** 21) / 2.0 ** 21)
                p3 = float(two_pi - p1 - p2)
                a3 = ang[:, :].rearrange("p (b f) -> p b f", b=BLOCKS)
                link(0, V_.tensor_tensor(a3, pos_f[:, :].unsqueeze(2).to_broadcast([P, BLOCKS, HR]),
                                         freq[:, :].unsqueeze(1).to_broadcast([P, BLOCKS, HR]), ALU.mult))
                magic = 1.5 * 2.0 ** 23
                link(0, V_.tensor_scalar(ang_n[:, :], ang[:, :], float(1 / two_pi), None, ALU.mult))
                link(0, V_.tensor_scalar(ang_n[:, :], ang_n[:, :], magic, None, ALU.add))
                link(0, V_.tensor_scalar(ang_n[:, :], ang_n[:, :], -magic, None, ALU.add))
                for part in (p1, p2, p3):
                    link(0, V_.scalar_tensor_tensor(ang[:, :], ang_n[:, :], -part, ang[:, :], ALU.mult, ALU.add))
                pi = 3.1415925
                link(0, V_.tensor_scalar(ang[:, :], ang[:, :], pi, -pi, ALU.min, ALU.max))
                link(0, V_.scalar_tensor_tensor(ang_c[:, :], ang[:, :], -1.0, ang[:, :], ALU.mult, ALU.max))
                link(0, V_.tensor_scalar(ang_c[:, :], ang_c[:, :], -1.0, float(np.pi / 2), ALU.mult, ALU.add))
                V_.tensor_copy(rt[:, 0:1], ang[:, 0:1]).then_inc(ang_ready, 1)
                dve.wait_ge(rope_ready, 1)
                link(0, V_.tensor_copy(rt[:, 0:1], cs[:, 0:1]))
                link(0, V_.tensor_copy(rt[:, 0:1], cs[:, 0:1]))
                of_setup[0] = links[0]
                dve.wait_ge(tables_f, 1)
                dve.wait_ge(x_in, 16)

            def norm1(u):
                links[0] = 0
                dve.wait_ge(params_in, nth(u, 16 * 7, 16 * 7))
                hold()
                V_.tensor_copy(csb[:, :], cs[:, ds((u % BLOCKS) * ROPE, ROPE)])
                V_.tensor_copy(h[:, :], xs[:, ds((u % BLOCKS) * D, D)]).then_inc(h_ready, 1)
                V_.tensor_scalar(mask[:, :], key_no[:, :], qpos[:, ds(u, 1)], -1e30, ALU.is_gt, ALU.mult)
                dve.wait_ge(ms_ready, nth(u, 3, 1))
                V_.tensor_scalar(var[:, 0:1], ms[:, 0:1], EPS, None, ALU.add).then_inc(var_ready, 1)
                rsqrt(u, 1, 0, 1)
                V_.scalar_tensor_tensor(xn[:, :], h[:, :], rs[:, 0:1], row("g1"), ALU.mult,
                                        ALU.mult).then_inc(xn_ready, 1)

            def project(u):
                dve.wait_ge(ms_ready, nth(u, 3, 2))
                V_.tensor_scalar(var[:, 1:3], ms[:, 1:3], EPS, None, ALU.add).then_inc(var_ready, 1)
                kr = pA[:, QR + KVR:A1]
                V_.tensor_copy(heads(qk[:, :], 8)[:, HEADS:8, NOPE:],
                               kr.unsqueeze(1).to_broadcast([P, HEADS, ROPE]))
                dve.wait_ge(ebd_ready, nth(u, 1, 1))
                link(u, V_.tensor_scalar(ebd[:, :], ebd[:, :], 1.0, None, ALU.add))
                link(u, V_.reciprocal(ebd[:, :], ebd[:, :]))
                V_.tensor_tensor(glu[:, :].rearrange("p (j t) -> p j t", j=2)[:, :, KD - 1:],
                                 bank(0, 0, 2 * P).rearrange("p (j t) -> p j t", j=2),
                                 ebd[:, :].rearrange("p (j t) -> p j t", j=2), ALU.mult).then_inc(glu_ready, 1)
                rsqrt(u, 2, 1, 3)
                V_.tensor_scalar(lat[:, 0:QR], pA[:, 0:QR], rs[:, 1:2], None, ALU.mult)
                V_.tensor_scalar(lat[:, QR:], pA[:, QR:QR + KVR], rs[:, 2:3], None, ALU.mult) \
                    .then_inc(lat_ready, 1)

            def qkv(u):
                dve.wait_ge(qk_evac, nth(u, 1, 1))
                q3 = heads(qk[:, :], 8)
                link(u, V_.tensor_tensor(qk_sq[:, :], qk[:, :], qk[:, :], ALU.mult))
                link(u, V_.tensor_reduce(rt[:, 3:11], heads(qk_sq[:, :], 8), AX.X, ALU.add))
                V_.tensor_scalar(var[:, 3:11], rt[:, 3:11], 1.0 / QK, EPS, ALU.mult, ALU.add).then_inc(var_ready, 1)
                rsqrt(u, 3, 3, 11)
                link(u, V_.tensor_tensor(q3, q3, over(rs[:, 3:11], 8, QK), ALU.mult))
                q4 = qk[:, :].rearrange("p (g h d) -> p g h d", g=2, h=HEADS)
                g4 = row("qkg").rearrange("p (g d) -> p g d", g=2).unsqueeze(2).to_broadcast([P, 2, HEADS, QK])
                link(u, V_.tensor_tensor(q4, q4, g4, ALU.mult))
                x1, x2 = q3[:, :, NOPE:NOPE + HR], q3[:, :, NOPE + HR:]
                cos = csb[:, 0:HR].unsqueeze(1).to_broadcast([P, 8, HR])
                sin = csb[:, HR:].unsqueeze(1).to_broadcast([P, 8, HR])
                r = [heads(rp[:, i * 8 * HR:(i + 1) * 8 * HR], 8) for i in range(4)]
                V_.tensor_tensor(r[0], x1, cos, ALU.mult)
                V_.tensor_tensor(r[1], x2, sin, ALU.mult)
                V_.tensor_tensor(r[2], x1, sin, ALU.mult)
                link(u, V_.tensor_tensor(r[3], x2, cos, ALU.mult))
                V_.tensor_tensor(x1, r[0], r[1], ALU.subtract)
                V_.tensor_tensor(x2, r[2], r[3], ALU.add).then_inc(qk_ready, 1)

            def attend(u):
                dve.wait_ge(S_ps, nth(u, 1, 1))
                b3 = heads(big[:, :])
                link(u, V_.tensor_tensor(b3, ps[:, 2 * 512:6 * 512].rearrange("p (h t) -> p h t", h=HEADS),
                                         mask[:, :].unsqueeze(1).to_broadcast([P, HEADS, SEQ]), ALU.add))
                link(u, V_.tensor_reduce(mx[:, :], b3, AX.X, ALU.max))
                V_.tensor_scalar(mx[:, :], mx[:, :], -float(QK ** -0.5), None, ALU.mult).then_inc(mx_ready, 1)
                dve.wait_ge(P_ready, nth(u, HEADS, HEADS))
                link(u, V_.reciprocal(rsum_p[:, :], psum_p[:, :]))
                dve.wait_ge(o_ps, nth(u, 1, 1))
                V_.tensor_tensor(heads(mix[:, 0:GW]), heads(bank(1, 0, GW)), over(rsum_p[:, :], HEADS, HD),
                                 ALU.mult).then_inc(oA_done, 1)

            def mlstm_in(u):
                dve.wait_ge(cbuf_ready, nth(u, 1, 1))
                c3 = cbuf[:, :].rearrange("p (j t) -> p j t", j=2)
                for k in range(KB):
                    for j in range(2):
                        src, dst = c3[:, j, k:k + P], yb[:, j * P:(j + 1) * P]
                        w = col("bw", j * KB + k)
                        if k == 0:
                            last = V_.tensor_scalar(dst, src, w, col("bb", j), ALU.mult, ALU.add)
                        else:
                            last = V_.scalar_tensor_tensor(dst, src, w, dst, ALU.mult, ALU.add)
                        if k < KB - 1 and j == 1:
                            link(u, last)
                last.then_inc(yb_ready, 1)
                dve.wait_ge(yb_ready, nth(u, 1, 1))
                V_.tensor_scalar(c3[:, :, 0:KB - 1], c3[:, :, P:P + KB - 1], carry[:, ds(u + 1, 1)], None, ALU.mult)
                link(u, V_.tensor_tensor(gl[:, 8:16], pB[:, 512:520], row("gb"), ALU.add))
                z = gl[:, 12:16]
                V_.scalar_tensor_tensor(gl[:, 16:20], z, -1.0, z, ALU.mult, ALU.min).then_inc(negz_ready, 1)
                link(u, V_.tensor_scalar(gl[:, 32:36], z, 0.0, None, ALU.min))
                dve.wait_ge(softplus_ready, nth(u, 1, 1))
                V_.tensor_tensor(gl[:, 36:40], gl[:, 32:36], gl[:, 28:32], ALU.subtract).then_inc(gates_ready, 1)
                dve.wait_ge(eb_ready, nth(u, 1, 1))
                sigmoid_mul(u, xcT[:, :], eb[:, :], yb[:, :]).then_inc(xcT_ready, 1)
                dve.wait_ge(gT_ps, nth(u, 1, 1))
                g = [gr[:, i * P:(i + 1) * P] for i in range(8)]
                link(u, V_.tensor_copy(gr[:, 0:2 * P], bank(0, 0, 2 * P, 0, HEADS)))
                link(u, V_.tensor_tensor_scan(g[2], ones4[:, :], g[1], 0.0, ALU.mult, ALU.add))
                link(u, V_.tensor_tensor(g[3], g[0], g[2], ALU.subtract))
                link(u, V_.tensor_tensor_scan(g[4], g[3], g[3], m_st[:, 0:1], ALU.max, ALU.max))
                V_.tensor_tensor(g[5], g[2], g[4], ALU.add).then_inc(rows_ready, 1)
                dve.wait_ge(col_ps, nth(u, 1, 1))
                link(u, V_.tensor_copy(gc[:, 0:12], bank(0, 0, 12)))
                link(u, V_.tensor_copy(gc[:, 16:18], bank(0, 16, 18)))
                for hd in range(HEADS):
                    last = V_.tensor_scalar(Dm[:, hd * P:(hd + 1) * P], bank(2, hd * P, (hd + 1) * P),
                                            gc[:, hd:hd + 1], 0.0, ALU.subtract, ALU.max)
                last.then_inc(y_ready, 1)
                link(u, V_.tensor_copy(heads(v1[:, :])[:, :, 0:HD], heads(pB[:, 0:GW])))

            def mlstm_out(u):
                v = HD + 1
                dve.wait_ge(D_ready, nth(u, 1, 1))
                V_.tensor_tensor(heads(wgv[:, :]), heads(v1[:, :]),
                                 heads(Dm[:, :])[:, :, P - 1:P].to_broadcast([P, HEADS, v]),
                                 ALU.mult).then_inc(wgv_ready, 1)
                dve.wait_ge(SI_ps, nth(u, 1, 1))
                dve.wait_ge(wgv_ready, nth(u, 1, 1))
                def of_half(ap, half):
                    return ap.rearrange("p (j c d) -> p j c d", j=2, c=2)[:, :, half, :]

                for half, b in ((0, 5), (1, 3)):
                    d = of_half(Dm[:, :], half)
                    last = V_.tensor_tensor(d, d, bank(b, 0, 2 * P).rearrange("p (j t) -> p j t", j=2), ALU.mult)
                link(u, last)
                V_.tensor_tensor(heads(Dm[:, :]), heads(Dm[:, :]), tri[:, :].unsqueeze(1).to_broadcast([P, HEADS, P]),
                                 ALU.mult).then_inc(Wt_ready, 1)
                for half, b in ((0, 4), (1, 2)):
                    last = V_.tensor_tensor(of_half(t1[:, :], half),
                                            bank(b, 0, 2 * v).rearrange("p (j d) -> p j d", j=2),
                                            over(gc[:, 4 + half:8:2], 2, v), ALU.mult)
                link(u, last)
                dve.wait_ge(num_ps, nth(u, 1, 1))
                link(u, V_.tensor_tensor(nd[:, :], bank(0, 0, HEADS * v), t1[:, :], ALU.add))
                n3 = heads(nd[:, :])
                d3 = n3[:, :, HD:v]
                link(u, V_.scalar_tensor_tensor(den[:, :].unsqueeze(2), d3, -1.0, d3, ALU.mult, ALU.max))
                link(u, V_.tensor_tensor(den[:, :], den[:, :], gc[:, 8:12], ALU.max))
                link(u, V_.reciprocal(den[:, :], den[:, :]))
                link(u, V_.tensor_tensor(heads(hh[:, :]), n3[:, :, 0:HD], over(den[:, :], HEADS, HD), ALU.mult))
                link(u, V_.tensor_tensor(vn[:, :], hh[:, :], hh[:, :], ALU.mult))
                link(u, V_.tensor_reduce(rt[:, 11:15], heads(vn[:, :]), AX.X, ALU.add))
                V_.tensor_scalar(var[:, 11:15], rt[:, 11:15], 1.0 / HD, EPS, ALU.mult, ALU.add) \
                    .then_inc(var_ready, 1)
                dve.wait_ge(st_ps, nth(u, 1, 1))
                for j in range(2):
                    for half in range(2):
                        p0 = half * HD
                        C = Cst[p0:p0 + HD, j * v:(j + 1) * v]
                        a = (j * 2 + half) * v
                        last = V_.scalar_tensor_tensor(C, C, gc[p0:p0 + HD, 16 + j:17 + j],
                                                       bank(1, a, a + v, p0, p0 + HD), ALU.mult, ALU.add)
                link(u, last)
                V_.tensor_scalar(Cst[:, :], Cst[:, :], carry[:, ds(u + 1, 1)], None, ALU.mult)
                link(u, V_.tensor_scalar(m_st[:, :], gr[:, 6 * P - 1:6 * P], carry[0:HEADS, ds(u + 1, 1)], None,
                                         ALU.mult))
                rsqrt(u, 4, 11, 15)
                link(u, V_.tensor_tensor(heads(hh[:, :]), heads(hh[:, :]), over(rs[:, 11:15], HEADS, HD), ALU.mult))
                link(u, V_.tensor_tensor(hh[:, :], hh[:, :], row("hg"), ALU.mult))
                link(u, sigmoid_mul(u, mix[:, GW:2 * GW], exo[:, :], hh[:, :]))

            def spatial(u):
                dve.wait_ge(pC_ready, nth(u, 1, 1))
                v_in = pC[:, GW:2 * GW]
                link(u, V_.bn_stats(bn[:, 0:6], v_in), held=True)
                link(u, V_.bn_aggr(mv[:, 0:2], bn[:, 0:6]))
                V_.tensor_scalar(var[:, 15:16], mv[:, 1:2], EPS, None, ALU.add).then_inc(var_ready, 1)
                V_.tensor_tensor(heads(mat("ws")), heads(mat("ws")), tri[:, :].unsqueeze(1).to_broadcast([P, HEADS, P]),
                                 ALU.mult)
                rsqrt(u, 5, 15, 16)
                link(u, V_.tensor_scalar(vn[:, :], v_in, mv[:, 0:1], rs[:, 15:16], ALU.subtract, ALU.mult))
                link(u, V_.tensor_tensor(vn[:, :], vn[:, :], row("cg"), ALU.mult))
                V_.tensor_tensor(vn[:, :], vn[:, :], row("cb"), ALU.add).then_inc(vn_ready, 1)
                dve.wait_ge(sg_ps, nth(u, 1, 1))
                link(u, V_.tensor_tensor(heads(yt[:, :]), heads(bank(5, 0, GW)), over(col("bs"), HEADS, HD), ALU.add))
                link(u, V_.tensor_tensor(mix[:, 2 * GW:3 * GW], yt[:, :], pC[:, 0:GW], ALU.mult))

            def convmod(u):
                g3 = glu[:, :].rearrange("p (j t) -> p j t", j=2)
                for k in range(KD):
                    for j in range(2):
                        src, dst = g3[:, j, k:k + P], yd[:, j * P:(j + 1) * P]
                        w = col("dw", j * KD + k)
                        if k == 0:
                            last = V_.tensor_scalar(dst, src, w, col("db", j), ALU.mult, ALU.add)
                        else:
                            last = V_.scalar_tensor_tensor(dst, src, w, dst, ALU.mult, ALU.add)
                        if k < KD - 1 and j == 1:
                            link(u, last)
                last.then_inc(yd_ready, 1)
                dve.wait_ge(yd_ready, nth(u, 1, 1))
                link(u, V_.tensor_scalar(g3[:, :, 0:KD - 1], g3[:, :, P:P + KD - 1], carry[:, ds(u + 1, 1)], None,
                                         ALU.mult))
                dve.wait_ge(ydT_ps, nth(u, 1, 1))
                for hd in range(HEADS):
                    last = V_.bn_stats(bn[:, hd * 6:(hd + 1) * 6], bank(4, hd * HD, (hd + 1) * HD))
                link(u, last, held=True)
                for hd in range(HEADS):
                    last = V_.bn_aggr(mv[:, hd * 2:(hd + 1) * 2], bn[:, hd * 6:(hd + 1) * 6])
                link(u, last)
                m3 = mv[:, :].rearrange("p (h d) -> p h d", h=HEADS)
                V_.tensor_scalar(var[:, 16:20].unsqueeze(2), m3[:, :, 1:2], EPS, None, ALU.add).then_inc(var_ready, 1)
                rsqrt(u, 6, 16, 20)
                for hd in range(HEADS):
                    last = V_.tensor_scalar(yt[:, hd * HD:(hd + 1) * HD], bank(4, hd * HD, (hd + 1) * HD),
                                            mv[:, 2 * hd:2 * hd + 1], rs[:, 16 + hd:17 + hd], ALU.subtract, ALU.mult)
                link(u, last)
                link(u, V_.tensor_tensor(yt[:, :], yt[:, :], row("dg"), ALU.mult))
                V_.tensor_tensor(yt[:, :], yt[:, :], row("db"), ALU.add).then_inc(yt_ready, 1)
                dve.wait_ge(eyt_ready, nth(u, 1, 1))
                sigmoid_mul(u, mix[:, 3 * GW:], vn[:, :], yt[:, :]).then_inc(mix_ready, 1)

            def mix_out(u):
                dve.wait_ge(chunk_done, nth(u, NW, AFTER_OUT))
                V_.tensor_tensor(h[:, :], h[:, :], ps[:, 2 * 512:4 * 512], ALU.add).then_inc(h2_ready, 1)
                dve.wait_ge(h2_ready, nth(u, 1, 1))
                hold()
                V_.tensor_copy(xs[:, ds((u % BLOCKS) * D, D)], h[:, :])
                dve.wait_ge(ms_ready, nth(u, 3, 3))
                V_.tensor_scalar(var[:, 20:21], ms[:, 3:4], EPS, None, ALU.add).then_inc(var_ready, 1)
                rsqrt(u, 7, 20, 21)
                V_.scalar_tensor_tensor(xn[:, :], h[:, :], rs[:, 20:21], row("g2"), ALU.mult,
                                        ALU.mult).then_inc(xn_ready, 1)

            def top16(u, n, count, s_out, i_out):
                lists = range(count)
                for half in range(2):
                    def best(i):
                        return slice(i * TOPK + half * 8, i * TOPK + half * 8 + 8)

                    for i in lists:
                        last = V_.max(s_out[:, best(i)], big[:, i * n:(i + 1) * n])
                    link(u, last, held=True)
                    for i in lists:
                        last = V_.max_index(i_out[:, best(i)], s_out[:, best(i)], big[:, i * n:(i + 1) * n])
                    link(u, last, held=True)
                    if half == 0:
                        for i in lists:
                            v = big[:, i * n:(i + 1) * n]
                            last = V_.match_replace(v, s_out[:, best(i)], v, LOWEST)
                        link(u, last, held=True)

            def route(u):
                dve.wait_ge(scs_ready, nth(u, 4, 4))
                hold()
                top16(u, KEYS, 2 * PH, s_top, i_top)
                s4 = s_top[:, :].rearrange("p (c h k) -> p c h k", h=PH, c=2)
                grid = big[:, :].rearrange("p (h a b) -> p h a b", h=PH, a=TOPK)
                link(u, V_.tensor_tensor(grid, s4[:, 0, :, :].unsqueeze(3).to_broadcast([P, PH, TOPK, TOPK]),
                                         s4[:, 1, :, :].unsqueeze(2).to_broadcast([P, PH, TOPK, TOPK]), ALU.add), held=True)
                top16(u, TOPK * TOPK, PH, c_top, ci_top)
                c3 = heads(c_top[:, :], PH)
                V_.tensor_tensor(heads(eg[:, :], PH), c3, c3[:, :, 0:1].to_broadcast([P, PH, TOPK]),
                                 ALU.subtract).then_inc(top_ready, 1)
                V_.tensor_scalar(c_hi[:, :], ci_top[:, :], 4, None, ALU.logical_shift_right)
                V_.tensor_scalar(c_lo[:, :], ci_top[:, :], TOPK - 1, None, ALU.bitwise_and)
                link(u, V_.tensor_copy(if_top[:, :], i_top[:, :]))
                V_.tensor_copy(f_hi[:, :], c_hi[:, :])
                link(u, V_.tensor_copy(f_lo[:, :], c_lo[:, :]))
                i4 = if_top[:, :].rearrange("p (c h k) -> p c h k", h=PH, c=2)
                work = big[:, :].rearrange("p (s k) -> p s k", k=TOPK)
                work4 = big[:, :].rearrange("p (h s k) -> p h s k", h=PH, k=TOPK)
                for c, place, dst in ((0, f_hi, e1), (1, f_lo, e2)):
                    link(u, V_.tensor_tensor(work, place[:, :].unsqueeze(2).to_broadcast([P, SLOTS, TOPK]),
                                             n16[:, :].unsqueeze(1).to_broadcast([P, SLOTS, TOPK]), ALU.is_equal))
                    link(u, V_.tensor_tensor(work4, work4,
                                             i4[:, c, :, :].unsqueeze(2).to_broadcast([P, PH, TOPK, TOPK]), ALU.mult))
                    link(u, V_.tensor_reduce(dst[:, :], work, AX.X, ALU.add))
                link(u, V_.scalar_tensor_tensor(e1[:, :], e1[:, :], float(KEYS), e2[:, :], ALU.mult, ALU.add))
                link(u, V_.tensor_scalar(e1[:, :], e1[:, :], lbase[:, ds(u, 1)], None, ALU.add))
                dve.wait_ge(eg_ready, nth(u, 1, 1))
                link(u, V_.tensor_reduce(gs[:, :], heads(eg[:, :], PH), AX.X, ALU.add))
                link(u, V_.reciprocal(gs[:, :], gs[:, :]))
                link(u, V_.tensor_tensor(heads(eg[:, :], PH), heads(eg[:, :], PH), over(gs[:, :], PH, TOPK), ALU.mult))
                assert links[0] == DVE_LINKS, links

            def turn(u, j):
                for q in range(RING // GROUP):
                    k = j * (RING // GROUP) + q + 1
                    at = j * RING + q * GROUP
                    for g in range(GROUP):
                        s = q * GROUP + g
                        dve.wait_ge(row_in[s], nth(u, 16 * PAIRS, 16 * (j + 1)) if isinstance(j, int)
                                    else nth(u, 16 * PAIRS, j * 16 + 16))
                        V_.tensor_tensor_reduce(out=ring[:, s * 2 * D:s * 2 * D + D], in0=xp[:, :], in1=ring[:, s * 2 * D:s * 2 * D + D],
                                                scale=1.0, scalar=0.0, op0=ALU.mult, op1=ALU.add,
                                                accum_out=dots[:, s:s + 1]).then_inc(dot_done, 1)
                        dve.wait_ge(dot_done, nth(u, SLOTS, at + g + 1))
                    dve.wait_ge(gelu_done, nth(u, SLOTS // GROUP, k))
                    V_.tensor_tensor(acts[:, q * GROUP:(q + 1) * GROUP], gel[:, q * GROUP:(q + 1) * GROUP],
                                     gates[:, ds(at, GROUP)], ALU.mult).then_inc(act_done, 1)

            def handoff(u):
                if u is not 0:
                    before = u - 1
                    dve.wait_ge(experts_ps, u)
                    r = xs[:, ds((before % BLOCKS) * D, D)]
                    V_.tensor_tensor(r, r, acc[:, :], ALU.add).then_inc(x_done, 1)
                    dve.wait_ge(x_done, u)
                    hold()
                if u is not UNITS:
                    V_.tensor_copy(xp[:, :], xn[:, :])
                    V_.tensor_copy(gates[:, :], eg[:, :]).then_inc(handover, 1)
                    V_.tensor_copy(eidx[:, :], e1[:, :]).then_inc(handover, 1)
                    dve.wait_ge(handover, nth(u, 2, 2))

            setup()
            interleave(dve, [norm1, project, qkv, attend, mlstm_in, mlstm_out, spatial, convmod,
                             lambda u: (mix_out(u), route(u))], turn, handoff, hold)


def kernel(**inputs):
    import concourse.bacc as bacc
    from concourse.bass_utils import run_bass_kernel_spmd

    a = {k: np.asarray(v) for k, v in inputs.items()}
    L = DEPTH

    def chunked(w):
        return w.reshape(L, KC, P, -1).transpose(0, 2, 1, 3).reshape(L, -1)

    w_all = np.concatenate(
        [chunked(a["w_in"][:, :, lo:hi]) for lo, hi in IN_CHUNKS]
        + [chunked(a["w_out"][:, :, n * 256:(n + 1) * 256]) for n in range(4)]
        + [chunked(a["p_w_q"][:, :, n * 256:(n + 1) * 256]) for n in range(4)], axis=1)
    rows = np.concatenate(
        [a["norm1_g"], a["norm2_g"], a["a_qn_g"], a["a_kn_g"], a["c_ln_g"], a["c_ln_b"],
         a["d_cn_g"].reshape(L, GW), a["d_cn_b"].reshape(L, GW), a["b_hn_g"].reshape(L, GW),
         a["b_b_i"], a["b_b_f"]], axis=1)

    def channels(v):
        n = v.shape[1]
        return v.reshape(L, n, 2, P).transpose(0, 3, 2, 1).reshape(L, P, 2 * n)

    cols = np.concatenate(
        [a["a_cq_g"].reshape(L, 2, P).transpose(0, 2, 1), a["a_ckv_g"].reshape(L, 1, P).transpose(0, 2, 1),
         channels(a["b_conv_w"]), channels(a["b_conv_b"][:, None]), channels(a["d_dw_w"]),
         channels(a["d_dw_b"][:, None]), a["c_b_s"].transpose(0, 2, 1)], axis=2)
    mats = np.concatenate(
        [a["a_w_uq"].reshape(L, 2, P, -1).transpose(0, 2, 1, 3).reshape(L, P, -1), a["a_w_ukv"],
         a["c_w_s"].transpose(0, 3, 1, 2).reshape(L, P, -1),
         a["p_sub_keys"].transpose(0, 2, 4, 1, 3).reshape(L, P, -1)], axis=2)

    def halves(w):
        return w.reshape(L, 2, 2, HD, HD).transpose(0, 2, 3, 1, 4).reshape(L, 2, HD, 2 * HD)

    uv = np.concatenate([a["p_u"], a["p_v"]], axis=2).reshape(L * EXPERTS, 2 * D)
    arrays = {"x": a["x"], "positions": a["positions"], "w_all": w_all, "rows": rows, "cols": cols, "mats": mats,
              "bq": halves(a["b_w_q"]), "bk": halves(a["b_w_k"]), "uv": uv}
    arrays = {k: np.ascontiguousarray(v) for k, v in arrays.items()}
    nc = bacc.Bacc("TRN2", target_bir_lowering=False, num_devices=1)
    args = [nc.dram_tensor(n, v.shape, mybir.dt.from_np(v.dtype), kind="ExternalInput").ap()
            for n, v in arrays.items()]
    args.append(nc.dram_tensor("out", a["x"].shape, F32, kind="ExternalOutput").ap())
    build(nc, *args)
    return run_bass_kernel_spmd(nc, [arrays], core_ids=[0]).results[0]["out"]
```

```python
from contextlib import ExitStack

import numpy as np

import concourse.bass as bass
from concourse import mybir

F32 = mybir.dt.float32
I32 = mybir.dt.int32
U32 = mybir.dt.uint32
ALU = mybir.AluOpType
ACT = mybir.ActivationFunctionType
AX = mybir.AxisListType
ds = bass.ds

P = 128
D = 1024
SEQ = 512
DEPTH = 2
BLOCKS = SEQ // P
UNITS = DEPTH * BLOCKS
KC = D // P
HEADS = 4
HD = 64
GW = HEADS * HD
NOPE, ROPE = 64, 32
QK = NOPE + ROPE
HR = ROPE // 2
QR, KVR = 256, 128
KB = 4
KD = 31
PH = 8
KEYS = 128
TOPK = 16
SLOTS = PH * TOPK
EXPERTS = KEYS * KEYS
EPS = 1e-6
LOWEST = -3.4028234663852886e38

A0, A1 = 0, QR + KVR + ROPE
Q0, Q1 = A1, A1 + GW
B0, B1 = Q1, Q1 + 2 * GW + 2 * HEADS
C0, C1 = B1, B1 + 2 * GW
D0, D1 = C1, C1 + 2 * GW
IN_CHUNKS = [(D0, D0 + 256), (D0 + 256, D1), (0, 128), (128, 256), (256, A1), (Q0, Q1),
             (B0, B0 + 256), (B0 + 256, B1), (C0, C0 + 256), (C0 + 256, C1)]
WIDTHS = [b - a for a, b in IN_CHUNKS] + [256] * 8
AFTER_D, AFTER_A, AFTER_Q, AFTER_B, AFTER_C, AFTER_OUT = 2, 5, 6, 8, 10, 14
NW = len(WIDTHS)
WSLOTS = 3
WMAX = KC * max(WIDTHS)

ROWS = [("g1", D), ("g2", D), ("qkg", 2 * QK), ("cg", GW), ("cb", GW), ("dg", GW), ("db", GW),
        ("hg", GW), ("gb", 2 * HEADS)]
ROW_AT, _n = {}, 0
for _name, _w in ROWS:
    ROW_AT[_name] = (_n, _n + _w)
    _n += _w
ROW_W = _n
COLS = [("lat", 3), ("bw", 2 * KB), ("bb", 2), ("dw", 2 * KD), ("db", 2), ("bs", HEADS)]
COL_AT, _n = {}, 0
for _name, _w in COLS:
    COL_AT[_name] = (_n, _n + _w)
    _n += _w
COL_W = _n
MATS = [("uq", 2 * HEADS * QK), ("ukv", 2 * GW), ("ws", HEADS * P), ("sk", PH * KEYS)]
MAT_AT, _n = {}, 0
for _name, _w in MATS:
    MAT_AT[_name] = (_n, _n + _w)
    _n += _w
MAT_W = _n

ARENA = A1 + 384 + 3 * P + 8 * QK + HEADS * P + SEQ
GROUP = 4
RING = 8
PAIRS = SLOTS // RING
DVE_LINKS = 135
ACT_LINKS = 8


PER_RING = RING // GROUP
CONV_PARTS = 8
SCHEDULE = [
    "norm1",
    "pe.D0",
    "pe.D1 act.D pe.A0",
    "pe.A1 act.A dve.glu dve.conv0",
    "pe.Q act.Q dve.lat act.lat pe.lat dve.conv1",
    "dve.qk act.qk pe.B0",
    "pe.B1 act.B pe.qkT act.qkT dve.conv2 dve.conv3",
    "pe.S",
    "dve.max act.exp pe.C0",
    "pe.PV act.PT dve.conv4",
    "pe.C1 act.C dve.oA dve.qkconv act.qkconv pe.qkconv act.qkb",
    "dve.vn act.vn dve.rows act.rows pe.cols",
    "dve.decay act.decay pe.scores dve.conv5",
    "dve.weigh pe.num pe.sg dve.conv6",
    "dve.hidden act.hidden",
    "dve.sg dve.conv7 pe.ydT",
    "dve.swish act.swish pe.mixT act.mixT pe.out0",
    "pe.out1",
    "pe.out2",
    "pe.out3",
    "dve.norm2 act.norm2 pe.norm2 pe.q0",
    "pe.q1 act.q01",
    "pe.q2",
    "pe.q3 act.q23 pe.sc act.sc",
    "dve.r0",
    "dve.r1",
    "dve.r2",
    "dve.r3",
    "dve.r4",
    "dve.r5 act.gates",
    "dve.r6",
    "dve.r7",
]
assert len(SCHEDULE) == SLOTS // GROUP


def nth(u, per, n):
    return u * per + n


def build(nc, x, positions, w_all, rows, cols, mats, bq, bk, uv, out):
    ctx = ExitStack()
    with ctx:
        def sb(name, shape, dt=F32):
            return ctx.enter_context(nc.sbuf_tensor(name, shape, dt))

        def sem(name):
            return ctx.enter_context(nc.semaphore(name))

        xs = sb("xs", [P, BLOCKS * D])
        h = sb("h", [P, D])
        xn = sb("xn", [P, D])
        xT = sb("xT", [P, D])
        mix = sb("mix", [P, D])
        wr = sb("wr", [P, WSLOTS * WMAX])
        prow = sb("prow", [P, ROW_W])
        pcol = sb("pcol", [P, COL_W])
        pmat = sb("pmat", [P, MAT_W])
        wqd = sb("wqd", [P, 2 * P])
        wkd = sb("wkd", [P, 2 * P])
        ident = sb("ident", [P, P])
        tri = sb("tri", [P, P])
        key_no = sb("key_no", [P, SEQ])
        qpos_i = sb("qpos_i", [P, UNITS], I32)
        qpos = sb("qpos", [P, UNITS])
        carry = sb("carry", [P, UNITS + 1])
        lbase = sb("lbase", [P, UNITS])
        n16 = sb("n16", [P, TOPK])
        sel = sb("sel", [HEADS, HEADS * P])
        pair_sel = sb("pair_sel", [HEADS, 2 * P])
        ones4 = sb("ones4", [HEADS, P])
        one_col = sb("one_col", [P, 1])
        pos_i = sb("pos_i", [P, BLOCKS], I32)
        pos_f = sb("pos_f", [P, BLOCKS])
        freq = sb("freq", [P, HR])
        cs = sb("cs", [P, BLOCKS * ROPE])
        csb = sb("csb", [P, ROPE])
        ms = sb("ms", [P, 4])
        var = sb("var", [P, 24])
        rs = sb("rs", [P, 24])
        rt = sb("rt", [P, 24])
        pB = sb("pB", [P, B1 - B0])
        pC = sb("pC", [P, 2 * GW])
        KT = sb("KT", [QK, HEADS * SEQ])
        V = sb("V", [P, BLOCKS * GW])
        zrow = sb("zrow", [1, P])
        yt = sb("yt", [P, GW])
        big = sb("big", [P, HEADS * SEQ])
        arena = sb("arena", [P, ARENA])

        def views(tensor, *parts):
            at = 0
            for width, parts_, dt in parts:
                v = tensor[0:parts_, at:at + width]
                yield v if dt is F32 else v.bitcast(dt)
                at += width

        pA, lat, latT, qk, qT, mask = views(
            arena, (A1 - A0, P, F32), (QR + KVR, P, F32), (3 * P, P, F32), (8 * QK, P, F32), (HEADS * P, QK, F32),
            (SEQ, P, F32))
        qk_sq, rp = views(big, (8 * QK, P, F32), (4 * 8 * HR, P, F32))
        gr, wgv, nd, t1, hh, exo = views(
            arena, (8 * P, HEADS, F32), (HEADS * (HD + 1), P, F32), (HEADS * (HD + 1), P, F32),
            (HEADS * (HD + 1), P, F32), (GW, P, F32), (GW, P, F32))
        Dm, qkTb, ktok, yb, eb, xcT = views(
            big, (HEADS * P, P, F32), (4 * P, P, F32), (GW, P, F32), (2 * P, P, F32), (2 * P, P, F32), (2 * P, P, F32))
        n_ = 2 * PH * TOPK
        (s_top, i_top, if_top, swk, c_top, ci_top, c_hi, c_lo, f_hi, f_lo, e1, e2, eg) = views(
            arena, (n_, P, F32), (n_, P, U32), (n_, P, F32), (TOPK * TOPK, P, F32), (SLOTS, P, F32), (SLOTS, P, U32),
            (SLOTS, P, U32), (SLOTS, P, U32), *[(SLOTS, P, F32)] * 5)
        key_i, ang, ang_n, ang_c = views(big, (SEQ, P, I32), *[(BLOCKS * HR, P, F32)] * 3)
        ebd = yt
        yd = mix[:, 3 * GW:]
        mx = sb("mx", [P, HEADS])
        psum_p = sb("psum_p", [P, HEADS])
        rsum_p = sb("rsum_p", [P, HEADS])
        cbuf = sb("cbuf", [P, 2 * (KB - 1 + P)])
        gl = sb("gl", [P, 5 * 2 * HEADS])
        m_st = sb("m_st", [HEADS, 1])
        gc = sb("gc", [P, 24])
        v1 = sb("v1", [P, HEADS * (HD + 1)])
        den = sb("den", [P, HEADS])
        Cst = sb("Cst", [P, 2 * (HD + 1)])
        bn = sb("bn", [P, HEADS * 6])
        mv = sb("mv", [P, HEADS * 2])
        vn = sb("vn", [P, GW])
        glu = sb("glu", [P, 2 * (KD - 1 + P)])
        gs = sb("gs", [P, PH])
        xp = sb("xp", [P, D])
        gates = sb("gates", [P, SLOTS])
        eidx = sb("eidx", [P, SLOTS], I32)
        idxb = sb("idxb", [P, RING], I32)
        ring = sb("ring", [P, RING * 2 * D])
        dots = sb("dots", [P, RING])
        gel = sb("gel", [P, RING])
        acts = sb("acts", [P, RING])
        diag = sb("diag", [P, RING * P])
        acc = ctx.enter_context(nc.psum_tensor("acc", [P, D], F32))
        ps = ctx.enter_context(nc.psum_tensor("ps", [P, 6 * 512], F32))

        def bank(n, a=0, b=512, p0=0, p1=P):
            return ps[p0:p1, n * 512 + a:n * 512 + b]

        def row(name):
            a, b = ROW_AT[name]
            return prow[:, a:b]

        def col(name, i=None):
            a, b = COL_AT[name]
            return pcol[:, a:b] if i is None else pcol[:, a + i:a + i + 1]

        def mat(name):
            a, b = MAT_AT[name]
            return pmat[:, a:b]

        def wchunk(c):
            s = c % WSLOTS
            return wr[:, s * WMAX:s * WMAX + KC * WIDTHS[c]].rearrange("p (k n) -> p k n", k=KC)

        x_in = sem("x_in")
        tables = sem("tables")
        tables_f = sem("tables_f")
        pos_in = sem("pos_in")
        ang_ready = sem("ang_ready")
        rope_ready = sem("rope_ready")
        params_in = sem("params_in")
        w_in = [sem(f"w_in{s}") for s in range(WSLOTS)]
        chunk_done = sem("chunk_done")
        dve_link = sem("dve_link")
        act_link = sem("act_link")
        pool_link = sem("pool_link")
        h_ready = sem("h_ready")
        uses = ("norm1", "latents", "qk", "hidden", "spatial", "conv", "norm2")
        ms_ready = {n: sem(f"ms_{n}") for n in ("norm1", "latents", "norm2")}
        var_ready = {n: sem(f"var_{n}") for n in uses}
        rs_ready = {n: sem(f"rs_{n}") for n in uses}
        xn_ready = sem("xn_ready")
        xT_ps = sem("xT_ps")
        xT_ready = sem("xT_ready")
        pA_ready = sem("pA_ready")
        pB_ready = sem("pB_ready")
        pC_ready = sem("pC_ready")
        cbuf_ready = sem("cbuf_ready")
        ebd_ready = sem("ebd_ready")
        glu_ready = sem("glu_ready")
        lat_ready = sem("lat_ready")
        latT_ps = sem("latT_ps")
        latT_ready = sem("latT_ready")
        qkv_ps = sem("qkv_ps")
        qk_evac = sem("qk_evac")
        V_ready = sem("V_ready")
        qk_ready = sem("qk_ready")
        qkT_ps = sem("qkT_ps")
        qkT_ready = sem("qkT_ready")
        S_ps = sem("S_ps")
        mx_ready = sem("mx_ready")
        P_ready = sem("P_ready")
        PT_ps = sem("PT_ps")
        PT_ready = sem("PT_ready")
        o_ps = sem("o_ps")
        oA_done = sem("oA_done")
        yb_ready = sem("yb_ready")
        eb_ready = sem("eb_ready")
        xcT_ready = sem("xcT_ready")
        negz_ready = sem("negz_ready")
        softplus_ready = sem("softplus_ready")
        gates_ready = sem("gates_ready")
        gT_ps = sem("gT_ps")
        rows_ready = sem("rows_ready")
        EN_ready = sem("EN_ready")
        col_ps = sem("col_ps")
        y_ready = sem("y_ready")
        D_ready = sem("D_ready")
        qkb_ps = sem("qkb_ps")
        qkb_ready = sem("qkb_ready")
        SI_ps = sem("SI_ps")
        Wt_ready = sem("Wt_ready")
        wgv_ready = sem("wgv_ready")
        num_ps = sem("num_ps")
        st_ps = sem("st_ps")
        vn_ready = sem("vn_ready")
        sg_ps = sem("sg_ps")
        yd_ready = sem("yd_ready")
        ydT_ps = sem("ydT_ps")
        yt_ready = sem("yt_ready")
        eyt_ready = sem("eyt_ready")
        mix_ready = sem("mix_ready")
        h2_ready = sem("h2_ready")
        qpT_ready = sem("qpT_ready")
        sc_ps = sem("sc_ps")
        scs_ready = sem("scs_ready")
        top_ready = sem("top_ready")
        eg_ready = sem("eg_ready")
        handover = sem("handover")
        row_in = [sem(f"row_in{s}") for s in range(RING)]
        row_used = sem("row_used")
        pool_gate = sem("pool_gate")
        dve_hold = sem("dve_hold")
        pe_hold = sem("pe_hold")
        sp_hold = sem("sp_hold")
        idx_ready = sem("idx_ready")
        dot_done = sem("dot_done")
        gelu_done = sem("gelu_done")
        act_done = sem("act_done")
        diag_ready = sem("diag_ready")
        experts_ps = sem("experts_ps")
        x_done = sem("x_done")
        out_done = sem("out_done")

        def interleave(eng, pieces, turn, handoff):
            mine = [[pieces[name] for name in gap.split() if name in pieces] for gap in SCHEDULE]
            for gap in mine:
                for piece in gap:
                    piece(0)
            handoff(0)
            with eng.Fori(1, UNITS) as u:
                for group, gap in enumerate(mine):
                    for piece in gap:
                        piece(u)
                    turn(u - 1, group // PER_RING, group % PER_RING)
                handoff(u)
            with eng.Fori(0, PAIRS) as j:
                for q in range(PER_RING):
                    turn(UNITS - 1, j, q)
            handoff(UNITS)

        block = ctx.enter_context(nc.Block())

        @block.sync
        def _(sp):
            sp.dma_start(pos_i[:, :], positions.rearrange("a (b p) -> p (a b)", p=P),
                         allow_slow_non_contiguous=True).then_inc(pos_in, 16)
            sp.dma_start(xs[:, :].rearrange("p (b d) -> p b d", b=BLOCKS),
                         x.rearrange("a (b p) d -> p (a b) d", p=P)).then_inc(x_in, 16)

            def loads(u):
                layer = u // BLOCKS
                if u is not 0:
                    sp.wait_ge(sc_ps, u)
                    sp.sem_inc(sp_hold, 1)
                    sp.wait_ge(xn_ready, u * 2)
                    sp.sem_inc(sp_hold, 1)
                else:
                    sp.wait_ge(tables, 2)
                one = ds(layer, 1)
                sp.dma_start(prow[:, :], rows[one, :].to_broadcast([P, ROW_W])).then_inc(params_in, 16)
                sp.dma_start(pcol[:, :], cols[one, :, :].rearrange("a p n -> (a p) n")).then_inc(params_in, 16)
                sp.dma_start(pmat[:, :], mats[one, :, :].rearrange("a p n -> (a p) n")).then_inc(params_in, 16)
                for tile, src in ((wqd, bq), (wkd, bk)):
                    for half in range(2):
                        p0 = half * HD
                        dst = tile[p0:p0 + HD, :].rearrange("p (j n) -> p j n", j=2)[:, :, p0:p0 + HD]
                        sp.dma_start(dst, src[one, half, :, :].rearrange("a p (j n) -> (a p) j n", j=2)) \
                            .then_inc(params_in, 16)
                for c in range(NW):
                    if u is not 0 or c >= WSLOTS:
                        sp.wait_ge(chunk_done, nth(u, NW, c + 1 - WSLOTS))
                        sp.sem_inc(sp_hold, 1)
                    n = KC * WIDTHS[c]
                    s = c % WSLOTS
                    at = sum(KC * P * w for w in WIDTHS[:c])
                    src = w_all[one, at:at + P * n].rearrange("a (p n) -> (a p) n", p=P)
                    sp.dma_start(wr[:, s * WMAX:s * WMAX + n], src).then_inc(w_in[s], 16)

            loads(0)
            with sp.Fori(1, UNITS) as u:
                loads(u)
            o = out.rearrange("a (b p) d -> p (a b) d", p=P)
            xv = xs[:, :].rearrange("p (b d) -> p b d", b=BLOCKS)
            sp.wait_ge(x_done, UNITS - 1)
            sp.dma_start(o[:, 0:BLOCKS - 1, :], xv[:, 0:BLOCKS - 1, :]).then_inc(out_done, 16)
            sp.wait_ge(x_done, UNITS)
            sp.dma_start(o[:, BLOCKS - 1, :], xv[:, BLOCKS - 1, :]).then_inc(out_done, 16)
            sp.wait_ge(out_done, 32)

        @block.gpsimd
        def _(pool):
            nc.gpsimd.memset(wqd[:, :], 0.0).then_inc(tables, 1)
            nc.gpsimd.memset(wkd[:, :], 0.0).then_inc(tables, 1)
            nc.gpsimd.memset(ident[:, :], 0.0)
            nc.gpsimd.memset(tri[:, :], 1.0)
            nc.gpsimd.memset(sel[:, :], 0.0)
            nc.gpsimd.memset(pair_sel[:, :], 0.0)
            nc.gpsimd.memset(carry[:, :], 1.0)
            nc.gpsimd.memset(lbase[:, 0:BLOCKS], 0.0)
            nc.gpsimd.memset(lbase[:, BLOCKS:UNITS], float(EXPERTS)).then_inc(pool_link, 1)
            pool.wait_ge(pool_link, 1)
            for b in range(0, UNITS + 1, BLOCKS):
                nc.gpsimd.memset(carry[:, b:b + 1], 0.0)
            nc.gpsimd.affine_select(out=ident[:, :], in_=ident[:, :], compare_op=ALU.not_equal, fill=1.0, base=0,
                                    pattern=[[-1, P]], channel_multiplier=1)
            nc.gpsimd.affine_select(out=tri[:, :], in_=tri[:, :], compare_op=ALU.is_ge, fill=0.0, base=0,
                                    pattern=[[1, P]], channel_multiplier=-1)
            for t, n in ((sel, P), (pair_sel, HD)):
                v = t[:, :].rearrange("p (h n) -> p h n", h=HEADS)
                nc.gpsimd.affine_select(out=v, in_=v, compare_op=ALU.not_equal, fill=1.0, base=0,
                                        pattern=[[-1, HEADS], [0, n]], channel_multiplier=1)
            nc.gpsimd.iota(key_i[:, :], pattern=[[1, SEQ]], base=0, channel_multiplier=0)
            nc.gpsimd.iota(qpos_i[:, :], pattern=[[0, DEPTH], [P, BLOCKS]], base=0, channel_multiplier=1)
            for j in range(HR):
                f = np.float32(10000.0) ** (np.float32(-2 * j) / np.float32(ROPE))
                nc.gpsimd.memset(freq[:, j:j + 1], float(f))
            nc.gpsimd.memset(ones4[:, :], 1.0)
            nc.gpsimd.memset(zrow[:, :], 0.0)
            nc.gpsimd.memset(one_col[:, :], 1.0)
            for t in (KT, V, cbuf, glu, Cst, m_st):
                nc.gpsimd.memset(t[:, :], 0.0)
            nc.gpsimd.memset(v1[:, :], 1.0).then_inc(tables, 1)

            def turn(u, j, q):
                at = j * RING + q * GROUP
                pool.wait_ge(row_used, nth(u, SLOTS, at + GROUP))
                pool.sem_inc(pool_gate, 1)
                nc.gpsimd.tensor_copy(idxb[:, q * GROUP:(q + 1) * GROUP],
                                      eidx[:, ds(at, GROUP)]).then_inc(idx_ready, 1)
                pool.wait_ge(idx_ready, nth(u, SLOTS // GROUP, j * (RING // GROUP) + q + 1))
                for g in range(GROUP):
                    s = q * GROUP + g
                    pool.wait_ge(row_used, nth(u, SLOTS, at + g + 1))
                    pool.sem_inc(pool_gate, 1)
                    nc.gpsimd.indirect_dma_start(
                        out=ring[:, s * 2 * D:(s + 1) * 2 * D], out_offset=None, in_=uv[:, :],
                        in_offset=bass.IndirectOffsetOnAxis(ap=idxb[:, s:s + 1], axis=0),
                    ).then_inc(row_in[s], 16)

            def handoff(u):
                if u is not UNITS:
                    pool.wait_ge(handover, nth(u, 2, 2))
                    pool.sem_inc(pool_gate, 1)

            interleave(pool, {}, turn, handoff)

        @block.scalar
        def _(act):
            links = [0]
            sc = nc.scalar

            def link(u, ins):
                links[0] += 1
                ins.then_inc(act_link, 1)
                act.wait_ge(act_link, nth(u, ACT_LINKS, links[0]))

            def rsqrt(u, k, a, b):
                act.wait_ge(var_ready[k], nth(u, 1, 1))
                link(u, sc.activation(rs[:, a:b], var[:, a:b], ACT.Ln))
                sc.activation(rs[:, a:b], rs[:, a:b], ACT.Exp, scale=-0.5).then_inc(rs_ready[k], 1)

            def evac_xT(u, k):
                for n in range(2):
                    act.wait_ge(xT_ps, nth(u, 6, 2 * k + n + 1))
                    sc.activation(xT[:, n * 512:(n + 1) * 512], bank(n), ACT.Copy).then_inc(xT_ready, 1)

            def tables_stage():
                act.wait_ge(ang_ready, 1)
                c4 = cs[:, :].rearrange("p (b c f) -> p b c f", b=BLOCKS, c=2)
                sc.activation(c4[:, :, 0, :], ang_c[:, :].rearrange("p (b f) -> p b f", b=BLOCKS), ACT.Sin)
                sc.activation(c4[:, :, 1, :], ang[:, :].rearrange("p (b f) -> p b f", b=BLOCKS),
                              ACT.Sin).then_inc(rope_ready, 1)

            def norm1(u):
                links[0] = 0
                act.wait_ge(h_ready, nth(u, 1, 1))
                sc.activation(mix[:, :], h[:, :], ACT.Square, scale=float(D ** -0.5),
                              accum_out=ms[:, 0:1]).then_inc(ms_ready["norm1"], 1)
                rsqrt(u, "norm1", 0, 1)
                evac_xT(u, 0)

            def exp_d(u):
                act.wait_ge(chunk_done, nth(u, NW, AFTER_D))
                sc.activation(ebd[:, :], bank(0, 256, 512), ACT.Exp, scale=-1.0).then_inc(ebd_ready, 1)

            def latents(u):
                act.wait_ge(chunk_done, nth(u, NW, AFTER_A))
                sc.activation(pA[:, :], bank(2, 0, A1 - A0), ACT.Copy).then_inc(pA_ready, 1)
                sc.activation(mix[:, 0:QR], bank(2, 0, QR), ACT.Square, scale=float(QR ** -0.5),
                              accum_out=ms[:, 1:2])
                sc.activation(mix[:, QR:QR + KVR], bank(2, QR, QR + KVR), ACT.Square, scale=float(KVR ** -0.5),
                              accum_out=ms[:, 2:3]).then_inc(ms_ready["latents"], 1)

            def conv_input(u):
                act.wait_ge(chunk_done, nth(u, NW, AFTER_Q))
                if u is not 0:
                    act.wait_ge(xcT_ready, u)
                sc.activation(cbuf[:, :].rearrange("p (j t) -> p j t", j=2)[:, :, KB - 1:],
                              bank(3, 0, 2 * P).rearrange("p (j t) -> p j t", j=2), ACT.Copy).then_inc(cbuf_ready, 1)

            def mlstm_input(u):
                act.wait_ge(chunk_done, nth(u, NW, AFTER_B))
                sc.activation(pB[:, 0:512], bank(4), ACT.Copy)
                sc.activation(pB[:, 512:520], bank(3, 256, 264), ACT.Copy).then_inc(pB_ready, 1)

            def gelu_c(u):
                act.wait_ge(chunk_done, nth(u, NW, AFTER_C))
                sc.activation(pC[:, :], bank(0), ACT.Gelu_apprx_tanh).then_inc(pC_ready, 1)

            def latents_out(u):
                rsqrt(u, "latents", 1, 3)
                act.wait_ge(latT_ps, nth(u, 1, 1))
                for k in range(3):
                    last = sc.activation(latT[:, k * P:(k + 1) * P], bank(1, k * P, (k + 1) * P), ACT.Copy,
                                         scale=col("lat", k))
                last.then_inc(latT_ready, 1)
                qk3 = qk[:, :].rearrange("p (h d) -> p h d", h=8)
                act.wait_ge(qkv_ps, nth(u, 2, 1))
                sc.activation(qk[:, 0:HEADS * QK], bank(2, 0, HEADS * QK), ACT.Copy)
                act.wait_ge(qkv_ps, nth(u, 2, 2))
                kv3 = bank(1).rearrange("p (h d) -> p h d", h=HEADS)
                sc.activation(qk3[:, HEADS:8, 0:NOPE], kv3[:, :, 0:NOPE], ACT.Copy).then_inc(qk_evac, 1)
                sc.activation(V[:, ds((u % BLOCKS) * GW, GW)].rearrange("p (h d) -> p h d", h=HEADS),
                              kv3[:, :, NOPE:], ACT.Copy).then_inc(V_ready, 1)

            def qk_root(u):
                rsqrt(u, "qk", 3, 11)

            def qkT_out(u):
                act.wait_ge(qkT_ps, nth(u, 2, 1))
                sc.activation(qT[:, :], bank(2, 0, 512, 0, QK), ACT.Copy).then_inc(qkT_ready, 1)
                act.wait_ge(qkT_ps, nth(u, 2, 2))
                sc.activation(KT[:, :].rearrange("p (h t) -> p h t", h=HEADS)[:, :, ds((u % BLOCKS) * P, P)],
                              bank(1, 0, 512, 0, QK).rearrange("p (h t) -> p h t", h=HEADS),
                              ACT.Copy).then_inc(qkT_ready, 1)

            def exp_scores(u):
                act.wait_ge(mx_ready, nth(u, 1, 1))
                for hd in range(HEADS):
                    sc.activation(big[:, hd * SEQ:(hd + 1) * SEQ], big[:, hd * SEQ:(hd + 1) * SEQ], ACT.Exp,
                                  bias=mx[:, hd:hd + 1], scale=float(QK ** -0.5),
                                  accum_out=psum_p[:, hd:hd + 1]).then_inc(P_ready, 1)

            def probsT_out(u):
                for hd in range(HEADS):
                    act.wait_ge(PT_ps, nth(u, HEADS, hd + 1))
                    sc.activation(big[:, hd * SEQ:(hd + 1) * SEQ], bank(2 + hd), ACT.Copy).then_inc(PT_ready, 1)

            def mlstm_exps(u):
                act.wait_ge(yb_ready, nth(u, 1, 1))
                act.wait_ge(pB_ready, nth(u, 1, 1))
                sc.activation(exo[:, :], pB[:, GW:2 * GW], ACT.Exp, scale=-1.0)
                sc.activation(eb[:, :], yb[:, :], ACT.Exp, scale=-1.0).then_inc(eb_ready, 1)
                act.wait_ge(negz_ready, nth(u, 1, 1))
                link(u, sc.activation(gl[:, 24:28], gl[:, 16:20], ACT.Exp))
                sc.activation(gl[:, 28:32], gl[:, 24:28], ACT.Ln, bias=one_col[:, 0:1]).then_inc(softplus_ready, 1)

            def qkb_out(u):
                act.wait_ge(qkb_ps, nth(u, 1, 1))
                sc.activation(qkTb[:, 0:2 * P], bank(3, 0, 2 * P), ACT.Copy)
                sc.activation(qkTb[:, 2 * P:4 * P], bank(3, 2 * P, 4 * P), ACT.Copy, scale=float(HD ** -0.5))
                sc.activation(ktok[:, :], bank(4, 0, GW), ACT.Copy, scale=float(HD ** -0.5)).then_inc(qkb_ready, 1)

            def row_exps(u):
                act.wait_ge(rows_ready, nth(u, 1, 1))
                sc.activation(gr[:, 6 * P:7 * P], gr[:, 4 * P:5 * P], ACT.Exp, bias=m_st[:, 0:1], scale=-1.0)
                sc.activation(gr[:, 7 * P:8 * P], gr[:, 5 * P:6 * P], ACT.Exp, scale=-1.0).then_inc(EN_ready, 1)

            def decay_exp(u):
                act.wait_ge(y_ready, nth(u, 1, 1))
                sc.activation(Dm[:, :], Dm[:, :], ACT.Exp, scale=-1.0).then_inc(D_ready, 1)

            def swish(u):
                rsqrt(u, "conv", 16, 20)
                act.wait_ge(yt_ready, nth(u, 1, 1))
                sc.activation(vn[:, :], yt[:, :], ACT.Exp, scale=-1.0).then_inc(eyt_ready, 1)

            def norm2(u):
                act.wait_ge(h2_ready, nth(u, 1, 1))
                sc.activation(mix[:, :], h[:, :], ACT.Square, scale=float(D ** -0.5),
                              accum_out=ms[:, 3:4]).then_inc(ms_ready["norm2"], 1)
                rsqrt(u, "norm2", 20, 21)
                evac_xT(u, 2)

            def queries_out(u, n):
                act.wait_ge(chunk_done, nth(u, NW, AFTER_OUT + 2 * n + 2))
                sc.activation(mix[:, n * 512:(n + 1) * 512], bank(4 + n), ACT.Copy).then_inc(qpT_ready, 1)

            def key_scores_out(u):
                act.wait_ge(sc_ps, nth(u, 1, 1))
                for n in range(4):
                    sc.activation(big[:, n * 512:(n + 1) * 512], bank(2 + n), ACT.Copy).then_inc(scs_ready, 1)

            def gate_exps(u):
                act.wait_ge(top_ready, nth(u, 1, 1))
                sc.activation(eg[:, :], eg[:, :], ACT.Exp).then_inc(eg_ready, 1)
                assert links[0] == ACT_LINKS, links

            def turn(u, j, q):
                at = j * RING + q * GROUP
                k = j * (RING // GROUP) + q + 1
                act.wait_ge(dot_done, nth(u, SLOTS, at + GROUP))
                sc.activation(gel[:, q * GROUP:(q + 1) * GROUP], dots[:, q * GROUP:(q + 1) * GROUP],
                              ACT.Gelu_apprx_tanh).then_inc(gelu_done, 1)
                act.wait_ge(act_done, nth(u, SLOTS // GROUP, k))
                for g in range(GROUP):
                    s = q * GROUP + g
                    sc.activation(diag[:, s * P:(s + 1) * P], ident[:, :], ACT.Copy,
                                  scale=acts[:, s:s + 1]).then_inc(diag_ready, 1)

            act.wait_ge(tables, 3)
            tables_stage()
            interleave(act, {
                "norm1": norm1, "act.D": exp_d, "act.A": latents, "act.Q": conv_input, "act.lat": latents_out,
                "act.qk": qk_root, "act.B": mlstm_input, "act.qkT": qkT_out, "act.exp": exp_scores,
                "act.PT": probsT_out, "act.C": gelu_c, "act.qkconv": mlstm_exps, "act.qkb": qkb_out,
                "act.vn": lambda u: rsqrt(u, "spatial", 15, 16), "act.rows": row_exps, "act.decay": decay_exp,
                "act.hidden": lambda u: rsqrt(u, "hidden", 11, 15), "act.swish": swish,
                "act.mixT": lambda u: evac_xT(u, 1), "act.norm2": norm2, "act.q01": lambda u: queries_out(u, 0),
                "act.q23": lambda u: queries_out(u, 1), "act.sc": key_scores_out, "act.gates": gate_exps,
            }, turn, lambda u: None)

        @block.tensor
        def _(pe):
            T = nc.tensor

            def transposes(src, u, k):
                for n in range(2):
                    for i in range(4):
                        c = n * 4 + i
                        last = T.transpose(bank(n, i * P, (i + 1) * P), src[:, c * P:(c + 1) * P], ident[:, :])
                    last.then_inc(xT_ps, 1)

            def wait_w(u, c):
                s = c % WSLOTS
                per = NW // WSLOTS
                pe.wait_ge(w_in[s], nth(u, 16 * per, 16 * (c // WSLOTS + 1)))

            def tokens_by(c, n0, n1, dst):
                w = wchunk(c)
                for k in range(KC):
                    last = T.matmul(dst, xT[:, k * P:(k + 1) * P], w[:, k, n0:n1], start=(k == 0), stop=(k == KC - 1))
                return last

            def channels_by(c, b, a, blocks=2):
                w = wchunk(c)
                for i in range(blocks):
                    for k in range(KC):
                        last = T.matmul(bank(b, a + i * P, a + (i + 1) * P), w[:, k, i * P:(i + 1) * P],
                                        xT[:, k * P:(k + 1) * P], start=(k == 0), stop=(k == KC - 1))
                return last

            def norm1(u):
                pe.wait_ge(xn_ready, nth(u, 2, 1))
                transposes(xn, u, 0)
                pe.wait_ge(xT_ready, nth(u, 6, 2))

            def in_A(u, *cs_):
                for c in cs_:
                    at = IN_CHUNKS[c][0]
                    wait_w(u, c)
                    tokens_by(c, 0, WIDTHS[c], bank(2, at, at + WIDTHS[c])).then_inc(chunk_done, 1)

            def in_Q(u):
                wait_w(u, AFTER_A)
                channels_by(AFTER_A, 3, 0).then_inc(chunk_done, 1)

            def in_B(u, n):
                c = AFTER_Q + n
                wait_w(u, c)
                last = tokens_by(c, 0, 256, bank(4, n * 256, (n + 1) * 256))
                if n == 1:
                    pe.wait_ge(cbuf_ready, nth(u, 1, 1))
                    last = tokens_by(c, 256, 256 + 2 * HEADS, bank(3, 256, 256 + 2 * HEADS))
                last.then_inc(chunk_done, 1)

            def in_C(u, n):
                c = AFTER_B + n
                if n == 0:
                    pe.wait_ge(glu_ready, nth(u, 1, 1))
                wait_w(u, c)
                tokens_by(c, 0, 256, bank(0, n * 256, (n + 1) * 256)).then_inc(chunk_done, 1)

            def in_D(u, n):
                wait_w(u, n)
                channels_by(n, 0, n * 256).then_inc(chunk_done, 1)

            def latents(u):
                pe.wait_ge(lat_ready, nth(u, 1, 1))
                for k in range(3):
                    last = T.transpose(bank(1, k * P, (k + 1) * P), lat[:, k * P:(k + 1) * P], ident[:, :])
                last.then_inc(latT_ps, 1)
                pe.wait_ge(latT_ready, nth(u, 1, 1))
                for k in range(2):
                    last = T.matmul(bank(2, 0, HEADS * QK), latT[:, k * P:(k + 1) * P],
                                    mat("uq")[:, k * HEADS * QK:(k + 1) * HEADS * QK], start=(k == 0), stop=(k == 1))
                last.then_inc(qkv_ps, 1)
                T.matmul(bank(1), latT[:, 2 * P:3 * P], mat("ukv"), start=True, stop=True).then_inc(qkv_ps, 1)

            def qk_transposes(u):
                pe.wait_ge(qk_ready, nth(u, 1, 1))
                pe.wait_ge(V_ready, nth(u, 1, 1))
                for n in range(2):
                    for hd in range(HEADS):
                        c = n * HEADS + hd
                        last = T.transpose(bank(2 - n, hd * P, (hd + 1) * P, 0, QK), qk[:, c * QK:(c + 1) * QK],
                                           ident[:, :])
                    last.then_inc(qkT_ps, 1)

            def scores(u):
                pe.wait_ge(qkT_ready, nth(u, 2, 2))
                pe.wait_ge(pB_ready, nth(u, 1, 1))
                for hd in range(HEADS):
                    last = T.matmul(bank(2 + hd), qT[:, hd * P:(hd + 1) * P], KT[:, hd * SEQ:(hd + 1) * SEQ],
                                    start=True, stop=True)
                last.then_inc(S_ps, 1)

            def attend(u):
                for hd in range(HEADS):
                    pe.wait_ge(P_ready, nth(u, HEADS, hd + 1))
                    for k in range(BLOCKS):
                        last = T.transpose(bank(2 + hd, k * P, (k + 1) * P),
                                           big[:, hd * SEQ + k * P:hd * SEQ + (k + 1) * P], ident[:, :])
                    last.then_inc(PT_ps, 1)
                for hd in range(HEADS):
                    pe.wait_ge(PT_ready, nth(u, HEADS, hd + 1))
                    for k in range(BLOCKS):
                        last = T.matmul(bank(1, hd * HD, (hd + 1) * HD),
                                        big[:, hd * SEQ + k * P:hd * SEQ + (k + 1) * P],
                                        V[:, k * GW + hd * HD:k * GW + (hd + 1) * HD],
                                        start=(k == 0), stop=(k == BLOCKS - 1))
                last.then_inc(o_ps, 1)

            def mlstm_qk(u):
                pe.wait_ge(gates_ready, nth(u, 1, 1))
                T.transpose(bank(5, 0, P, 0, HEADS), gl[:, 8:12], ident[:, :])
                T.transpose(bank(5, P, 2 * P, 0, HEADS), gl[:, 36:40], ident[:, :]).then_inc(gT_ps, 1)
                pe.wait_ge(xcT_ready, nth(u, 1, 1))
                for j in range(2):
                    T.matmul(bank(3, j * P, (j + 1) * P), wqd[:, j * P:(j + 1) * P], xcT[:, j * P:(j + 1) * P],
                             start=True, stop=True)
                    T.matmul(bank(3, (2 + j) * P, (3 + j) * P), wkd[:, j * P:(j + 1) * P],
                             xcT[:, j * P:(j + 1) * P], start=True, stop=True)
                    last = T.matmul(bank(4, j * P, (j + 1) * P), xcT[:, j * P:(j + 1) * P],
                                    wkd[:, j * P:(j + 1) * P], start=True, stop=True)
                last.then_inc(qkb_ps, 1)

            def mlstm_cols(u):
                pe.wait_ge(EN_ready, nth(u, 1, 1))
                pe.sem_inc(pe_hold, 1)
                for i, r in enumerate((3, 6, 7)):
                    T.transpose(bank(5, 4 * i, 4 * i + 4), gr[:, r * P:(r + 1) * P], ident[0:HEADS, 0:HEADS])
                for j in range(2):
                    T.matmul(bank(5, 16 + j, 17 + j), pair_sel[:, j * P:(j + 1) * P], gr[:, 7 * P - 1:7 * P],
                             start=True, stop=True)
                for hd in range(HEADS):
                    last = T.matmul(bank(2, hd * P, (hd + 1) * P), sel[:, hd * P:(hd + 1) * P],
                                    gr[:, 4 * P:5 * P], start=True, stop=True)
                last.then_inc(col_ps, 1)

            def mlstm_scores(u):
                pe.wait_ge(qkb_ready, nth(u, 1, 1))
                pe.wait_ge(y_ready, nth(u, 1, 1))
                v = HD + 1
                for hd in range(HEADS):
                    j, p0 = hd // 2, hd % 2 * HD
                    T.matmul(bank((5, 3)[hd % 2], j * P, (j + 1) * P), qkTb[p0:p0 + HD, (2 + j) * P:(3 + j) * P],
                             qkTb[p0:p0 + HD, j * P:(j + 1) * P], start=True, stop=True)
                    last = T.matmul(bank((4, 2)[hd % 2], j * v, (j + 1) * v), qkTb[p0:p0 + HD, j * P:(j + 1) * P],
                                    Cst[p0:p0 + HD, j * v:(j + 1) * v], start=True, stop=True)
                last.then_inc(SI_ps, 1)

            def mlstm_num(u):
                v = HD + 1
                pe.wait_ge(wgv_ready, nth(u, 1, 1))
                for j in range(2):
                    last = T.matmul(bank(1, j * 2 * v, (j + 1) * 2 * v), ktok[:, j * P:(j + 1) * P],
                                    wgv[:, j * 2 * v:(j + 1) * 2 * v], start=True, stop=True)
                last.then_inc(st_ps, 1)
                pe.wait_ge(Wt_ready, nth(u, 1, 1))
                pe.wait_ge(pC_ready, nth(u, 1, 1))
                for hd in range(HEADS):
                    last = T.matmul(bank(0, hd * v, (hd + 1) * v), Dm[:, hd * P:(hd + 1) * P],
                                    v1[:, hd * v:(hd + 1) * v], start=True, stop=True)
                last.then_inc(num_ps, 1)

            def spatial(u):
                pe.wait_ge(vn_ready, nth(u, 1, 1))
                for hd in range(HEADS):
                    last = T.matmul(bank(3, hd * HD, (hd + 1) * HD), mat("ws")[:, hd * P:(hd + 1) * P],
                                    vn[:, hd * HD:(hd + 1) * HD], start=True, stop=True)
                last.then_inc(sg_ps, 1)

            def conv_transposes(u):
                pe.wait_ge(yd_ready, nth(u, 1, 1))
                for j in range(2):
                    last = T.transpose(bank(4, j * P, (j + 1) * P), yd[:, j * P:(j + 1) * P], ident[:, :])
                last.then_inc(ydT_ps, 1)

            def mix_transposes(u):
                pe.wait_ge(mix_ready, nth(u, 1, 1))
                transposes(mix, u, 1)
                pe.wait_ge(xT_ready, nth(u, 6, 4))

            def w_out(u, n):
                wait_w(u, AFTER_C + n)
                tokens_by(AFTER_C + n, 0, 256, bank(2 + n // 2, n % 2 * 256, n % 2 * 256 + 256)) \
                    .then_inc(chunk_done, 1)

            def norm2(u):
                pe.wait_ge(xn_ready, nth(u, 2, 2))
                transposes(xn, u, 2)
                pe.wait_ge(xT_ready, nth(u, 6, 6))

            def queries(u, n):
                wait_w(u, AFTER_OUT + n)
                channels_by(AFTER_OUT + n, 4 + n // 2, n % 2 * 256).then_inc(chunk_done, 1)

            def key_scores(u):
                pe.wait_ge(qpT_ready, nth(u, 2, 2))
                for hd in range(PH):
                    for half in range(2):
                        p0 = half * HD
                        i = half * PH + hd
                        last = T.matmul(bank(2 + i // 4, i % 4 * P, (i % 4 + 1) * P),
                                        mix[p0:p0 + HD, hd * P:(hd + 1) * P],
                                        mat("sk")[p0:p0 + HD, hd * KEYS:(hd + 1) * KEYS], start=True, stop=True)
                last.then_inc(sc_ps, 1)

            def turn(u, j, q):
                for s in range(q * GROUP, (q + 1) * GROUP):
                    pe.wait_ge(diag_ready, nth(u, SLOTS, j * RING + s + 1))
                    for n in range(2):
                        a = s * 2 * D + D + n * 512
                        last = T.matmul(acc[:, n * 512:(n + 1) * 512], diag[:, s * P:(s + 1) * P],
                                        ring[:, a:a + 512], start=False, stop=False, skip_group_check=True)
                    last.then_inc(row_used, 1)

            def handoff(u):
                if u is not 0:
                    T.matmul(acc[:, 0:1], zrow[:, 0:P], zrow[:, 0:1], start=False, stop=False,
                             skip_group_check=True).then_inc(experts_ps, 1)
                if u is not UNITS:
                    pe.wait_ge(handover, nth(u, 2, 2))
                    for n in range(2):
                        T.matmul(acc[:, n * 512:(n + 1) * 512], zrow[:, 0:P], key_no[0:1, :], start=True, stop=False,
                                 skip_group_check=True)

            pe.sem_inc(row_used, RING)
            pe.wait_ge(tables, 3)
            interleave(pe, {
                "norm1": norm1, "pe.D0": lambda u: in_D(u, 0), "pe.D1": lambda u: in_D(u, 1),
                "pe.A0": lambda u: in_A(u, 2), "pe.A1": lambda u: in_A(u, 3, 4), "pe.Q": in_Q, "pe.lat": latents,
                "pe.B0": lambda u: in_B(u, 0), "pe.B1": lambda u: in_B(u, 1), "pe.qkT": qk_transposes,
                "pe.S": scores, "pe.C0": lambda u: in_C(u, 0), "pe.C1": lambda u: in_C(u, 1), "pe.PV": attend,
                "pe.qkconv": mlstm_qk, "pe.cols": mlstm_cols, "pe.scores": mlstm_scores, "pe.num": mlstm_num,
                "pe.sg": spatial, "pe.ydT": conv_transposes, "pe.mixT": mix_transposes,
                "pe.out0": lambda u: w_out(u, 0), "pe.out1": lambda u: w_out(u, 1),
                "pe.out2": lambda u: w_out(u, 2), "pe.out3": lambda u: w_out(u, 3), "pe.norm2": norm2,
                "pe.q0": lambda u: queries(u, 0), "pe.q1": lambda u: queries(u, 1),
                "pe.q2": lambda u: queries(u, 2), "pe.q3": lambda u: queries(u, 3), "pe.sc": key_scores,
            }, turn, handoff)

        @block.vector
        def _(dve):
            V_ = nc.vector
            links, of_setup = [0], [0]

            def link(u, ins, held=False):
                links[0] += 1
                ins.then_inc(dve_link, 1)
                dve.wait_ge(dve_link, nth(u, DVE_LINKS, of_setup[0] + links[0]))
                if held:
                    hold()

            def hold():
                dve.sem_inc(dve_hold, 1)

            def rsqrt(u, k, a, b):
                dve.wait_ge(rs_ready[k], nth(u, 1, 1))
                v, r, t = var[:, a:b], rs[:, a:b], rt[:, a:b]
                link(u, V_.tensor_tensor(t, r, r, ALU.mult))
                link(u, V_.tensor_tensor(t, t, v, ALU.mult))
                link(u, V_.tensor_scalar(t, t, -0.5, 1.5, ALU.mult, ALU.add))
                link(u, V_.tensor_tensor(r, r, t, ALU.mult))

            def sigmoid_mul(u, dst, e, other):
                link(u, V_.tensor_scalar(e, e, 1.0, None, ALU.add))
                link(u, V_.reciprocal(e, e))
                return V_.tensor_tensor(dst, other, e, ALU.mult)

            def heads(ap, n=HEADS):
                return ap.rearrange("p (h d) -> p h d", h=n)

            def of_half(ap, half):
                return ap.rearrange("p (j c d) -> p j c d", j=2, c=2)[:, :, half, :]

            def over(ap, n, d):
                return ap.unsqueeze(2).to_broadcast([P, n, d])

            def setup():
                dve.wait_ge(tables, 3)
                V_.tensor_copy(key_no[:, :], key_i[:, :])
                V_.tensor_copy(n16[:, :], key_i[:, 0:TOPK])
                V_.tensor_copy(qpos[:, :], qpos_i[:, :]).then_inc(tables_f, 1)
                dve.wait_ge(pos_in, 16)
                link(0, V_.tensor_copy(pos_f[:, :], pos_i[:, :]))
                two_pi = 2.0 * np.pi
                p1 = 6.28125
                p2 = float(np.round((two_pi - p1) * 2.0 ** 21) / 2.0 ** 21)
                p3 = float(two_pi - p1 - p2)
                a3 = ang[:, :].rearrange("p (b f) -> p b f", b=BLOCKS)
                link(0, V_.tensor_tensor(a3, pos_f[:, :].unsqueeze(2).to_broadcast([P, BLOCKS, HR]),
                                         freq[:, :].unsqueeze(1).to_broadcast([P, BLOCKS, HR]), ALU.mult))
                magic = 1.5 * 2.0 ** 23
                link(0, V_.tensor_scalar(ang_n[:, :], ang[:, :], float(1 / two_pi), None, ALU.mult))
                link(0, V_.tensor_scalar(ang_n[:, :], ang_n[:, :], magic, None, ALU.add))
                link(0, V_.tensor_scalar(ang_n[:, :], ang_n[:, :], -magic, None, ALU.add))
                for part in (p1, p2, p3):
                    link(0, V_.scalar_tensor_tensor(ang[:, :], ang_n[:, :], -part, ang[:, :], ALU.mult, ALU.add))
                pi = 3.1415925
                link(0, V_.tensor_scalar(ang[:, :], ang[:, :], pi, -pi, ALU.min, ALU.max))
                link(0, V_.scalar_tensor_tensor(ang_c[:, :], ang[:, :], -1.0, ang[:, :], ALU.mult, ALU.max))
                link(0, V_.tensor_scalar(ang_c[:, :], ang_c[:, :], -1.0, float(np.pi / 2), ALU.mult, ALU.add))
                V_.tensor_copy(rt[:, 0:1], ang[:, 0:1]).then_inc(ang_ready, 1)
                dve.wait_ge(rope_ready, 1)
                link(0, V_.tensor_copy(rt[:, 0:1], cs[:, 0:1]))
                link(0, V_.tensor_copy(rt[:, 0:1], cs[:, 0:1]))
                of_setup[0] = links[0]
                dve.wait_ge(tables_f, 1)
                dve.wait_ge(x_in, 16)

            def norm1(u):
                links[0] = 0
                dve.wait_ge(params_in, nth(u, 16 * 7, 16 * 7))
                hold()
                V_.tensor_copy(csb[:, :], cs[:, ds((u % BLOCKS) * ROPE, ROPE)])
                V_.tensor_copy(h[:, :], xs[:, ds((u % BLOCKS) * D, D)]).then_inc(h_ready, 1)
                V_.tensor_scalar(mask[:, :], key_no[:, :], qpos[:, ds(u, 1)], -1e30, ALU.is_gt, ALU.mult)
                dve.wait_ge(ms_ready["norm1"], nth(u, 1, 1))
                V_.tensor_scalar(var[:, 0:1], ms[:, 0:1], EPS, None, ALU.add).then_inc(var_ready["norm1"], 1)
                rsqrt(u, "norm1", 0, 1)
                V_.scalar_tensor_tensor(xn[:, :], h[:, :], rs[:, 0:1], row("g1"), ALU.mult,
                                        ALU.mult).then_inc(xn_ready, 1)

            def gated(u):
                dve.wait_ge(ebd_ready, nth(u, 1, 1))
                link(u, V_.tensor_scalar(ebd[:, :], ebd[:, :], 1.0, None, ALU.add))
                link(u, V_.reciprocal(ebd[:, :], ebd[:, :]))
                V_.tensor_tensor(glu[:, :].rearrange("p (j t) -> p j t", j=2)[:, :, KD - 1:],
                                 bank(0, 0, 2 * P).rearrange("p (j t) -> p j t", j=2),
                                 ebd[:, :].rearrange("p (j t) -> p j t", j=2), ALU.mult).then_inc(glu_ready, 1)

            def latents(u):
                dve.wait_ge(ms_ready["latents"], nth(u, 1, 1))
                V_.tensor_scalar(var[:, 1:3], ms[:, 1:3], EPS, None, ALU.add).then_inc(var_ready["latents"], 1)
                kr = pA[:, QR + KVR:A1]
                V_.tensor_copy(heads(qk[:, :], 8)[:, HEADS:8, NOPE:],
                               kr.unsqueeze(1).to_broadcast([P, HEADS, ROPE]))
                rsqrt(u, "latents", 1, 3)
                V_.tensor_scalar(lat[:, 0:QR], pA[:, 0:QR], rs[:, 1:2], None, ALU.mult)
                V_.tensor_scalar(lat[:, QR:], pA[:, QR:QR + KVR], rs[:, 2:3], None, ALU.mult) \
                    .then_inc(lat_ready, 1)

            def qkv(u):
                dve.wait_ge(qk_evac, nth(u, 1, 1))
                q3 = heads(qk[:, :], 8)
                link(u, V_.tensor_tensor(qk_sq[:, :], qk[:, :], qk[:, :], ALU.mult))
                link(u, V_.tensor_reduce(rt[:, 3:11], heads(qk_sq[:, :], 8), AX.X, ALU.add))
                V_.tensor_scalar(var[:, 3:11], rt[:, 3:11], 1.0 / QK, EPS, ALU.mult, ALU.add).then_inc(var_ready["qk"], 1)
                rsqrt(u, "qk", 3, 11)
                link(u, V_.tensor_tensor(q3, q3, over(rs[:, 3:11], 8, QK), ALU.mult))
                q4 = qk[:, :].rearrange("p (g h d) -> p g h d", g=2, h=HEADS)
                g4 = row("qkg").rearrange("p (g d) -> p g d", g=2).unsqueeze(2).to_broadcast([P, 2, HEADS, QK])
                link(u, V_.tensor_tensor(q4, q4, g4, ALU.mult))
                x1, x2 = q3[:, :, NOPE:NOPE + HR], q3[:, :, NOPE + HR:]
                cos = csb[:, 0:HR].unsqueeze(1).to_broadcast([P, 8, HR])
                sin = csb[:, HR:].unsqueeze(1).to_broadcast([P, 8, HR])
                r = [heads(rp[:, i * 8 * HR:(i + 1) * 8 * HR], 8) for i in range(4)]
                V_.tensor_tensor(r[0], x1, cos, ALU.mult)
                V_.tensor_tensor(r[1], x2, sin, ALU.mult)
                V_.tensor_tensor(r[2], x1, sin, ALU.mult)
                link(u, V_.tensor_tensor(r[3], x2, cos, ALU.mult))
                V_.tensor_tensor(x1, r[0], r[1], ALU.subtract)
                V_.tensor_tensor(x2, r[2], r[3], ALU.add).then_inc(qk_ready, 1)

            def scores(u):
                dve.wait_ge(S_ps, nth(u, 1, 1))
                b3 = heads(big[:, :])
                link(u, V_.tensor_tensor(b3, ps[:, 2 * 512:6 * 512].rearrange("p (h t) -> p h t", h=HEADS),
                                         mask[:, :].unsqueeze(1).to_broadcast([P, HEADS, SEQ]), ALU.add))
                link(u, V_.tensor_reduce(mx[:, :], b3, AX.X, ALU.max))
                V_.tensor_scalar(mx[:, :], mx[:, :], -float(QK ** -0.5), None, ALU.mult).then_inc(mx_ready, 1)

            def attended(u):
                dve.wait_ge(P_ready, nth(u, HEADS, HEADS))
                link(u, V_.reciprocal(rsum_p[:, :], psum_p[:, :]))
                dve.wait_ge(o_ps, nth(u, 1, 1))
                V_.tensor_tensor(heads(mix[:, 0:GW]), heads(bank(1, 0, GW)), over(rsum_p[:, :], HEADS, HD),
                                 ALU.mult).then_inc(oA_done, 1)

            def mlstm_conv(u):
                dve.wait_ge(cbuf_ready, nth(u, 1, 1))
                c3 = cbuf[:, :].rearrange("p (j t) -> p j t", j=2)
                for k in range(KB):
                    for j in range(2):
                        src, dst = c3[:, j, k:k + P], yb[:, j * P:(j + 1) * P]
                        w = col("bw", j * KB + k)
                        if k == 0:
                            last = V_.tensor_scalar(dst, src, w, col("bb", j), ALU.mult, ALU.add)
                        else:
                            last = V_.scalar_tensor_tensor(dst, src, w, dst, ALU.mult, ALU.add)
                        if k < KB - 1 and j == 1:
                            link(u, last)
                last.then_inc(yb_ready, 1)
                dve.wait_ge(yb_ready, nth(u, 1, 1))
                V_.tensor_scalar(c3[:, :, 0:KB - 1], c3[:, :, P:P + KB - 1], carry[:, ds(u + 1, 1)], None, ALU.mult)
                link(u, V_.tensor_tensor(gl[:, 8:16], pB[:, 512:520], row("gb"), ALU.add))
                z = gl[:, 12:16]
                V_.scalar_tensor_tensor(gl[:, 16:20], z, -1.0, z, ALU.mult, ALU.min).then_inc(negz_ready, 1)
                link(u, V_.tensor_scalar(gl[:, 32:36], z, 0.0, None, ALU.min))
                dve.wait_ge(softplus_ready, nth(u, 1, 1))
                V_.tensor_tensor(gl[:, 36:40], gl[:, 32:36], gl[:, 28:32], ALU.subtract).then_inc(gates_ready, 1)
                dve.wait_ge(eb_ready, nth(u, 1, 1))
                sigmoid_mul(u, xcT[:, :], eb[:, :], yb[:, :]).then_inc(xcT_ready, 1)

            def mlstm_rows(u):
                dve.wait_ge(gT_ps, nth(u, 1, 1))
                g = [gr[:, i * P:(i + 1) * P] for i in range(8)]
                link(u, V_.tensor_copy(gr[:, 0:2 * P], bank(5, 0, 2 * P, 0, HEADS)))
                link(u, V_.tensor_tensor_scan(g[2], ones4[:, :], g[1], 0.0, ALU.mult, ALU.add))
                link(u, V_.tensor_tensor(g[3], g[0], g[2], ALU.subtract))
                link(u, V_.tensor_tensor_scan(g[4], g[3], g[3], m_st[:, 0:1], ALU.max, ALU.max))
                V_.tensor_tensor(g[5], g[2], g[4], ALU.add).then_inc(rows_ready, 1)

            def mlstm_decay(u):
                dve.wait_ge(col_ps, nth(u, 1, 1))
                link(u, V_.tensor_copy(gc[:, 0:12], bank(5, 0, 12)))
                link(u, V_.tensor_copy(gc[:, 16:18], bank(5, 16, 18)))
                for hd in range(HEADS):
                    last = V_.tensor_scalar(Dm[:, hd * P:(hd + 1) * P], bank(2, hd * P, (hd + 1) * P),
                                            gc[:, hd:hd + 1], 0.0, ALU.subtract, ALU.max)
                last.then_inc(y_ready, 1)
                link(u, V_.tensor_copy(heads(v1[:, :])[:, :, 0:HD], heads(pB[:, 0:GW])))

            def mlstm_weigh(u):
                v = HD + 1
                dve.wait_ge(D_ready, nth(u, 1, 1))
                V_.tensor_tensor(heads(wgv[:, :]), heads(v1[:, :]),
                                 heads(Dm[:, :])[:, :, P - 1:P].to_broadcast([P, HEADS, v]),
                                 ALU.mult).then_inc(wgv_ready, 1)
                dve.wait_ge(SI_ps, nth(u, 1, 1))
                dve.wait_ge(wgv_ready, nth(u, 1, 1))
                for half, b in ((0, 5), (1, 3)):
                    d = of_half(Dm[:, :], half)
                    last = V_.tensor_tensor(d, d, bank(b, 0, 2 * P).rearrange("p (j t) -> p j t", j=2), ALU.mult)
                link(u, last)
                V_.tensor_tensor(heads(Dm[:, :]), heads(Dm[:, :]), tri[:, :].unsqueeze(1).to_broadcast([P, HEADS, P]),
                                 ALU.mult).then_inc(Wt_ready, 1)

            def mlstm_hidden(u):
                v = HD + 1
                for half, b in ((0, 4), (1, 2)):
                    last = V_.tensor_tensor(of_half(t1[:, :], half),
                                            bank(b, 0, 2 * v).rearrange("p (j d) -> p j d", j=2),
                                            over(gc[:, 4 + half:8:2], 2, v), ALU.mult)
                link(u, last)
                dve.wait_ge(num_ps, nth(u, 1, 1))
                link(u, V_.tensor_tensor(nd[:, :], bank(0, 0, HEADS * v), t1[:, :], ALU.add))
                n3 = heads(nd[:, :])
                d3 = n3[:, :, HD:v]
                link(u, V_.scalar_tensor_tensor(den[:, :].unsqueeze(2), d3, -1.0, d3, ALU.mult, ALU.max))
                link(u, V_.tensor_tensor(den[:, :], den[:, :], gc[:, 8:12], ALU.max))
                link(u, V_.reciprocal(den[:, :], den[:, :]))
                link(u, V_.tensor_tensor(heads(hh[:, :]), n3[:, :, 0:HD], over(den[:, :], HEADS, HD), ALU.mult))
                link(u, V_.tensor_tensor(yt[:, :], hh[:, :], hh[:, :], ALU.mult))
                link(u, V_.tensor_reduce(rt[:, 11:15], heads(yt[:, :]), AX.X, ALU.add))
                V_.tensor_scalar(var[:, 11:15], rt[:, 11:15], 1.0 / HD, EPS, ALU.mult, ALU.add) \
                    .then_inc(var_ready["hidden"], 1)
                dve.wait_ge(st_ps, nth(u, 1, 1))
                for j in range(2):
                    for half in range(2):
                        p0 = half * HD
                        C = Cst[p0:p0 + HD, j * v:(j + 1) * v]
                        a = (j * 2 + half) * v
                        last = V_.scalar_tensor_tensor(C, C, gc[p0:p0 + HD, 16 + j:17 + j],
                                                       bank(1, a, a + v, p0, p0 + HD), ALU.mult, ALU.add)
                link(u, last)
                V_.tensor_scalar(Cst[:, :], Cst[:, :], carry[:, ds(u + 1, 1)], None, ALU.mult)
                link(u, V_.tensor_scalar(m_st[:, :], gr[:, 6 * P - 1:6 * P], carry[0:HEADS, ds(u + 1, 1)], None,
                                         ALU.mult))
                rsqrt(u, "hidden", 11, 15)
                link(u, V_.tensor_tensor(heads(hh[:, :]), heads(hh[:, :]), over(rs[:, 11:15], HEADS, HD), ALU.mult))
                link(u, V_.tensor_tensor(hh[:, :], hh[:, :], row("hg"), ALU.mult))
                link(u, sigmoid_mul(u, mix[:, GW:2 * GW], exo[:, :], hh[:, :]))

            def spatial(u):
                dve.wait_ge(pC_ready, nth(u, 1, 1))
                v_in = pC[:, GW:2 * GW]
                link(u, V_.bn_stats(bn[:, 0:6], v_in), held=True)
                link(u, V_.bn_aggr(mv[:, 0:2], bn[:, 0:6]))
                V_.tensor_scalar(var[:, 15:16], mv[:, 1:2], EPS, None, ALU.add).then_inc(var_ready["spatial"], 1)
                V_.tensor_tensor(heads(mat("ws")), heads(mat("ws")), tri[:, :].unsqueeze(1).to_broadcast([P, HEADS, P]),
                                 ALU.mult)
                rsqrt(u, "spatial", 15, 16)
                link(u, V_.tensor_scalar(vn[:, :], v_in, mv[:, 0:1], rs[:, 15:16], ALU.subtract, ALU.mult))
                link(u, V_.tensor_tensor(vn[:, :], vn[:, :], row("cg"), ALU.mult))
                V_.tensor_tensor(vn[:, :], vn[:, :], row("cb"), ALU.add).then_inc(vn_ready, 1)

            def spatial_out(u):
                dve.wait_ge(sg_ps, nth(u, 1, 1))
                link(u, V_.tensor_tensor(heads(yt[:, :]), heads(bank(3, 0, GW)), over(col("bs"), HEADS, HD), ALU.add))
                link(u, V_.tensor_tensor(mix[:, 2 * GW:3 * GW], yt[:, :], pC[:, 0:GW], ALU.mult))

            def conv_taps(u, part):
                g3 = glu[:, :].rearrange("p (j t) -> p j t", j=2)
                if part == 0:
                    dve.wait_ge(glu_ready, nth(u, 1, 1))
                for k in range(KD * part // CONV_PARTS, KD * (part + 1) // CONV_PARTS):
                    for j in range(2):
                        src, dst = g3[:, j, k:k + P], yd[:, j * P:(j + 1) * P]
                        w = col("dw", j * KD + k)
                        if k == 0:
                            last = V_.tensor_scalar(dst, src, w, col("db", j), ALU.mult, ALU.add)
                        else:
                            last = V_.scalar_tensor_tensor(dst, src, w, dst, ALU.mult, ALU.add)
                        if k < KD - 1 and j == 1:
                            link(u, last)
                if part == CONV_PARTS - 1:
                    last.then_inc(yd_ready, 1)
                    dve.wait_ge(yd_ready, nth(u, 1, 1))
                    link(u, V_.tensor_scalar(g3[:, :, 0:KD - 1], g3[:, :, P:P + KD - 1], carry[:, ds(u + 1, 1)],
                                             None, ALU.mult))

            def swish(u):
                dve.wait_ge(ydT_ps, nth(u, 1, 1))
                for hd in range(HEADS):
                    last = V_.bn_stats(bn[:, hd * 6:(hd + 1) * 6], bank(4, hd * HD, (hd + 1) * HD))
                link(u, last, held=True)
                for hd in range(HEADS):
                    last = V_.bn_aggr(mv[:, hd * 2:(hd + 1) * 2], bn[:, hd * 6:(hd + 1) * 6])
                link(u, last)
                m3 = mv[:, :].rearrange("p (h d) -> p h d", h=HEADS)
                V_.tensor_scalar(var[:, 16:20].unsqueeze(2), m3[:, :, 1:2], EPS, None, ALU.add).then_inc(var_ready["conv"], 1)
                rsqrt(u, "conv", 16, 20)
                for hd in range(HEADS):
                    last = V_.tensor_scalar(yt[:, hd * HD:(hd + 1) * HD], bank(4, hd * HD, (hd + 1) * HD),
                                            mv[:, 2 * hd:2 * hd + 1], rs[:, 16 + hd:17 + hd], ALU.subtract, ALU.mult)
                link(u, last)
                link(u, V_.tensor_tensor(yt[:, :], yt[:, :], row("dg"), ALU.mult))
                V_.tensor_tensor(yt[:, :], yt[:, :], row("db"), ALU.add).then_inc(yt_ready, 1)
                dve.wait_ge(eyt_ready, nth(u, 1, 1))
                sigmoid_mul(u, mix[:, 3 * GW:], vn[:, :], yt[:, :]).then_inc(mix_ready, 1)

            def norm2(u):
                dve.wait_ge(chunk_done, nth(u, NW, AFTER_OUT))
                V_.tensor_tensor(h[:, :], h[:, :], ps[:, 2 * 512:4 * 512], ALU.add).then_inc(h2_ready, 1)
                dve.wait_ge(h2_ready, nth(u, 1, 1))
                hold()
                V_.tensor_copy(xs[:, ds((u % BLOCKS) * D, D)], h[:, :])
                dve.wait_ge(ms_ready["norm2"], nth(u, 1, 1))
                V_.tensor_scalar(var[:, 20:21], ms[:, 3:4], EPS, None, ALU.add).then_inc(var_ready["norm2"], 1)
                rsqrt(u, "norm2", 20, 21)
                V_.scalar_tensor_tensor(xn[:, :], h[:, :], rs[:, 20:21], row("g2"), ALU.mult,
                                        ALU.mult).then_inc(xn_ready, 1)

            def best(i, half):
                return slice(i * TOPK + half * 8, i * TOPK + half * 8 + 8)

            def top8(u, n, count, s_out, half):
                for i in range(count):
                    last = V_.max(s_out[:, best(i, half)], big[:, i * n:(i + 1) * n])
                link(u, last, held=True)

            def places(u, n, count, s_out, i_out, half):
                for i in range(count):
                    last = V_.max_index(i_out[:, best(i, half)], s_out[:, best(i, half)], big[:, i * n:(i + 1) * n])
                link(u, last, held=True)

            def without8(u, n, count, s_out):
                for i in range(count):
                    v = big[:, i * n:(i + 1) * n]
                    last = V_.match_replace(v, s_out[:, best(i, 0)], v, LOWEST)
                link(u, last, held=True)

            KEY_LISTS = (KEYS, 2 * PH)
            SUM_LISTS = (TOPK * TOPK, PH)

            def route0(u):
                dve.wait_ge(scs_ready, nth(u, 4, 4))
                hold()
                top8(u, *KEY_LISTS, s_top, 0)
                places(u, *KEY_LISTS, s_top, i_top, 0)

            def route1(u):
                without8(u, *KEY_LISTS, s_top)
                top8(u, *KEY_LISTS, s_top, 1)

            def route2(u):
                places(u, *KEY_LISTS, s_top, i_top, 1)
                s4 = s_top[:, :].rearrange("p (c h k) -> p c h k", h=PH, c=2)
                grid = big[:, :].rearrange("p (h a b) -> p h a b", h=PH, a=TOPK)
                link(u, V_.tensor_tensor(grid, s4[:, 0, :, :].unsqueeze(3).to_broadcast([P, PH, TOPK, TOPK]),
                                         s4[:, 1, :, :].unsqueeze(2).to_broadcast([P, PH, TOPK, TOPK]), ALU.add),
                     held=True)

            def route3(u):
                top8(u, *SUM_LISTS, c_top, 0)
                places(u, *SUM_LISTS, c_top, ci_top, 0)

            def route4(u):
                without8(u, *SUM_LISTS, c_top)
                top8(u, *SUM_LISTS, c_top, 1)

            def route5(u):
                c3 = heads(c_top[:, :], PH)
                V_.tensor_tensor(heads(eg[:, :], PH), c3, c3[:, :, 0:1].to_broadcast([P, PH, TOPK]),
                                 ALU.subtract).then_inc(top_ready, 1)
                places(u, *SUM_LISTS, c_top, ci_top, 1)
                V_.tensor_scalar(c_hi[:, :], ci_top[:, :], 4, None, ALU.logical_shift_right)
                V_.tensor_scalar(c_lo[:, :], ci_top[:, :], TOPK - 1, None, ALU.bitwise_and)
                link(u, V_.tensor_copy(if_top[:, :], i_top[:, :]))
                V_.tensor_copy(f_hi[:, :], c_hi[:, :])
                link(u, V_.tensor_copy(f_lo[:, :], c_lo[:, :]))

            def key_at(u, c, place, dst):
                i4 = if_top[:, :].rearrange("p (c h k) -> p c h k", h=PH, c=2)
                work = big[:, :].rearrange("p (s k) -> p s k", k=TOPK)
                work4 = big[:, :].rearrange("p (h s k) -> p h s k", h=PH, k=TOPK)
                link(u, V_.tensor_tensor(work, place[:, :].unsqueeze(2).to_broadcast([P, SLOTS, TOPK]),
                                         n16[:, :].unsqueeze(1).to_broadcast([P, SLOTS, TOPK]), ALU.is_equal))
                link(u, V_.tensor_tensor(work4, work4,
                                         i4[:, c, :, :].unsqueeze(2).to_broadcast([P, PH, TOPK, TOPK]), ALU.mult))
                link(u, V_.tensor_reduce(dst[:, :], work, AX.X, ALU.add))

            def route7(u):
                key_at(u, 1, f_lo, e2)
                link(u, V_.scalar_tensor_tensor(e1[:, :], e1[:, :], float(KEYS), e2[:, :], ALU.mult, ALU.add))
                link(u, V_.tensor_scalar(e1[:, :], e1[:, :], lbase[:, ds(u, 1)], None, ALU.add))
                dve.wait_ge(eg_ready, nth(u, 1, 1))
                link(u, V_.tensor_reduce(gs[:, :], heads(eg[:, :], PH), AX.X, ALU.add))
                link(u, V_.reciprocal(gs[:, :], gs[:, :]))
                link(u, V_.tensor_tensor(heads(eg[:, :], PH), heads(eg[:, :], PH), over(gs[:, :], PH, TOPK), ALU.mult))
                assert links[0] == DVE_LINKS, links

            def turn(u, j, q):
                k = j * (RING // GROUP) + q + 1
                at = j * RING + q * GROUP
                for g in range(GROUP):
                    s = q * GROUP + g
                    dve.wait_ge(row_in[s], nth(u, 16 * PAIRS, j * 16 + 16))
                    V_.tensor_tensor_reduce(out=ring[:, s * 2 * D:s * 2 * D + D], in0=xp[:, :], in1=ring[:, s * 2 * D:s * 2 * D + D],
                                            scale=1.0, scalar=0.0, op0=ALU.mult, op1=ALU.add,
                                            accum_out=dots[:, s:s + 1]).then_inc(dot_done, 1)
                    dve.wait_ge(dot_done, nth(u, SLOTS, at + g + 1))
                dve.wait_ge(gelu_done, nth(u, SLOTS // GROUP, k))
                V_.tensor_tensor(acts[:, q * GROUP:(q + 1) * GROUP], gel[:, q * GROUP:(q + 1) * GROUP],
                                 gates[:, ds(at, GROUP)], ALU.mult).then_inc(act_done, 1)

            def handoff(u):
                if u is not 0:
                    before = u - 1
                    dve.wait_ge(experts_ps, u)
                    r = xs[:, ds((before % BLOCKS) * D, D)]
                    V_.tensor_tensor(r, r, acc[:, :], ALU.add).then_inc(x_done, 1)
                    dve.wait_ge(x_done, u)
                    hold()
                if u is not UNITS:
                    V_.tensor_copy(xp[:, :], xn[:, :])
                    V_.tensor_copy(gates[:, :], eg[:, :]).then_inc(handover, 1)
                    V_.tensor_copy(eidx[:, :], e1[:, :]).then_inc(handover, 1)
                    dve.wait_ge(handover, nth(u, 2, 2))

            setup()
            conv = {f"dve.conv{k}": (lambda u, k=k: conv_taps(u, k)) for k in range(CONV_PARTS)}
            interleave(dve, {
                **conv, "norm1": norm1, "dve.glu": gated, "dve.lat": latents, "dve.qk": qkv, "dve.max": scores,
                "dve.oA": attended, "dve.qkconv": mlstm_conv, "dve.vn": spatial, "dve.rows": mlstm_rows,
                "dve.decay": mlstm_decay, "dve.weigh": mlstm_weigh, "dve.hidden": mlstm_hidden,
                "dve.sg": spatial_out, "dve.swish": swish, "dve.norm2": norm2, "dve.r0": route0,
                "dve.r1": route1, "dve.r2": route2, "dve.r3": route3, "dve.r4": route4, "dve.r5": route5,
                "dve.r6": lambda u: key_at(u, 0, f_hi, e1), "dve.r7": route7,
            }, turn, handoff)


def kernel(**inputs):
    import concourse.bacc as bacc
    from concourse.bass_utils import run_bass_kernel_spmd

    a = {k: np.asarray(v) for k, v in inputs.items()}
    L = DEPTH

    def chunked(w):
        return w.reshape(L, KC, P, -1).transpose(0, 2, 1, 3).reshape(L, -1)

    w_all = np.concatenate(
        [chunked(a["w_in"][:, :, lo:hi]) for lo, hi in IN_CHUNKS]
        + [chunked(a["w_out"][:, :, n * 256:(n + 1) * 256]) for n in range(4)]
        + [chunked(a["p_w_q"][:, :, n * 256:(n + 1) * 256]) for n in range(4)], axis=1)
    rows = np.concatenate(
        [a["norm1_g"], a["norm2_g"], a["a_qn_g"], a["a_kn_g"], a["c_ln_g"], a["c_ln_b"],
         a["d_cn_g"].reshape(L, GW), a["d_cn_b"].reshape(L, GW), a["b_hn_g"].reshape(L, GW),
         a["b_b_i"], a["b_b_f"]], axis=1)

    def channels(v):
        n = v.shape[1]
        return v.reshape(L, n, 2, P).transpose(0, 3, 2, 1).reshape(L, P, 2 * n)

    cols = np.concatenate(
        [a["a_cq_g"].reshape(L, 2, P).transpose(0, 2, 1), a["a_ckv_g"].reshape(L, 1, P).transpose(0, 2, 1),
         channels(a["b_conv_w"]), channels(a["b_conv_b"][:, None]), channels(a["d_dw_w"]),
         channels(a["d_dw_b"][:, None]), a["c_b_s"].transpose(0, 2, 1)], axis=2)
    mats = np.concatenate(
        [a["a_w_uq"].reshape(L, 2, P, -1).transpose(0, 2, 1, 3).reshape(L, P, -1), a["a_w_ukv"],
         a["c_w_s"].transpose(0, 3, 1, 2).reshape(L, P, -1),
         a["p_sub_keys"].transpose(0, 2, 4, 1, 3).reshape(L, P, -1)], axis=2)

    def halves(w):
        return w.reshape(L, 2, 2, HD, HD).transpose(0, 2, 3, 1, 4).reshape(L, 2, HD, 2 * HD)

    uv = np.concatenate([a["p_u"], a["p_v"]], axis=2).reshape(L * EXPERTS, 2 * D)
    arrays = {"x": a["x"], "positions": a["positions"], "w_all": w_all, "rows": rows, "cols": cols, "mats": mats,
              "bq": halves(a["b_w_q"]), "bk": halves(a["b_w_k"]), "uv": uv}
    arrays = {k: np.ascontiguousarray(v) for k, v in arrays.items()}
    nc = bacc.Bacc("TRN2", target_bir_lowering=False, num_devices=1)
    args = [nc.dram_tensor(n, v.shape, mybir.dt.from_np(v.dtype), kind="ExternalInput").ap()
            for n, v in arrays.items()]
    args.append(nc.dram_tensor("out", a["x"].shape, F32, kind="ExternalOutput").ap())
    build(nc, *args)
    return run_bass_kernel_spmd(nc, [arrays], core_ids=[0]).results[0]["out"]
```

```python
from contextlib import ExitStack

import numpy as np

import concourse.bass as bass
from concourse import mybir

F32 = mybir.dt.float32
I32 = mybir.dt.int32
U32 = mybir.dt.uint32
ALU = mybir.AluOpType
ACT = mybir.ActivationFunctionType
AX = mybir.AxisListType
ds = bass.ds

P = 128
D = 1024
SEQ = 512
DEPTH = 2
BLOCKS = SEQ // P
UNITS = DEPTH * BLOCKS
KC = D // P
HEADS = 4
HD = 64
GW = HEADS * HD
NOPE, ROPE = 64, 32
QK = NOPE + ROPE
HR = ROPE // 2
QR, KVR = 256, 128
KB = 4
KD = 31
PH = 8
KEYS = 128
TOPK = 16
ROUTED = ((0, 2), (2, PH))
SLOTS = PH * TOPK
EXPERTS = KEYS * KEYS
EPS = 1e-6
LOWEST = -3.4028234663852886e38

A0, A1 = 0, QR + KVR + ROPE
Q0, Q1 = A1, A1 + GW
B0, B1 = Q1, Q1 + 2 * GW + 2 * HEADS
C0, C1 = B1, B1 + 2 * GW
D0, D1 = C1, C1 + 2 * GW
IN_CHUNKS = [(D0, D0 + 256), (D0 + 256, D1), (0, 128), (128, 256), (256, A1), (Q0, Q1),
             (B0, B0 + 256), (B0 + 256, B1), (C0, C0 + 256), (C0 + 256, C1)]
WIDTHS = [b - a for a, b in IN_CHUNKS] + [256] * 8
AFTER_D, AFTER_A, AFTER_Q, AFTER_B, AFTER_C, AFTER_OUT = 2, 5, 6, 8, 10, 14
NW = len(WIDTHS)
WSLOTS = 3
KEPT = 2
STREAMED = NW - KEPT
WMAX = KC * max(WIDTHS)

ROWS = [("g2", D), ("qkg", 2 * QK), ("cg", GW), ("cb", GW), ("dg", GW), ("db", GW),
        ("hg", GW), ("gb", 2 * HEADS)]
ROW_AT, _n = {}, 0
for _name, _w in ROWS:
    ROW_AT[_name] = (_n, _n + _w)
    _n += _w
ROW_W = _n
COLS = [("g1", KC), ("lat", 3), ("bw", 2 * KB), ("bb", 2), ("dw", 2 * KD), ("db", 2), ("bs", HEADS)]
COL_AT, _n = {}, 0
for _name, _w in COLS:
    COL_AT[_name] = (_n, _n + _w)
    _n += _w
COL_W = _n
MATS = [("uq", 2 * HEADS * QK), ("ukv", 2 * GW), ("ws", HEADS * P), ("sk", PH * KEYS)]
MAT_AT, _n = {}, 0
for _name, _w in MATS:
    MAT_AT[_name] = (_n, _n + _w)
    _n += _w
MAT_W = _n

ARENA = 8 * P + 3 * HEADS * (HD + 1) + GW
DIAGS = 4
GROUP = 4
RING = 8
LAPS = SLOTS // (2 * RING)
LATE_LINKS = 23
DVE_LINKS = 136
ACT_LINKS = 7


PER_LAP = 2 * RING // GROUP
CONV_PARTS = 8
SCHEDULE = [
    "dve.norm1 act.norm1 dve.r1a",
    "dve.xn1 pe.norm1 act.norm1T dve.r1b",
    "dve.setup act.rope pe.D0 dve.r1c",
    "pe.D1 act.D pe.A0 dve.r1d act.gates1",
    "dve.glu dve.r1e pe.A1",
    "dve.r1f act.hand1 act.A dve.conv0",
    "pe.Q dve.lat act.lat act.Q pe.lat dve.conv1 dve.conv2",
    "dve.bconv act.bconv dve.qk act.qk pe.B0",
    "pool.late pe.B1 pe.qkT dve.mask dve.conv3",
    "act.B act.qkT dve.bgate act.bgate pe.S dve.conv4 dve.bin",
    "dve.max act.exp pe.C0 dve.conv5",
    "pe.PV act.PT",
    "pe.bqk act.bqk dve.oA pe.C1 dve.rows act.rows dve.conv6",
    "act.C dve.vn0 pe.cols",
    "dve.decay act.decay act.vn pe.scores dve.conv7 dve.vn",
    "dve.weigh pe.num pe.sg pe.ydT",
    "dve.hidden",
    "dve.swish0 act.late dve.sg",
    "dve.swish1 act.swish dve.gateb dve.swish2",
    "pe.mixT act.mixT pe.out0",
    "pe.out1",
    "pe.out2",
    "pe.out3",
    "dve.norm2 act.norm2",
    "dve.xn2 pe.norm2 act.norm2T pe.q0",
    "pe.q1 act.q01",
    "pe.q2",
    "pe.q3 act.q23",
    "pe.sc act.sc",
    "dve.r0a dve.r0b dve.r0c",
    "dve.r0d act.gates0 dve.r0e dve.r0f",
    "",
]
LATE = {"dve.r1a", "dve.r1b", "dve.r1c", "dve.r1d", "act.gates1", "dve.r1e", "dve.r1f", "act.hand1"}
FIRST_LAPS = ROUTED[0][1] * TOPK // (2 * RING)
assert len(SCHEDULE) == SLOTS // GROUP


def nth(u, per, n):
    return u * per + n


def build(nc, x, positions, w_all, rows, cols, mats, bq, bk, uv, out):
    ctx = ExitStack()
    with ctx:
        def sb(name, shape, dt=F32):
            return ctx.enter_context(nc.sbuf_tensor(name, shape, dt))

        def sem(name):
            return ctx.enter_context(nc.semaphore(name))

        xs = sb("xs", [P, BLOCKS * D])
        xn = sb("xn", [P, D])
        xT = sb("xT", [P, D])
        mix = sb("mix", [P, D])
        wr = sb("wr", [P, WSLOTS * WMAX])
        kept = sb("kept", [P, KEPT * KC * WIDTHS[-1]])
        prow = sb("prow", [P, ROW_W])
        pcol = sb("pcol", [P, COL_W])
        pmat = sb("pmat", [P, MAT_W])
        wqd = sb("wqd", [P, 2 * P])
        wkd = sb("wkd", [P, 2 * P])
        ident = sb("ident", [P, P])
        tri = sb("tri", [P, P])
        key_no = sb("key_no", [P, P])
        qpos_i = sb("qpos_i", [P, UNITS], I32)
        qpos = sb("qpos", [P, UNITS])
        carry = sb("carry", [P, UNITS + 1])
        lbase = sb("lbase", [P, UNITS])
        sel = sb("sel", [HEADS, HEADS * P])
        pair_sel = sb("pair_sel", [HEADS, 2 * P])
        ones4 = sb("ones4", [HEADS, P])
        one_col = sb("one_col", [P, 1])
        eps_col = sb("eps_col", [P, 1])
        pos_i = sb("pos_i", [P, BLOCKS], I32)
        pos_f = sb("pos_f", [P, BLOCKS])
        freq = sb("freq", [P, HR])
        cs = sb("cs", [P, BLOCKS * ROPE])
        csb = sb("csb", [P, ROPE])
        ms = sb("ms", [P, 4])
        var = sb("var", [P, 24])
        rs = sb("rs", [P, 24])
        rt = sb("rt", [P, 24])
        pB = sb("pB", [P, B1 - B0])
        pC = sb("pC", [P, 2 * GW])
        KT = sb("KT", [QK, HEADS * SEQ])
        V = sb("V", [P, BLOCKS * GW])
        yt = sb("yt", [P, GW])
        big = sb("big", [P, HEADS * SEQ])
        arena = sb("arena", [P, ARENA])

        def views(tensor, *parts):
            at = 0
            for width, parts_, dt in parts:
                v = tensor[0:parts_, at:at + width]
                yield v if dt is F32 else v.bitcast(dt)
                at += width

        pA, lat, latT, qk = views(arena, (A1 - A0, P, F32), (QR + KVR, P, F32), (3 * P, P, F32), (8 * QK, P, F32))
        mask, qT = views(arena, (SEQ, P, F32), (HEADS * P, QK, F32))
        assert SEQ + HEADS * P <= A1 - A0 + QR + KVR + 3 * P
        qk_sq, rp = views(big, (8 * QK, P, F32), (4 * 8 * HR, P, F32))
        gr, wgv, nd, t1, hh = views(
            arena, (8 * P, HEADS, F32), (HEADS * (HD + 1), P, F32), (HEADS * (HD + 1), P, F32),
            (HEADS * (HD + 1), P, F32), (GW, P, F32))
        Dm, qkTb, ktok = views(big, (HEADS * P, P, F32), (4 * P, P, F32), (GW, P, F32))
        yb, eb, xcT, exo = views(xn, *[(GW, P, F32)] * 4)
        n_ = 2 * PH * TOPK
        (s_top, i_top, if_top, c_top, ci_top, c_hi, c_lo, f_hi, f_lo, e1, e2, eg) = views(
            arena, (n_, P, F32), (n_, P, U32), (n_, P, F32), (SLOTS, P, F32), (SLOTS, P, U32),
            (SLOTS, P, U32), (SLOTS, P, U32), *[(SLOTS, P, F32)] * 5)
        key_i, ang, ang_n, ang_c = views(big, (SEQ, P, I32), *[(BLOCKS * HR, P, F32)] * 3)
        ebd = yt
        h = mix
        yd = mix[:, 3 * GW:]
        mx = sb("mx", [P, HEADS])
        psum_p = sb("psum_p", [P, HEADS])
        rsum_p = sb("rsum_p", [P, HEADS])
        cbuf = sb("cbuf", [P, 2 * (KB - 1 + P)])
        gl = sb("gl", [P, 5 * 2 * HEADS])
        m_st = sb("m_st", [HEADS, 1])
        gc = sb("gc", [P, 24])
        v1 = sb("v1", [P, HEADS * (HD + 1)])
        den = sb("den", [P, HEADS])
        Cst = sb("Cst", [P, 2 * (HD + 1)])
        bn = sb("bn", [P, HEADS * 6])
        mv = sb("mv", [P, HEADS * 2])
        vn = sb("vn", [P, GW])
        glu = sb("glu", [P, 2 * (KD - 1 + P)])
        gs = sb("gs", [P, PH])
        xp = sb("xp", [P, D])
        gates = sb("gates", [P, SLOTS])
        eidx = sb("eidx", [P, SLOTS], I32)
        idxb = sb("idxb", [P, 2 * RING], I32)
        ring = sb("ring", [P, RING * 2 * D])
        dots = sb("dots", [P, RING])
        gel = sb("gel", [P, RING])
        acts = sb("acts", [P, RING])
        diag = sb("diag", [P, DIAGS * P])
        acc = ctx.enter_context(nc.psum_tensor("acc", [P, D], F32))
        ps = ctx.enter_context(nc.psum_tensor("ps", [P, 6 * 512], F32))

        def bank(n, a=0, b=512, p0=0, p1=P):
            return ps[p0:p1, n * 512 + a:n * 512 + b]

        def of_routed(t, g, width):
            lo, hi = ROUTED[g]
            return t[:, lo * width:hi * width]

        def row(name):
            a, b = ROW_AT[name]
            return prow[:, a:b]

        def col(name, i=None):
            a, b = COL_AT[name]
            return pcol[:, a:b] if i is None else pcol[:, a + i:a + i + 1]

        def mat(name):
            a, b = MAT_AT[name]
            return pmat[:, a:b]

        def wchunk(c):
            if c >= STREAMED:
                n = KC * WIDTHS[c]
                return kept[:, (c - STREAMED) * n:(c - STREAMED + 1) * n].rearrange("p (k n) -> p k n", k=KC)
            s = c % WSLOTS
            return wr[:, s * WMAX:s * WMAX + KC * WIDTHS[c]].rearrange("p (k n) -> p k n", k=KC)

        x_in = sem("x_in")
        x_rest_in = sem("x_rest_in")
        pcol_in = sem("pcol_in")
        kept_in = sem("kept_in")
        ident_clear = sem("ident_clear")
        ident_ready = sem("ident_ready")
        tables = sem("tables")
        tables_f = sem("tables_f")
        pos_in = sem("pos_in")
        ang_ready = sem("ang_ready")
        rope_ready = sem("rope_ready")
        params_in = sem("params_in")
        w_in = [sem(f"w_in{s}") for s in range(WSLOTS)]
        chunk_done = sem("chunk_done")
        dve_link = sem("dve_link")
        late_link = sem("late_link")
        act_link = sem("act_link")
        pool_link = sem("pool_link")
        h_ready = sem("h_ready")
        uses = ("norm1", "latents", "qk", "late", "spatial", "norm2")
        ms_ready = {n: sem(f"ms_{n}") for n in ("norm1", "latents", "norm2")}
        var_ready = {n: sem(f"var_{n}") for n in ("qk", "late", "spatial")}
        rs_ready = {n: sem(f"rs_{n}") for n in uses}
        xn_ready = sem("xn_ready")
        xT_ps = sem("xT_ps")
        xT_ready = sem("xT_ready")
        pB_ready = sem("pB_ready")
        pC_ready = sem("pC_ready")
        cbuf_ready = sem("cbuf_ready")
        ebd_ready = sem("ebd_ready")
        glu_ready = sem("glu_ready")
        lat_ready = sem("lat_ready")
        latT_ps = sem("latT_ps")
        latT_ready = sem("latT_ready")
        qkv_ps = sem("qkv_ps")
        qk_evac = sem("qk_evac")
        V_ready = sem("V_ready")
        qk_ready = sem("qk_ready")
        qkT_ps = sem("qkT_ps")
        qkT_ready = sem("qkT_ready")
        S_ps = sem("S_ps")
        mx_ready = sem("mx_ready")
        P_ready = sem("P_ready")
        PT_ps = sem("PT_ps")
        PT_ready = sem("PT_ready")
        o_ps = sem("o_ps")
        yb_ready = sem("yb_ready")
        eb_ready = sem("eb_ready")
        xcT_ready = sem("xcT_ready")
        negz_ready = sem("negz_ready")
        softplus_ready = sem("softplus_ready")
        gates_ready = sem("gates_ready")
        gT_ps = sem("gT_ps")
        rows_ready = sem("rows_ready")
        EN_ready = sem("EN_ready")
        col_ps = sem("col_ps")
        y_ready = sem("y_ready")
        D_ready = sem("D_ready")
        qkb_ps = sem("qkb_ps")
        qkb_ready = sem("qkb_ready")
        SI_ps = sem("SI_ps")
        Wt_ready = sem("Wt_ready")
        wgv_ready = sem("wgv_ready")
        num_ps = sem("num_ps")
        st_ps = sem("st_ps")
        vn_ready = sem("vn_ready")
        sg_ps = sem("sg_ps")
        yd_ready = sem("yd_ready")
        ydT_ps = sem("ydT_ps")
        yt_ready = sem("yt_ready")
        eyt_ready = sem("eyt_ready")
        mix_ready = sem("mix_ready")
        h2_ready = sem("h2_ready")
        qpT_ready = sem("qpT_ready")
        sc_ps = sem("sc_ps")
        scs_ready = sem("scs_ready")
        top_ready = sem("top_ready")
        eg_ready = sem("eg_ready")
        eidx_ready = sem("eidx_ready")
        eg_norm_ready = sem("eg_norm_ready")
        handover = sem("handover")
        row_in = [sem(f"row_in{s}") for s in range(RING)]
        row_used = sem("row_used")
        pool_gate = sem("pool_gate")
        dve_hold = sem("dve_hold")
        pe_hold = sem("pe_hold")
        sp_hold = sem("sp_hold")
        idx_ready = sem("idx_ready")
        dot_done = sem("dot_done")
        gelu_done = sem("gelu_done")
        act_done = sem("act_done")
        diag_ready = sem("diag_ready")
        x_done = sem("x_done")
        out_done = sem("out_done")

        def interleave(eng, pieces, turn, close, handoff):
            mine = [[(pieces[name], name in LATE) for name in gap.split() if name in pieces] for gap in SCHEDULE]
            for gap in mine:
                for piece, late in gap:
                    if not late:
                        piece(0)
            handoff(0)
            with eng.Fori(1, UNITS) as u:
                for group, gap in enumerate(mine):
                    for piece, late in gap:
                        piece(u)
                    if group == 0:
                        close(u)
                    turn(u - 1, group // PER_LAP, group % PER_LAP)
                handoff(u)
            for group in range(FIRST_LAPS * PER_LAP):
                for piece, late in mine[group]:
                    if late:
                        piece(UNITS)
                if group == 0:
                    close(UNITS)
                turn(UNITS - 1, group // PER_LAP, group % PER_LAP)
            if "pool.late" in pieces:
                pieces["pool.late"](UNITS)
            with eng.Fori(FIRST_LAPS, LAPS) as j:
                for q in range(PER_LAP):
                    turn(UNITS - 1, j, q)
            close(UNITS + 1)

        block = ctx.enter_context(nc.Block())

        @block.sync
        def _(sp):
            sp.dma_start(pos_i[:, :], positions.rearrange("a (b p) -> p (a b)", p=P),
                         allow_slow_non_contiguous=True).then_inc(pos_in, 16)
            x_src = x.rearrange("a (b p) d -> p (a b) d", p=P)
            xv = xs[:, :].rearrange("p (b d) -> p b d", b=BLOCKS)
            sp.dma_start(xv[:, 0, :], x_src[:, 0, :]).then_inc(x_in, 16)

            def load_cols(layer):
                src = cols[layer:layer + 1, :, :].rearrange("a p n -> (a p) n")
                sp.dma_start(pcol[:, :], src).then_inc(pcol_in, 16)

            def chunk_source(layer, c):
                n = KC * WIDTHS[c]
                at = sum(KC * P * w for w in WIDTHS[:c])
                return w_all[ds(layer, 1), at:at + P * n].rearrange("a (p n) -> (a p) n", p=P)

            def load_params(layer):
                one = slice(layer, layer + 1)
                sp.dma_start(prow[:, :], rows[one, :].to_broadcast([P, ROW_W])).then_inc(params_in, 16)
                sp.dma_start(pmat[:, :], mats[one, :, :].rearrange("a p n -> (a p) n")).then_inc(params_in, 16)
                for tile, src in ((wqd, bq), (wkd, bk)):
                    for half in range(2):
                        p0 = half * HD
                        dst = tile[p0:p0 + HD, :].rearrange("p (j n) -> p j n", j=2)[:, :, p0:p0 + HD]
                        sp.dma_start(dst, src[one, half, :, :].rearrange("a p (j n) -> (a p) j n", j=2)) \
                            .then_inc(params_in, 16)

            def load_kept(layer):
                n = KC * WIDTHS[-1]
                for i in range(KEPT):
                    sp.dma_start(kept[:, i * n:(i + 1) * n], chunk_source(layer, STREAMED + i)).then_inc(kept_in, 16)

            def load_weights(u, first=0, end=STREAMED):
                for c in range(first, end):
                    if u is not 0 or c >= WSLOTS:
                        sp.wait_ge(chunk_done, nth(u, NW, c + 1 - WSLOTS))
                        sp.sem_inc(sp_hold, 1)
                    n = KC * WIDTHS[c]
                    s = c % WSLOTS
                    sp.dma_start(wr[:, s * WMAX:s * WMAX + n], chunk_source(u // BLOCKS, c)).then_inc(w_in[s], 16)

            load_cols(0)
            load_weights(0, 0, WSLOTS)
            sp.wait_ge(tables, 2)
            load_params(0)
            load_weights(0, WSLOTS, 2 * WSLOTS)
            sp.dma_start(xv[:, 1:, :], x_src[:, 1:, :]).then_inc(x_rest_in, 16)
            load_kept(0)
            load_weights(0, 2 * WSLOTS)
            for layer in range(DEPTH):
                if layer:
                    u = layer * BLOCKS
                    sp.wait_ge(xn_ready, u * 2)
                    sp.wait_ge(sc_ps, u)
                    load_cols(layer)
                    load_params(layer)
                    load_weights(u, 0, WSLOTS)
                    sp.wait_ge(chunk_done, u * NW)
                    load_kept(layer)
                    load_weights(u, WSLOTS)
                with sp.Fori(layer * BLOCKS + 1, (layer + 1) * BLOCKS) as u:
                    load_weights(u)
            o = out.rearrange("a (b p) d -> p (a b) d", p=P)
            sp.wait_ge(x_done, UNITS)
            sp.dma_start(o[:, 0:BLOCKS - 1, :], xv[:, 0:BLOCKS - 1, :]).then_inc(out_done, 16)
            sp.wait_ge(x_done, UNITS + 1)
            sp.dma_start(o[:, BLOCKS - 1, :], xv[:, BLOCKS - 1, :]).then_inc(out_done, 16)
            sp.wait_ge(out_done, 32)

        @block.gpsimd
        def _(pool):
            nc.gpsimd.memset(eps_col[:, :], EPS)
            nc.gpsimd.memset(ident[:, :], 0.0).then_inc(ident_clear, 1)
            pool.wait_ge(ident_clear, 1)
            nc.gpsimd.affine_select(out=ident[:, :], in_=ident[:, :], compare_op=ALU.not_equal, fill=1.0, base=0,
                                    pattern=[[-1, P]], channel_multiplier=1).then_inc(ident_ready, 1)
            nc.gpsimd.memset(wqd[:, :], 0.0).then_inc(tables, 1)
            nc.gpsimd.memset(wkd[:, :], 0.0).then_inc(tables, 1)
            nc.gpsimd.memset(tri[:, :], 1.0)
            nc.gpsimd.memset(sel[:, :], 0.0)
            nc.gpsimd.memset(pair_sel[:, :], 0.0)
            nc.gpsimd.memset(carry[:, :], 1.0)
            nc.gpsimd.memset(lbase[:, 0:BLOCKS], 0.0)
            nc.gpsimd.memset(lbase[:, BLOCKS:UNITS], float(EXPERTS)).then_inc(pool_link, 1)
            pool.wait_ge(pool_link, 1)
            for b in range(0, UNITS + 1, BLOCKS):
                nc.gpsimd.memset(carry[:, b:b + 1], 0.0)
            nc.gpsimd.affine_select(out=tri[:, :], in_=tri[:, :], compare_op=ALU.is_ge, fill=0.0, base=0,
                                    pattern=[[1, P]], channel_multiplier=-1)
            for t, n in ((sel, P), (pair_sel, HD)):
                v = t[:, :].rearrange("p (h n) -> p h n", h=HEADS)
                nc.gpsimd.affine_select(out=v, in_=v, compare_op=ALU.not_equal, fill=1.0, base=0,
                                        pattern=[[-1, HEADS], [0, n]], channel_multiplier=1)
            nc.gpsimd.iota(key_i[:, :], pattern=[[1, SEQ]], base=0, channel_multiplier=0)
            nc.gpsimd.iota(qpos_i[:, :], pattern=[[0, DEPTH], [P, BLOCKS]], base=0, channel_multiplier=1)
            for j in range(HR):
                f = np.float32(10000.0) ** (np.float32(-2 * j) / np.float32(ROPE))
                nc.gpsimd.memset(freq[:, j:j + 1], float(f))
            nc.gpsimd.memset(ones4[:, :], 1.0)
            nc.gpsimd.memset(one_col[:, :], 1.0)
            for t in (KT, V, cbuf, glu, Cst, m_st):
                nc.gpsimd.memset(t[:, :], 0.0)
            nc.gpsimd.memset(v1[:, :], 1.0).then_inc(tables, 1)

            def turn(u, j, q):
                at = j * 2 * RING + q * GROUP
                nc.gpsimd.tensor_copy(idxb[:, q * GROUP:(q + 1) * GROUP],
                                      eidx[:, ds(at, GROUP)]).then_inc(idx_ready, 1)
                pool.wait_ge(idx_ready, nth(u, SLOTS // GROUP, j * PER_LAP + q + 1))
                for i in range(q * GROUP, (q + 1) * GROUP):
                    s = i % RING
                    pool.wait_ge(row_used, nth(u, SLOTS, j * 2 * RING + i + 1))
                    pool.sem_inc(pool_gate, 1)
                    nc.gpsimd.indirect_dma_start(
                        out=ring[:, s * 2 * D:(s + 1) * 2 * D], out_offset=None, in_=uv[:, :],
                        in_offset=bass.IndirectOffsetOnAxis(ap=idxb[:, i:i + 1], axis=0),
                    ).then_inc(row_in[s], 16)

            def handoff(u):
                pool.wait_ge(eidx_ready, nth(u, 2, 1))
                pool.sem_inc(pool_gate, 1)

            def later_indices(u):
                if u is not 0:
                    pool.wait_ge(eidx_ready, nth(u - 1, 2, 2))
                    pool.sem_inc(pool_gate, 1)

            interleave(pool, {"pool.late": later_indices}, turn, lambda u: None, handoff)

        @block.scalar
        def _(act):
            links = [0]
            sc = nc.scalar

            def link(u, ins):
                links[0] += 1
                ins.then_inc(act_link, 1)
                act.wait_ge(act_link, nth(u, ACT_LINKS, links[0]))

            def rsqrt(u, k, a, b):
                act.wait_ge(var_ready[k], nth(u, 1, 1))
                link(u, sc.activation(rs[:, a:b], var[:, a:b], ACT.Ln))
                sc.activation(rs[:, a:b], rs[:, a:b], ACT.Exp, scale=-0.5).then_inc(rs_ready[k], 1)

            def rsqrt_of_mean(u, k, i, at, b):
                act.wait_ge(ms_ready[k], nth(u, 1, 1))
                link(u, sc.activation(rs[:, at:b], ms[:, i:i + b - at], ACT.Ln, bias=eps_col[:, 0:1]))
                sc.activation(rs[:, at:b], rs[:, at:b], ACT.Exp, scale=-0.5).then_inc(rs_ready[k], 1)

            def evac_xT1(u):
                act.wait_ge(pcol_in, nth(u // BLOCKS, 16, 16))
                for n in range(2):
                    act.wait_ge(xT_ps, nth(u, 6, n + 1))
                    for k in range(4 * n, 4 * n + 4):
                        last = sc.activation(xT[:, k * P:(k + 1) * P], ps[:, k * P:(k + 1) * P], ACT.Copy,
                                             scale=col("g1", k))
                    last.then_inc(xT_ready, 1)

            def evac_xT(u, k):
                for n in range(2):
                    act.wait_ge(xT_ps, nth(u, 6, 2 * k + n + 1))
                    sc.activation(xT[:, n * 512:(n + 1) * 512], bank(n), ACT.Copy).then_inc(xT_ready, 1)

            def rope(u):
                if u is not 0:
                    return
                act.wait_ge(ang_ready, 1)
                c4 = cs[:, :].rearrange("p (b c f) -> p b c f", b=BLOCKS, c=2)
                sc.activation(c4[:, :, 0, :], ang_c[:, :].rearrange("p (b f) -> p b f", b=BLOCKS), ACT.Sin)
                sc.activation(c4[:, :, 1, :], ang[:, :].rearrange("p (b f) -> p b f", b=BLOCKS),
                              ACT.Sin).then_inc(rope_ready, 1)

            def norm1(u):
                links[0] = 0
                act.wait_ge(h_ready, nth(u, 1, 1))
                sc.activation(xT[:, :], h[:, :], ACT.Square, scale=float(D ** -0.5),
                              accum_out=ms[:, 0:1]).then_inc(ms_ready["norm1"], 1)
                if u is 0:
                    act.wait_ge(ident_ready, 1)
                rsqrt_of_mean(u, "norm1", 0, 0, 1)

            def exp_d(u):
                act.wait_ge(chunk_done, nth(u, NW, AFTER_D))
                sc.activation(ebd[:, :], bank(0, 256, 512), ACT.Exp, scale=-1.0).then_inc(ebd_ready, 1)

            def latents(u):
                act.wait_ge(chunk_done, nth(u, NW, AFTER_A))
                sc.activation(pA[:, :], bank(2, 0, A1 - A0), ACT.Copy)
                sc.activation(mix[:, 0:QR], bank(2, 0, QR), ACT.Square, scale=float(QR ** -0.5),
                              accum_out=ms[:, 1:2])
                sc.activation(mix[:, QR:QR + KVR], bank(2, QR, QR + KVR), ACT.Square, scale=float(KVR ** -0.5),
                              accum_out=ms[:, 2:3]).then_inc(ms_ready["latents"], 1)

            def conv_input(u):
                act.wait_ge(chunk_done, nth(u, NW, AFTER_Q))
                if u is not 0:
                    act.wait_ge(xcT_ready, u)
                sc.activation(cbuf[:, :].rearrange("p (j t) -> p j t", j=2)[:, :, KB - 1:],
                              bank(3, 0, 2 * P).rearrange("p (j t) -> p j t", j=2), ACT.Copy).then_inc(cbuf_ready, 1)

            def mlstm_input(u):
                act.wait_ge(chunk_done, nth(u, NW, AFTER_B))
                sc.activation(pB[:, 0:512], bank(4), ACT.Copy)
                sc.activation(pB[:, 512:520], bank(3, 256, 264), ACT.Copy).then_inc(pB_ready, 1)

            def gelu_c(u):
                act.wait_ge(chunk_done, nth(u, NW, AFTER_C))
                sc.activation(pC[:, :], bank(0), ACT.Gelu_apprx_tanh).then_inc(pC_ready, 1)

            def latents_out(u):
                rsqrt_of_mean(u, "latents", 1, 1, 3)
                act.wait_ge(latT_ps, nth(u, 1, 1))
                for k in range(3):
                    last = sc.activation(latT[:, k * P:(k + 1) * P], bank(1, k * P, (k + 1) * P), ACT.Copy,
                                         scale=col("lat", k))
                last.then_inc(latT_ready, 1)
                qk3 = qk[:, :].rearrange("p (h d) -> p h d", h=8)
                act.wait_ge(qkv_ps, nth(u, 2, 1))
                sc.activation(qk[:, 0:HEADS * QK], bank(2, 0, HEADS * QK), ACT.Copy)
                act.wait_ge(qkv_ps, nth(u, 2, 2))
                kv3 = bank(1).rearrange("p (h d) -> p h d", h=HEADS)
                sc.activation(qk3[:, HEADS:8, 0:NOPE], kv3[:, :, 0:NOPE], ACT.Copy).then_inc(qk_evac, 1)
                sc.activation(V[:, ds((u % BLOCKS) * GW, GW)].rearrange("p (h d) -> p h d", h=HEADS),
                              kv3[:, :, NOPE:], ACT.Copy).then_inc(V_ready, 1)

            def qk_root(u):
                rsqrt(u, "qk", 3, 11)

            def qkT_out(u):
                act.wait_ge(qkT_ps, nth(u, 2, 1))
                sc.activation(qT[:, :], bank(2, 0, 512, 0, QK), ACT.Copy).then_inc(qkT_ready, 1)
                act.wait_ge(qkT_ps, nth(u, 2, 2))
                sc.activation(KT[:, :].rearrange("p (h t) -> p h t", h=HEADS)[:, :, ds((u % BLOCKS) * P, P)],
                              bank(1, 0, 512, 0, QK).rearrange("p (h t) -> p h t", h=HEADS),
                              ACT.Copy).then_inc(qkT_ready, 1)

            def exp_scores(u):
                act.wait_ge(mx_ready, nth(u, 1, 1))
                for hd in range(HEADS):
                    sc.activation(big[:, hd * SEQ:(hd + 1) * SEQ], big[:, hd * SEQ:(hd + 1) * SEQ], ACT.Exp,
                                  bias=mx[:, hd:hd + 1], scale=float(QK ** -0.5),
                                  accum_out=psum_p[:, hd:hd + 1]).then_inc(P_ready, 1)

            def probsT_out(u):
                for hd in range(HEADS):
                    act.wait_ge(PT_ps, nth(u, HEADS, hd + 1))
                    sc.activation(big[:, hd * SEQ:(hd + 1) * SEQ], bank(2 + hd), ACT.Copy).then_inc(PT_ready, 1)

            def conv_exp(u):
                act.wait_ge(yb_ready, nth(u, 1, 1))
                sc.activation(eb[:, :], yb[:, :], ACT.Exp, scale=-1.0).then_inc(eb_ready, 1)

            def gate_softplus(u):
                act.wait_ge(pB_ready, nth(u, 1, 1))
                sc.activation(exo[:, :], pB[:, GW:2 * GW], ACT.Exp, scale=-1.0)
                act.wait_ge(negz_ready, nth(u, 1, 1))
                link(u, sc.activation(gl[:, 24:28], gl[:, 16:20], ACT.Exp))
                sc.activation(gl[:, 28:32], gl[:, 24:28], ACT.Ln, bias=one_col[:, 0:1]).then_inc(softplus_ready, 1)

            def qkb_out(u):
                act.wait_ge(qkb_ps, nth(u, 1, 1))
                sc.activation(qkTb[:, 0:2 * P], bank(3, 0, 2 * P), ACT.Copy)
                sc.activation(qkTb[:, 2 * P:4 * P], bank(3, 2 * P, 4 * P), ACT.Copy, scale=float(HD ** -0.5))
                sc.activation(ktok[:, :], bank(4, 0, GW), ACT.Copy, scale=float(HD ** -0.5)).then_inc(qkb_ready, 1)

            def row_exps(u):
                act.wait_ge(rows_ready, nth(u, 1, 1))
                sc.activation(gr[:, 6 * P:7 * P], gr[:, 4 * P:5 * P], ACT.Exp, bias=m_st[:, 0:1], scale=-1.0)
                sc.activation(gr[:, 7 * P:8 * P], gr[:, 5 * P:6 * P], ACT.Exp, scale=-1.0).then_inc(EN_ready, 1)

            def decay_exp(u):
                act.wait_ge(y_ready, nth(u, 1, 1))
                sc.activation(Dm[:, :], Dm[:, :], ACT.Exp, scale=-1.0).then_inc(D_ready, 1)

            def swish(u):
                act.wait_ge(yt_ready, nth(u, 1, 1))
                sc.activation(vn[:, :], yt[:, :], ACT.Exp, scale=-1.0).then_inc(eyt_ready, 1)

            def norm2(u):
                act.wait_ge(h2_ready, nth(u, 1, 1))
                sc.activation(xT[:, :], h[:, :], ACT.Square, scale=float(D ** -0.5),
                              accum_out=ms[:, 3:4]).then_inc(ms_ready["norm2"], 1)
                rsqrt_of_mean(u, "norm2", 3, 20, 21)

            def queries_out(u, n):
                act.wait_ge(chunk_done, nth(u, NW, AFTER_OUT + 2 * n + 2))
                sc.activation(mix[:, n * 512:(n + 1) * 512], bank(4 + n), ACT.Copy).then_inc(qpT_ready, 1)

            def key_scores_out(u):
                act.wait_ge(sc_ps, nth(u, 1, 1))
                for g, (lo, hi) in enumerate(ROUTED):
                    for half in range(2):
                        to = (2 * lo + half * (hi - lo)) * KEYS
                        for h0 in range(lo, hi, 4):
                            h0 -= h0 % 4
                            a, b = max(lo, h0), min(hi, h0 + 4)
                            n = (b - a) * KEYS
                            src = bank(2 + h0 // 4 * 2 + half, (a - h0) * KEYS, (b - h0) * KEYS)
                            last = sc.activation(big[:, to:to + n], src, ACT.Copy)
                            to += n
                    last.then_inc(scs_ready, 1)

            def gate_exps(u, g):
                act.wait_ge(top_ready, nth(u, 2, g + 1))
                e = of_routed(eg, g, TOPK)
                sc.activation(e, e, ACT.Exp).then_inc(eg_ready, 1)
                if g == 0:
                    assert links[0] == ACT_LINKS, links

            def gates_out(u, g):
                act.wait_ge(eg_norm_ready, nth(u, 2, g + 1))
                sc.activation(of_routed(gates, g, TOPK), of_routed(eg, g, TOPK), ACT.Copy)

            def turn(u, j, q):
                for i in range(q * GROUP, (q + 1) * GROUP):
                    s, n = i % RING, j * 2 * RING + i
                    act.wait_ge(dot_done, nth(u, SLOTS, n + 1))
                    sc.activation(gel[:, s:s + 1], dots[:, s:s + 1], ACT.Gelu_apprx_tanh).then_inc(gelu_done, 1)
                    act.wait_ge(gelu_done, nth(u, SLOTS, n + 1))
                    sc.activation(acts[:, s:s + 1], gel[:, s:s + 1], ACT.Copy,
                                  scale=gates[:, ds(n, 1)]).then_inc(act_done, 1)
                    act.wait_ge(act_done, nth(u, SLOTS, n + 1))
                    act.wait_ge(row_used, nth(u, SLOTS, RING + n + 1 - DIAGS))
                    d = i % DIAGS
                    sc.activation(diag[:, d * P:(d + 1) * P], ident[:, :], ACT.Copy,
                                  scale=acts[:, s:s + 1]).then_inc(diag_ready, 1)

            def handoff(u):
                gates_out(u, 0)
                sc.activation(xp[:, :], xn[:, :], ACT.Copy).then_inc(handover, 1)

            interleave(act, {
                "act.norm1": norm1, "act.D": exp_d, "act.A": latents, "act.Q": conv_input, "act.lat": latents_out,
                "act.qk": qk_root, "act.B": mlstm_input, "act.qkT": qkT_out, "act.exp": exp_scores,
                "act.PT": probsT_out, "act.C": gelu_c, "act.rope": rope, "act.bconv": conv_exp,
                "act.bgate": gate_softplus, "act.bqk": qkb_out,
                "act.vn": lambda u: rsqrt(u, "spatial", 19, 20), "act.rows": row_exps, "act.decay": decay_exp,
                "act.late": lambda u: rsqrt(u, "late", 11, 19), "act.swish": swish,
                "act.mixT": lambda u: evac_xT(u, 1), "act.norm2": norm2, "act.q01": lambda u: queries_out(u, 0),
                "act.q23": lambda u: queries_out(u, 1), "act.sc": key_scores_out, 
                "act.gates0": lambda u: gate_exps(u, 0), "act.gates1": lambda u: gate_exps(u - 1, 1),
                "act.hand1": lambda u: gates_out(u - 1, 1), "act.norm1T": evac_xT1,
                "act.norm2T": lambda u: evac_xT(u, 2),
            }, turn, lambda u: None, handoff)

        @block.tensor
        def _(pe):
            T = nc.tensor

            def transposes(src, u, k):
                for n in range(2):
                    for i in range(4):
                        c = n * 4 + i
                        last = T.transpose(bank(n, i * P, (i + 1) * P), src[:, c * P:(c + 1) * P], ident[:, :])
                    last.then_inc(xT_ps, 1)

            def wait_w(u, c):
                if c >= STREAMED:
                    pe.wait_ge(kept_in, nth(u // BLOCKS, 16 * KEPT, 16 * KEPT))
                    return
                s = c % WSLOTS
                per = len(range(s, STREAMED, WSLOTS))
                pe.wait_ge(w_in[s], nth(u, 16 * per, 16 * (c // WSLOTS + 1)))

            def tokens_by(c, n0, n1, dst):
                w = wchunk(c)
                for k in range(KC):
                    last = T.matmul(dst, xT[:, k * P:(k + 1) * P], w[:, k, n0:n1], start=(k == 0), stop=(k == KC - 1))
                return last

            def channels_by(c, b, a, blocks=2):
                w = wchunk(c)
                for i in range(blocks):
                    for k in range(KC):
                        last = T.matmul(bank(b, a + i * P, a + (i + 1) * P), w[:, k, i * P:(i + 1) * P],
                                        xT[:, k * P:(k + 1) * P], start=(k == 0), stop=(k == KC - 1))
                return last

            def norm1(u):
                pe.wait_ge(xn_ready, nth(u, 2, 1))
                transposes(xn, u, 0)
                pe.wait_ge(xT_ready, nth(u, 6, 2))

            def in_A(u, *cs_):
                for c in cs_:
                    at = IN_CHUNKS[c][0]
                    wait_w(u, c)
                    tokens_by(c, 0, WIDTHS[c], bank(2, at, at + WIDTHS[c])).then_inc(chunk_done, 1)

            def in_Q(u):
                if u is 0:
                    pe.wait_ge(tables, 3)
                wait_w(u, AFTER_A)
                channels_by(AFTER_A, 3, 0).then_inc(chunk_done, 1)

            def in_B(u, n):
                c = AFTER_Q + n
                wait_w(u, c)
                last = tokens_by(c, 0, 256, bank(4, n * 256, (n + 1) * 256))
                if n == 1:
                    pe.wait_ge(cbuf_ready, nth(u, 1, 1))
                    last = tokens_by(c, 256, 256 + 2 * HEADS, bank(3, 256, 256 + 2 * HEADS))
                last.then_inc(chunk_done, 1)

            def in_C(u, n):
                c = AFTER_B + n
                if n == 0:
                    pe.wait_ge(glu_ready, nth(u, 1, 1))
                wait_w(u, c)
                tokens_by(c, 0, 256, bank(0, n * 256, (n + 1) * 256)).then_inc(chunk_done, 1)

            def in_D(u, n):
                wait_w(u, n)
                channels_by(n, 0, n * 256).then_inc(chunk_done, 1)

            def latents(u):
                pe.wait_ge(lat_ready, nth(u, 1, 1))
                for k in range(3):
                    last = T.transpose(bank(1, k * P, (k + 1) * P), lat[:, k * P:(k + 1) * P], ident[:, :])
                last.then_inc(latT_ps, 1)
                pe.wait_ge(latT_ready, nth(u, 1, 1))
                for k in range(2):
                    last = T.matmul(bank(2, 0, HEADS * QK), latT[:, k * P:(k + 1) * P],
                                    mat("uq")[:, k * HEADS * QK:(k + 1) * HEADS * QK], start=(k == 0), stop=(k == 1))
                last.then_inc(qkv_ps, 1)
                T.matmul(bank(1), latT[:, 2 * P:3 * P], mat("ukv"), start=True, stop=True).then_inc(qkv_ps, 1)

            def qk_transposes(u):
                pe.wait_ge(qk_ready, nth(u, 1, 1))
                pe.wait_ge(V_ready, nth(u, 1, 1))
                for n in range(2):
                    for hd in range(HEADS):
                        c = n * HEADS + hd
                        last = T.transpose(bank(2 - n, hd * P, (hd + 1) * P, 0, QK), qk[:, c * QK:(c + 1) * QK],
                                           ident[:, :])
                    last.then_inc(qkT_ps, 1)

            def scores(u):
                pe.wait_ge(qkT_ready, nth(u, 2, 2))
                pe.wait_ge(pB_ready, nth(u, 1, 1))
                for hd in range(HEADS):
                    last = T.matmul(bank(2 + hd), qT[:, hd * P:(hd + 1) * P], KT[:, hd * SEQ:(hd + 1) * SEQ],
                                    start=True, stop=True)
                last.then_inc(S_ps, 1)

            def attend(u):
                for hd in range(HEADS):
                    pe.wait_ge(P_ready, nth(u, HEADS, hd + 1))
                    for k in range(BLOCKS):
                        last = T.transpose(bank(2 + hd, k * P, (k + 1) * P),
                                           big[:, hd * SEQ + k * P:hd * SEQ + (k + 1) * P], ident[:, :])
                    last.then_inc(PT_ps, 1)
                for hd in range(HEADS):
                    pe.wait_ge(PT_ready, nth(u, HEADS, hd + 1))
                    for k in range(BLOCKS):
                        last = T.matmul(bank(1, hd * HD, (hd + 1) * HD),
                                        big[:, hd * SEQ + k * P:hd * SEQ + (k + 1) * P],
                                        V[:, k * GW + hd * HD:k * GW + (hd + 1) * HD],
                                        start=(k == 0), stop=(k == BLOCKS - 1))
                last.then_inc(o_ps, 1)

            def mlstm_qk(u):
                pe.wait_ge(gates_ready, nth(u, 1, 1))
                T.transpose(bank(5, 0, P, 0, HEADS), gl[:, 8:12], ident[:, :])
                T.transpose(bank(5, P, 2 * P, 0, HEADS), gl[:, 36:40], ident[:, :]).then_inc(gT_ps, 1)
                pe.wait_ge(xcT_ready, nth(u, 1, 1))
                for j in range(2):
                    T.matmul(bank(3, j * P, (j + 1) * P), wqd[:, j * P:(j + 1) * P], xcT[:, j * P:(j + 1) * P],
                             start=True, stop=True)
                    T.matmul(bank(3, (2 + j) * P, (3 + j) * P), wkd[:, j * P:(j + 1) * P],
                             xcT[:, j * P:(j + 1) * P], start=True, stop=True)
                    last = T.matmul(bank(4, j * P, (j + 1) * P), xcT[:, j * P:(j + 1) * P],
                                    wkd[:, j * P:(j + 1) * P], start=True, stop=True)
                last.then_inc(qkb_ps, 1)

            def mlstm_cols(u):
                pe.wait_ge(EN_ready, nth(u, 1, 1))
                pe.sem_inc(pe_hold, 1)
                for i, r in enumerate((3, 6, 7)):
                    T.transpose(bank(5, 4 * i, 4 * i + 4), gr[:, r * P:(r + 1) * P], ident[0:HEADS, 0:HEADS])
                for j in range(2):
                    T.matmul(bank(5, 16 + j, 17 + j), pair_sel[:, j * P:(j + 1) * P], gr[:, 7 * P - 1:7 * P],
                             start=True, stop=True)
                for hd in range(HEADS):
                    last = T.matmul(bank(2, hd * P, (hd + 1) * P), sel[:, hd * P:(hd + 1) * P],
                                    gr[:, 4 * P:5 * P], start=True, stop=True)
                last.then_inc(col_ps, 1)

            def mlstm_scores(u):
                pe.wait_ge(qkb_ready, nth(u, 1, 1))
                pe.wait_ge(y_ready, nth(u, 1, 1))
                v = HD + 1
                for hd in range(HEADS):
                    j, p0 = hd // 2, hd % 2 * HD
                    T.matmul(bank((5, 3)[hd % 2], j * P, (j + 1) * P), qkTb[p0:p0 + HD, (2 + j) * P:(3 + j) * P],
                             qkTb[p0:p0 + HD, j * P:(j + 1) * P], start=True, stop=True)
                    last = T.matmul(bank((4, 2)[hd % 2], j * v, (j + 1) * v), qkTb[p0:p0 + HD, j * P:(j + 1) * P],
                                    Cst[p0:p0 + HD, j * v:(j + 1) * v], start=True, stop=True)
                last.then_inc(SI_ps, 1)

            def mlstm_num(u):
                v = HD + 1
                pe.wait_ge(wgv_ready, nth(u, 1, 1))
                for j in range(2):
                    last = T.matmul(bank(1, j * 2 * v, (j + 1) * 2 * v), ktok[:, j * P:(j + 1) * P],
                                    wgv[:, j * 2 * v:(j + 1) * 2 * v], start=True, stop=True)
                last.then_inc(st_ps, 1)
                pe.wait_ge(Wt_ready, nth(u, 1, 1))
                pe.wait_ge(pC_ready, nth(u, 1, 1))
                for hd in range(HEADS):
                    last = T.matmul(bank(0, hd * v, (hd + 1) * v), Dm[:, hd * P:(hd + 1) * P],
                                    v1[:, hd * v:(hd + 1) * v], start=True, stop=True)
                last.then_inc(num_ps, 1)

            def spatial(u):
                pe.wait_ge(vn_ready, nth(u, 1, 1))
                for hd in range(HEADS):
                    last = T.matmul(bank(3, hd * HD, (hd + 1) * HD), mat("ws")[:, hd * P:(hd + 1) * P],
                                    vn[:, hd * HD:(hd + 1) * HD], start=True, stop=True)
                last.then_inc(sg_ps, 1)

            def conv_transposes(u):
                pe.wait_ge(yd_ready, nth(u, 1, 1))
                for j in range(2):
                    last = T.transpose(bank(5, j * P, (j + 1) * P), yd[:, j * P:(j + 1) * P], ident[:, :])
                last.then_inc(ydT_ps, 1)
                if u is 0:
                    clear_acc().then_inc(row_used, RING)

            def mix_transposes(u):
                pe.wait_ge(mix_ready, nth(u, 1, 1))
                transposes(mix, u, 1)
                pe.wait_ge(xT_ready, nth(u, 6, 4))

            def w_out(u, n):
                wait_w(u, AFTER_C + n)
                tokens_by(AFTER_C + n, 0, 256, bank(2 + n // 2, n % 2 * 256, n % 2 * 256 + 256)) \
                    .then_inc(chunk_done, 1)

            def norm2(u):
                pe.wait_ge(xn_ready, nth(u, 2, 2))
                transposes(xn, u, 2)
                pe.wait_ge(xT_ready, nth(u, 6, 6))

            def queries(u, n):
                wait_w(u, AFTER_OUT + n)
                channels_by(AFTER_OUT + n, 4 + n // 2, n % 2 * 256).then_inc(chunk_done, 1)

            def key_scores(u):
                pe.wait_ge(qpT_ready, nth(u, 2, 2))
                for hd in range(PH):
                    for half in range(2):
                        p0 = half * HD
                        i = (hd // 4 * 2 + half) * 4 + hd % 4
                        last = T.matmul(bank(2 + i // 4, i % 4 * P, (i % 4 + 1) * P),
                                        mix[p0:p0 + HD, hd * P:(hd + 1) * P],
                                        mat("sk")[p0:p0 + HD, hd * KEYS:(hd + 1) * KEYS], start=True, stop=True)
                last.then_inc(sc_ps, 1)

            def turn(u, j, q):
                for i in range(q * GROUP, (q + 1) * GROUP):
                    s = i % RING
                    pe.wait_ge(diag_ready, nth(u, SLOTS, j * 2 * RING + i + 1))
                    for n in range(2):
                        a = s * 2 * D + D + n * 512
                        d = i % DIAGS
                        last = T.matmul(acc[:, n * 512:(n + 1) * 512], diag[:, d * P:(d + 1) * P],
                                        ring[:, a:a + 512], start=False, stop=False, skip_group_check=True)
                    last.then_inc(row_used, 1)

            def clear_acc():
                for n in range(D // P):
                    last = T.matmul(acc[:, n * P:(n + 1) * P], sel[0:1, P:2 * P], ident[0:1, :], start=True,
                                    stop=False, skip_group_check=True)
                return last

            def close(u):
                if u is not UNITS + 1:
                    pe.wait_ge(x_done, u)
                    clear_acc()

            pe.wait_ge(ident_ready, 1)
            interleave(pe, {
                "pe.norm1": norm1, "pe.D0": lambda u: in_D(u, 0), "pe.D1": lambda u: in_D(u, 1),
                "pe.A0": lambda u: in_A(u, 2), "pe.A1": lambda u: in_A(u, 3, 4), "pe.Q": in_Q, "pe.lat": latents,
                "pe.B0": lambda u: in_B(u, 0), "pe.B1": lambda u: in_B(u, 1), "pe.qkT": qk_transposes,
                "pe.S": scores, "pe.C0": lambda u: in_C(u, 0), "pe.C1": lambda u: in_C(u, 1), "pe.PV": attend,
                "pe.bqk": mlstm_qk, "pe.cols": mlstm_cols, "pe.scores": mlstm_scores, "pe.num": mlstm_num,
                "pe.sg": spatial, "pe.ydT": conv_transposes, "pe.mixT": mix_transposes,
                "pe.out0": lambda u: w_out(u, 0), "pe.out1": lambda u: w_out(u, 1),
                "pe.out2": lambda u: w_out(u, 2), "pe.out3": lambda u: w_out(u, 3), "pe.norm2": norm2,
                "pe.q0": lambda u: queries(u, 0), "pe.q1": lambda u: queries(u, 1),
                "pe.q2": lambda u: queries(u, 2), "pe.q3": lambda u: queries(u, 3), "pe.sc": key_scores,
            }, turn, close, lambda u: None)

        @block.vector
        def _(dve):
            V_ = nc.vector
            links, of_setup = [0], [0]

            def link(u, ins, held=False):
                links[0] += 1
                ins.then_inc(dve_link, 1)
                dve.wait_ge(dve_link, nth(u, DVE_LINKS, of_setup[0] + links[0]))
                if held:
                    hold()

            def hold():
                dve.sem_inc(dve_hold, 1)

            def rsqrt(u, k, a, b):
                dve.wait_ge(rs_ready[k], nth(u, 1, 1))
                v, r, t = var[:, a:b], rs[:, a:b], rt[:, a:b]
                link(u, V_.tensor_tensor(t, r, r, ALU.mult))
                link(u, V_.tensor_tensor(t, t, v, ALU.mult))
                link(u, V_.tensor_scalar(t, t, -0.5, 1.5, ALU.mult, ALU.add))
                link(u, V_.tensor_tensor(r, r, t, ALU.mult))

            def sigmoid_mul(u, dst, e, other):
                link(u, V_.tensor_scalar(e, e, 1.0, None, ALU.add))
                link(u, V_.reciprocal(e, e))
                return V_.tensor_tensor(dst, other, e, ALU.mult)

            def heads(ap, n=HEADS):
                return ap.rearrange("p (h d) -> p h d", h=n)

            def of_half(ap, half):
                return ap.rearrange("p (j c d) -> p j c d", j=2, c=2)[:, :, half, :]

            def over(ap, n, d):
                return ap.unsqueeze(2).to_broadcast([P, n, d])

            def setup():
                before = links[0]
                dve.wait_ge(tables, 3)
                V_.tensor_copy(key_no[:, :], key_i[:, 0:P])
                V_.tensor_copy(qpos[:, :], qpos_i[:, :]).then_inc(tables_f, 1)
                dve.wait_ge(pos_in, 16)
                link(0, V_.tensor_copy(pos_f[:, :], pos_i[:, :]))
                two_pi = 2.0 * np.pi
                p1 = 6.28125
                p2 = float(np.round((two_pi - p1) * 2.0 ** 21) / 2.0 ** 21)
                p3 = float(two_pi - p1 - p2)
                a3 = ang[:, :].rearrange("p (b f) -> p b f", b=BLOCKS)
                link(0, V_.tensor_tensor(a3, pos_f[:, :].unsqueeze(2).to_broadcast([P, BLOCKS, HR]),
                                         freq[:, :].unsqueeze(1).to_broadcast([P, BLOCKS, HR]), ALU.mult))
                magic = 1.5 * 2.0 ** 23
                link(0, V_.tensor_scalar(ang_n[:, :], ang[:, :], float(1 / two_pi), None, ALU.mult))
                link(0, V_.tensor_scalar(ang_n[:, :], ang_n[:, :], magic, None, ALU.add))
                link(0, V_.tensor_scalar(ang_n[:, :], ang_n[:, :], -magic, None, ALU.add))
                for part in (p1, p2, p3):
                    link(0, V_.scalar_tensor_tensor(ang[:, :], ang_n[:, :], -part, ang[:, :], ALU.mult, ALU.add))
                pi = 3.1415925
                link(0, V_.tensor_scalar(ang[:, :], ang[:, :], pi, -pi, ALU.min, ALU.max))
                link(0, V_.scalar_tensor_tensor(ang_c[:, :], ang[:, :], -1.0, ang[:, :], ALU.mult, ALU.max))
                link(0, V_.tensor_scalar(ang_c[:, :], ang_c[:, :], -1.0, float(np.pi / 2), ALU.mult, ALU.add))
                V_.tensor_copy(rt[:, 0:1], ang[:, 0:1]).then_inc(ang_ready, 1)
                dve.wait_ge(rope_ready, 1)
                link(0, V_.tensor_copy(rt[:, 0:1], cs[:, 0:1]))
                link(0, V_.tensor_copy(rt[:, 0:1], cs[:, 0:1]))
                of_setup[0] = links[0] - before
                links[0] = before
                dve.wait_ge(tables_f, 1)

            def norm1(u):
                links[0] = 0
                if u is 0:
                    dve.wait_ge(x_in, 16)
                V_.tensor_copy(h[:, :], xs[:, ds((u % BLOCKS) * D, D)]).then_inc(h_ready, 1)

            def norm1_out(u):
                dve.wait_ge(ms_ready["norm1"], nth(u, 1, 1))
                link(u, V_.tensor_scalar(var[:, 0:1], ms[:, 0:1], EPS, None, ALU.add))
                rsqrt(u, "norm1", 0, 1)
                V_.tensor_scalar(xn[:, :], h[:, :], rs[:, 0:1], None, ALU.mult).then_inc(xn_ready, 1)

            def rotation(u):
                if u is 0:
                    setup()
                V_.tensor_copy(csb[:, :], cs[:, ds((u % BLOCKS) * ROPE, ROPE)])

            def attention_mask(u):
                for b in range(BLOCKS):
                    last = V_.tensor_scalar(mask[:, b * P:(b + 1) * P], key_no[:, :], float(b * P),
                                            qpos[:, ds(u, 1)], ALU.add, ALU.is_gt)
                link(u, last)
                link(u, V_.tensor_scalar(mask[:, :], mask[:, :], -1e30, None, ALU.mult))

            def gated(u):
                dve.wait_ge(params_in, nth(u // BLOCKS, 16 * 6, 16 * 6))
                dve.wait_ge(ebd_ready, nth(u, 1, 1))
                link(u, V_.tensor_scalar(ebd[:, :], ebd[:, :], 1.0, None, ALU.add))
                link(u, V_.reciprocal(ebd[:, :], ebd[:, :]))
                V_.tensor_tensor(glu[:, :].rearrange("p (j t) -> p j t", j=2)[:, :, KD - 1:],
                                 bank(0, 0, 2 * P).rearrange("p (j t) -> p j t", j=2),
                                 ebd[:, :].rearrange("p (j t) -> p j t", j=2), ALU.mult).then_inc(glu_ready, 1)

            def latents(u):
                dve.wait_ge(ms_ready["latents"], nth(u, 1, 1))
                link(u, V_.tensor_scalar(var[:, 1:3], ms[:, 1:3], EPS, None, ALU.add))
                kr = pA[:, QR + KVR:A1]
                V_.tensor_copy(heads(qk[:, :], 8)[:, HEADS:8, NOPE:],
                               kr.unsqueeze(1).to_broadcast([P, HEADS, ROPE]))
                rsqrt(u, "latents", 1, 3)
                V_.tensor_scalar(lat[:, 0:QR], pA[:, 0:QR], rs[:, 1:2], None, ALU.mult)
                V_.tensor_scalar(lat[:, QR:], pA[:, QR:QR + KVR], rs[:, 2:3], None, ALU.mult) \
                    .then_inc(lat_ready, 1)

            def qkv(u):
                dve.wait_ge(qk_evac, nth(u, 1, 1))
                q3 = heads(qk[:, :], 8)
                link(u, V_.tensor_tensor(qk_sq[:, :], qk[:, :], qk[:, :], ALU.mult))
                link(u, V_.tensor_reduce(rt[:, 3:11], heads(qk_sq[:, :], 8), AX.X, ALU.add))
                V_.tensor_scalar(var[:, 3:11], rt[:, 3:11], 1.0 / QK, EPS, ALU.mult, ALU.add) \
                    .then_inc(var_ready["qk"], 1)
                rsqrt(u, "qk", 3, 11)
                link(u, V_.tensor_tensor(q3, q3, over(rs[:, 3:11], 8, QK), ALU.mult))
                q4 = qk[:, :].rearrange("p (g h d) -> p g h d", g=2, h=HEADS)
                g4 = row("qkg").rearrange("p (g d) -> p g d", g=2).unsqueeze(2).to_broadcast([P, 2, HEADS, QK])
                link(u, V_.tensor_tensor(q4, q4, g4, ALU.mult))
                x1, x2 = q3[:, :, NOPE:NOPE + HR], q3[:, :, NOPE + HR:]
                cos = csb[:, 0:HR].unsqueeze(1).to_broadcast([P, 8, HR])
                sin = csb[:, HR:].unsqueeze(1).to_broadcast([P, 8, HR])
                r = [heads(rp[:, i * 8 * HR:(i + 1) * 8 * HR], 8) for i in range(4)]
                V_.tensor_tensor(r[0], x1, cos, ALU.mult)
                V_.tensor_tensor(r[1], x2, sin, ALU.mult)
                V_.tensor_tensor(r[2], x1, sin, ALU.mult)
                link(u, V_.tensor_tensor(r[3], x2, cos, ALU.mult))
                V_.tensor_tensor(x1, r[0], r[1], ALU.subtract)
                V_.tensor_tensor(x2, r[2], r[3], ALU.add).then_inc(qk_ready, 1)

            def scores(u):
                dve.wait_ge(S_ps, nth(u, 1, 1))
                b3 = heads(big[:, :])
                link(u, V_.tensor_tensor(b3, ps[:, 2 * 512:6 * 512].rearrange("p (h t) -> p h t", h=HEADS),
                                         mask[:, :].unsqueeze(1).to_broadcast([P, HEADS, SEQ]), ALU.add))
                link(u, V_.tensor_reduce(mx[:, :], b3, AX.X, ALU.max))
                V_.tensor_scalar(mx[:, :], mx[:, :], -float(QK ** -0.5), None, ALU.mult).then_inc(mx_ready, 1)

            def attended(u):
                dve.wait_ge(P_ready, nth(u, HEADS, HEADS))
                link(u, V_.reciprocal(rsum_p[:, :], psum_p[:, :]))
                dve.wait_ge(o_ps, nth(u, 1, 1))
                V_.tensor_tensor(heads(mix[:, 0:GW]), heads(bank(1, 0, GW)), over(rsum_p[:, :], HEADS, HD),
                                 ALU.mult)

            def mlstm_conv(u):
                dve.wait_ge(cbuf_ready, nth(u, 1, 1))
                c3 = cbuf[:, :].rearrange("p (j t) -> p j t", j=2)
                for k in range(KB):
                    for j in range(2):
                        src, dst = c3[:, j, k:k + P], yb[:, j * P:(j + 1) * P]
                        w = col("bw", j * KB + k)
                        if k == 0:
                            last = V_.tensor_scalar(dst, src, w, col("bb", j), ALU.mult, ALU.add)
                        else:
                            last = V_.scalar_tensor_tensor(dst, src, w, dst, ALU.mult, ALU.add)
                        if k < KB - 1 and j == 1:
                            link(u, last)
                last.then_inc(yb_ready, 1)
                dve.wait_ge(yb_ready, nth(u, 1, 1))
                V_.tensor_scalar(c3[:, :, 0:KB - 1], c3[:, :, P:P + KB - 1], carry[:, ds(u + 1, 1)], None, ALU.mult)

            def mlstm_gates(u):
                dve.wait_ge(pB_ready, nth(u, 1, 1))
                link(u, V_.tensor_tensor(gl[:, 8:16], pB[:, 512:520], row("gb"), ALU.add))
                z = gl[:, 12:16]
                V_.scalar_tensor_tensor(gl[:, 16:20], z, -1.0, z, ALU.mult, ALU.min).then_inc(negz_ready, 1)
                link(u, V_.tensor_scalar(gl[:, 32:36], z, 0.0, None, ALU.min))

            def mlstm_inputs(u):
                dve.wait_ge(softplus_ready, nth(u, 1, 1))
                V_.tensor_tensor(gl[:, 36:40], gl[:, 32:36], gl[:, 28:32], ALU.subtract).then_inc(gates_ready, 1)
                dve.wait_ge(eb_ready, nth(u, 1, 1))
                sigmoid_mul(u, xcT[:, :], eb[:, :], yb[:, :]).then_inc(xcT_ready, 1)

            def mlstm_rows(u):
                dve.wait_ge(gT_ps, nth(u, 1, 1))
                g = [gr[:, i * P:(i + 1) * P] for i in range(8)]
                link(u, V_.tensor_copy(gr[:, 0:2 * P], bank(5, 0, 2 * P, 0, HEADS)))
                link(u, V_.tensor_tensor_scan(g[2], ones4[:, :], g[1], 0.0, ALU.mult, ALU.add))
                link(u, V_.tensor_tensor(g[3], g[0], g[2], ALU.subtract))
                link(u, V_.tensor_tensor_scan(g[4], g[3], g[3], m_st[:, 0:1], ALU.max, ALU.max))
                V_.tensor_tensor(g[5], g[2], g[4], ALU.add).then_inc(rows_ready, 1)

            def mlstm_decay(u):
                dve.wait_ge(col_ps, nth(u, 1, 1))
                link(u, V_.tensor_copy(gc[:, 0:12], bank(5, 0, 12)))
                link(u, V_.tensor_copy(gc[:, 16:18], bank(5, 16, 18)))
                for hd in range(HEADS):
                    last = V_.tensor_scalar(Dm[:, hd * P:(hd + 1) * P], bank(2, hd * P, (hd + 1) * P),
                                            gc[:, hd:hd + 1], 0.0, ALU.subtract, ALU.max)
                last.then_inc(y_ready, 1)
                link(u, V_.tensor_copy(heads(v1[:, :])[:, :, 0:HD], heads(pB[:, 0:GW])))

            def mlstm_weigh(u):
                v = HD + 1
                dve.wait_ge(D_ready, nth(u, 1, 1))
                V_.tensor_tensor(heads(wgv[:, :]), heads(v1[:, :]),
                                 heads(Dm[:, :])[:, :, P - 1:P].to_broadcast([P, HEADS, v]),
                                 ALU.mult).then_inc(wgv_ready, 1)
                dve.wait_ge(SI_ps, nth(u, 1, 1))
                dve.wait_ge(wgv_ready, nth(u, 1, 1))
                for half, b in ((0, 5), (1, 3)):
                    d = of_half(Dm[:, :], half)
                    last = V_.tensor_tensor(d, d, bank(b, 0, 2 * P).rearrange("p (j t) -> p j t", j=2), ALU.mult)
                link(u, last)
                V_.tensor_tensor(heads(Dm[:, :]), heads(Dm[:, :]), tri[:, :].unsqueeze(1).to_broadcast([P, HEADS, P]),
                                 ALU.mult).then_inc(Wt_ready, 1)

            def mlstm_hidden(u):
                v = HD + 1
                for half, b in ((0, 4), (1, 2)):
                    last = V_.tensor_tensor(of_half(t1[:, :], half),
                                            bank(b, 0, 2 * v).rearrange("p (j d) -> p j d", j=2),
                                            over(gc[:, 4 + half:8:2], 2, v), ALU.mult)
                link(u, last)
                dve.wait_ge(num_ps, nth(u, 1, 1))
                link(u, V_.tensor_tensor(nd[:, :], bank(0, 0, HEADS * v), t1[:, :], ALU.add))
                n3 = heads(nd[:, :])
                d3 = n3[:, :, HD:v]
                link(u, V_.scalar_tensor_tensor(den[:, :].unsqueeze(2), d3, -1.0, d3, ALU.mult, ALU.max))
                link(u, V_.tensor_tensor(den[:, :], den[:, :], gc[:, 8:12], ALU.max))
                link(u, V_.reciprocal(den[:, :], den[:, :]))
                link(u, V_.tensor_tensor(heads(hh[:, :]), n3[:, :, 0:HD], over(den[:, :], HEADS, HD), ALU.mult))
                link(u, V_.tensor_tensor(yt[:, :], hh[:, :], hh[:, :], ALU.mult))
                link(u, V_.tensor_reduce(rt[:, 11:15], heads(yt[:, :]), AX.X, ALU.add))
                link(u, V_.tensor_scalar(var[:, 11:15], rt[:, 11:15], 1.0 / HD, EPS, ALU.mult, ALU.add))
                dve.wait_ge(st_ps, nth(u, 1, 1))
                for j in range(2):
                    for half in range(2):
                        p0 = half * HD
                        C = Cst[p0:p0 + HD, j * v:(j + 1) * v]
                        a = (j * 2 + half) * v
                        last = V_.scalar_tensor_tensor(C, C, gc[p0:p0 + HD, 16 + j:17 + j],
                                                       bank(1, a, a + v, p0, p0 + HD), ALU.mult, ALU.add)
                link(u, last)
                V_.tensor_scalar(Cst[:, :], Cst[:, :], carry[:, ds(u + 1, 1)], None, ALU.mult)
                link(u, V_.tensor_scalar(m_st[:, :], gr[:, 6 * P - 1:6 * P], carry[0:HEADS, ds(u + 1, 1)], None,
                                         ALU.mult))

            def gate_hidden(u):
                link(u, V_.tensor_tensor(heads(hh[:, :]), heads(hh[:, :]), over(rs[:, 11:15], HEADS, HD), ALU.mult))
                link(u, V_.tensor_tensor(hh[:, :], hh[:, :], row("hg"), ALU.mult))
                link(u, sigmoid_mul(u, mix[:, GW:2 * GW], exo[:, :], hh[:, :]))

            def spatial_stats(u):
                dve.wait_ge(pC_ready, nth(u, 1, 1))
                v_in = pC[:, GW:2 * GW]
                link(u, V_.bn_stats(bn[:, 0:6], v_in), held=True)
                link(u, V_.bn_aggr(mv[:, 0:2], bn[:, 0:6]))
                V_.tensor_scalar(var[:, 19:20], mv[:, 1:2], EPS, None, ALU.add).then_inc(var_ready["spatial"], 1)
                V_.tensor_tensor(heads(mat("ws")), heads(mat("ws")), tri[:, :].unsqueeze(1).to_broadcast([P, HEADS, P]),
                                 ALU.mult)

            def spatial(u):
                v_in = pC[:, GW:2 * GW]
                rsqrt(u, "spatial", 19, 20)
                link(u, V_.tensor_scalar(vn[:, :], v_in, mv[:, 0:1], rs[:, 19:20], ALU.subtract, ALU.mult))
                link(u, V_.tensor_tensor(vn[:, :], vn[:, :], row("cg"), ALU.mult))
                V_.tensor_tensor(vn[:, :], vn[:, :], row("cb"), ALU.add).then_inc(vn_ready, 1)

            def spatial_out(u):
                dve.wait_ge(sg_ps, nth(u, 1, 1))
                link(u, V_.tensor_tensor(heads(yt[:, :]), heads(bank(3, 0, GW)), over(col("bs"), HEADS, HD), ALU.add))
                link(u, V_.tensor_tensor(mix[:, 2 * GW:3 * GW], yt[:, :], pC[:, 0:GW], ALU.mult))

            def conv_taps(u, part):
                g3 = glu[:, :].rearrange("p (j t) -> p j t", j=2)
                if part == 0:
                    dve.wait_ge(glu_ready, nth(u, 1, 1))
                for k in range(KD * part // CONV_PARTS, KD * (part + 1) // CONV_PARTS):
                    for j in range(2):
                        src, dst = g3[:, j, k:k + P], yd[:, j * P:(j + 1) * P]
                        w = col("dw", j * KD + k)
                        if k == 0:
                            last = V_.tensor_scalar(dst, src, w, col("db", j), ALU.mult, ALU.add)
                        else:
                            last = V_.scalar_tensor_tensor(dst, src, w, dst, ALU.mult, ALU.add)
                        if k < KD - 1 and j == 1:
                            link(u, last)
                if part == CONV_PARTS - 1:
                    last.then_inc(yd_ready, 1)
                    dve.wait_ge(yd_ready, nth(u, 1, 1))
                    link(u, V_.tensor_scalar(g3[:, :, 0:KD - 1], g3[:, :, P:P + KD - 1], carry[:, ds(u + 1, 1)],
                                             None, ALU.mult))

            def conv_stats(u):
                dve.wait_ge(ydT_ps, nth(u, 1, 1))
                for hd in range(HEADS):
                    last = V_.bn_stats(bn[:, hd * 6:(hd + 1) * 6], bank(5, hd * HD, (hd + 1) * HD))
                link(u, last, held=True)
                for hd in range(HEADS):
                    last = V_.bn_aggr(mv[:, hd * 2:(hd + 1) * 2], bn[:, hd * 6:(hd + 1) * 6])
                link(u, last)
                m3 = mv[:, :].rearrange("p (h d) -> p h d", h=HEADS)
                V_.tensor_scalar(var[:, 15:19].unsqueeze(2), m3[:, :, 1:2], EPS, None, ALU.add) \
                    .then_inc(var_ready["late"], 1)

            def conv_norm(u):
                rsqrt(u, "late", 11, 19)
                for hd in range(HEADS):
                    last = V_.tensor_scalar(yt[:, hd * HD:(hd + 1) * HD], bank(5, hd * HD, (hd + 1) * HD),
                                            mv[:, 2 * hd:2 * hd + 1], rs[:, 15 + hd:16 + hd], ALU.subtract, ALU.mult)
                link(u, last)
                link(u, V_.tensor_tensor(yt[:, :], yt[:, :], row("dg"), ALU.mult))
                V_.tensor_tensor(yt[:, :], yt[:, :], row("db"), ALU.add).then_inc(yt_ready, 1)

            def swish(u):
                dve.wait_ge(eyt_ready, nth(u, 1, 1))
                sigmoid_mul(u, mix[:, 3 * GW:], vn[:, :], yt[:, :]).then_inc(mix_ready, 1)

            def norm2(u):
                dve.wait_ge(chunk_done, nth(u, NW, AFTER_OUT))
                V_.tensor_tensor(h[:, :], xs[:, ds((u % BLOCKS) * D, D)], ps[:, 2 * 512:4 * 512],
                                 ALU.add).then_inc(h2_ready, 1)
                dve.wait_ge(h2_ready, nth(u, 1, 1))
                hold()
                V_.tensor_copy(xs[:, ds((u % BLOCKS) * D, D)], h[:, :])

            def norm2_out(u):
                dve.wait_ge(ms_ready["norm2"], nth(u, 1, 1))
                link(u, V_.tensor_scalar(var[:, 20:21], ms[:, 3:4], EPS, None, ALU.add))
                rsqrt(u, "norm2", 20, 21)
                V_.scalar_tensor_tensor(xn[:, :], h[:, :], rs[:, 20:21], row("g2"), ALU.mult,
                                        ALU.mult).then_inc(xn_ready, 1)

            W = 2 * KEYS
            assert W == TOPK * TOPK
            KEY_LISTS = (KEYS, 2)
            SUM_LISTS = (TOPK * TOPK, 1)

            late_links = [0]

            def rlink(u, g, ins, held=False):
                if g == 0:
                    link(u, ins, held)
                else:
                    late_links[0] += 1
                    ins.then_inc(late_link, 1)
                    dve.wait_ge(late_link, nth(u, LATE_LINKS, late_links[0]))
                    if held:
                        hold()

            def count(g):
                return ROUTED[g][1] - ROUTED[g][0]

            def lists(g, n, per_head):
                lo, hi = ROUTED[g]
                return [(slice(i * n, (i + 1) * n), i * TOPK) for i in range(lo * per_head, hi * per_head)]

            def top8(u, g, n, per_head, s_out, at):
                for cols_, to in lists(g, n, per_head):
                    last = V_.max(s_out[:, to + at:to + at + 8], big[:, cols_])
                rlink(u, g, last, held=True)

            def places(u, g, n, per_head, s_out, i_out, at):
                for cols_, to in lists(g, n, per_head):
                    e = slice(to + at, to + at + 8)
                    last = V_.max_index(i_out[:, e], s_out[:, e], big[:, cols_])
                rlink(u, g, last, held=True)

            def without8(u, g, n, per_head, s_out):
                for cols_, to in lists(g, n, per_head):
                    last = V_.match_replace(big[:, cols_], s_out[:, to:to + 8], big[:, cols_], LOWEST)
                rlink(u, g, last, held=True)

            def route_a(u, g):
                if g == 1:
                    late_links[0] = 0
                dve.wait_ge(scs_ready, nth(u, 2, g + 1))
                hold()
                top8(u, g, *KEY_LISTS, s_top, 0)
                places(u, g, *KEY_LISTS, s_top, i_top, 0)

            def route_b(u, g):
                without8(u, g, *KEY_LISTS, s_top)
                top8(u, g, *KEY_LISTS, s_top, 8)

            def route_c(u, g):
                places(u, g, *KEY_LISTS, s_top, i_top, 8)
                s4 = of_routed(s_top, g, 2 * TOPK).rearrange("p (c h k) -> p c h k", h=count(g), c=2)
                grid = of_routed(big, g, W).rearrange("p (h a b) -> p h a b", h=count(g), a=TOPK)
                rlink(u, g, V_.tensor_tensor(grid, s4[:, 0, :, :].unsqueeze(3).to_broadcast([P, count(g), TOPK, TOPK]),
                                         s4[:, 1, :, :].unsqueeze(2).to_broadcast([P, count(g), TOPK, TOPK]), ALU.add),
                     held=True)
                top8(u, g, *SUM_LISTS, c_top, 0)
                places(u, g, *SUM_LISTS, c_top, ci_top, 0)

            def route_d(u, g):
                without8(u, g, *SUM_LISTS, c_top)
                top8(u, g, *SUM_LISTS, c_top, 8)
                c3 = heads(of_routed(c_top, g, TOPK), count(g))
                V_.tensor_tensor(heads(of_routed(eg, g, TOPK), count(g)), c3,
                                 c3[:, :, 0:1].to_broadcast([P, count(g), TOPK]),
                                 ALU.subtract).then_inc(top_ready, 1)
                places(u, g, *SUM_LISTS, c_top, ci_top, 8)
                ci = of_routed(ci_top, g, TOPK)
                V_.tensor_scalar(of_routed(c_hi, g, TOPK), ci, 4, None, ALU.logical_shift_right)
                V_.tensor_scalar(of_routed(c_lo, g, TOPK), ci, TOPK - 1, None, ALU.bitwise_and)
                rlink(u, g, V_.tensor_copy(of_routed(if_top, g, 2 * TOPK), of_routed(i_top, g, 2 * TOPK)))
                V_.tensor_copy(of_routed(f_hi, g, TOPK), of_routed(c_hi, g, TOPK))
                rlink(u, g, V_.tensor_copy(of_routed(f_lo, g, TOPK), of_routed(c_lo, g, TOPK)))

            def key_at(u, g, c, place, dst):
                i4 = of_routed(if_top, g, 2 * TOPK).rearrange("p (c h k) -> p c h k", h=count(g), c=2)
                work = of_routed(big, g, W).rearrange("p (s k) -> p s k", k=TOPK)
                work4 = of_routed(big, g, W).rearrange("p (h s k) -> p h s k", h=count(g), k=TOPK)
                n = count(g) * TOPK
                rlink(u, g, V_.tensor_tensor(work, of_routed(place, g, TOPK).unsqueeze(2).to_broadcast([P, n, TOPK]),
                                             key_no[:, 0:TOPK].unsqueeze(1).to_broadcast([P, n, TOPK]),
                                             ALU.is_equal))
                rlink(u, g, V_.tensor_tensor(work4, work4,
                                         i4[:, c, :, :].unsqueeze(2).to_broadcast([P, count(g), TOPK, TOPK]), ALU.mult))
                rlink(u, g, V_.tensor_reduce(of_routed(dst, g, TOPK), work, AX.X, ALU.add))

            def route_e(u, g):
                key_at(u, g, 0, f_hi, e1)

            def route_f(u, g):
                key_at(u, g, 1, f_lo, e2)
                n1, e, s_ = of_routed(e1, g, TOPK), heads(of_routed(eg, g, TOPK), count(g)), of_routed(gs, g, 1)
                rlink(u, g, V_.scalar_tensor_tensor(n1, n1, float(KEYS), of_routed(e2, g, TOPK), ALU.mult, ALU.add))
                rlink(u, g, V_.tensor_scalar(n1, n1, lbase[:, ds(u, 1)], None, ALU.add))
                indices_out(u, g)
                dve.wait_ge(eg_ready, nth(u, 2, g + 1))
                rlink(u, g, V_.tensor_reduce(s_, e, AX.X, ALU.add))
                rlink(u, g, V_.reciprocal(s_, s_))
                V_.tensor_tensor(e, e, over(s_, count(g), TOPK), ALU.mult).then_inc(eg_norm_ready, 1)
                if g == 0:
                    assert links[0] == DVE_LINKS, links
                else:
                    assert late_links[0] == LATE_LINKS, late_links

            def indices_out(u, g):
                if u is not 0:
                    dve.wait_ge(idx_ready, nth(u - 1, SLOTS // GROUP, ROUTED[g][1] * TOPK // GROUP))
                    hold()
                V_.tensor_copy(of_routed(eidx, g, TOPK), of_routed(e1, g, TOPK)).then_inc(eidx_ready, 1)
                dve.wait_ge(eidx_ready, nth(u, 2, g + 1))

            def turn(u, j, q):
                if q == 0:
                    dve.wait_ge(handover, nth(u, 1, 1))
                for i in range(q * GROUP, (q + 1) * GROUP):
                    s = i % RING
                    u_row = ring[:, s * 2 * D:s * 2 * D + D]
                    dve.wait_ge(row_in[s], nth(u, 16 * SLOTS // RING, j * 32 + (i // RING + 1) * 16))
                    V_.tensor_tensor_reduce(out=u_row, in0=xp[:, :], in1=u_row, scale=1.0, scalar=0.0, op0=ALU.mult,
                                            op1=ALU.add, accum_out=dots[:, s:s + 1]).then_inc(dot_done, 1)

            def close(u):
                dve.wait_ge(row_used, nth(u - 1, SLOTS, RING))
                r = xs[:, ds(((u + BLOCKS - 2) % BLOCKS) * D, D)]
                V_.tensor_tensor(r, r, acc[:, :], ALU.add).then_inc(x_done, 1)

            def handoff(u):
                if u is 0:
                    dve.wait_ge(x_rest_in, 16)
                dve.wait_ge(handover, nth(u, 1, 1))

            conv = {f"dve.conv{k}": (lambda u, k=k: conv_taps(u, k)) for k in range(CONV_PARTS)}
            interleave(dve, {
                **conv, "dve.norm1": norm1, "dve.xn1": norm1_out, "dve.xn2": norm2_out,
                "dve.setup": rotation, "dve.mask": attention_mask, "dve.glu": gated, "dve.lat": latents,
                "dve.bconv": mlstm_conv, "dve.qk": qkv, "dve.bgate": mlstm_gates, "dve.bin": mlstm_inputs,
                "dve.max": scores, "dve.oA": attended, "dve.vn0": spatial_stats, "dve.vn": spatial,
                "dve.rows": mlstm_rows, "dve.decay": mlstm_decay, "dve.weigh": mlstm_weigh,
                "dve.hidden": mlstm_hidden, "dve.swish0": conv_stats, "dve.sg": spatial_out,
                "dve.swish1": conv_norm, "dve.gateb": gate_hidden, "dve.swish2": swish, "dve.norm2": norm2,
                **{f"dve.r{g}{c}": (lambda u, g=g, f=f: f(u - 1 if g else u, g)) for g in range(2)
                   for c, f in zip("abcdef", (route_a, route_b, route_c, route_d, route_e, route_f))},
            }, turn, close, handoff)


def kernel(**inputs):
    import concourse.bacc as bacc
    from concourse.bass_utils import run_bass_kernel_spmd

    a = {k: np.asarray(v) for k, v in inputs.items()}
    L = DEPTH

    def chunked(w):
        return w.reshape(L, KC, P, -1).transpose(0, 2, 1, 3).reshape(L, -1)

    w_all = np.concatenate(
        [chunked(a["w_in"][:, :, lo:hi]) for lo, hi in IN_CHUNKS]
        + [chunked(a["w_out"][:, :, n * 256:(n + 1) * 256]) for n in range(4)]
        + [chunked(a["p_w_q"][:, :, n * 256:(n + 1) * 256]) for n in range(4)], axis=1)
    rows = np.concatenate(
        [a["norm2_g"], a["a_qn_g"], a["a_kn_g"], a["c_ln_g"], a["c_ln_b"],
         a["d_cn_g"].reshape(L, GW), a["d_cn_b"].reshape(L, GW), a["b_hn_g"].reshape(L, GW),
         a["b_b_i"], a["b_b_f"]], axis=1)

    def channels(v):
        n = v.shape[1]
        return v.reshape(L, n, 2, P).transpose(0, 3, 2, 1).reshape(L, P, 2 * n)

    cols = np.concatenate(
        [a["norm1_g"].reshape(L, KC, P).transpose(0, 2, 1), a["a_cq_g"].reshape(L, 2, P).transpose(0, 2, 1),
         a["a_ckv_g"].reshape(L, 1, P).transpose(0, 2, 1),
         channels(a["b_conv_w"]), channels(a["b_conv_b"][:, None]), channels(a["d_dw_w"]),
         channels(a["d_dw_b"][:, None]), a["c_b_s"].transpose(0, 2, 1)], axis=2)
    mats = np.concatenate(
        [a["a_w_uq"].reshape(L, 2, P, -1).transpose(0, 2, 1, 3).reshape(L, P, -1), a["a_w_ukv"],
         a["c_w_s"].transpose(0, 3, 1, 2).reshape(L, P, -1),
         a["p_sub_keys"].transpose(0, 2, 4, 1, 3).reshape(L, P, -1)], axis=2)

    def halves(w):
        return w.reshape(L, 2, 2, HD, HD).transpose(0, 2, 3, 1, 4).reshape(L, 2, HD, 2 * HD)

    uv = np.concatenate([a["p_u"], a["p_v"]], axis=2).reshape(L * EXPERTS, 2 * D)
    arrays = {"x": a["x"], "positions": a["positions"], "w_all": w_all, "rows": rows, "cols": cols, "mats": mats,
              "bq": halves(a["b_w_q"]), "bk": halves(a["b_w_k"]), "uv": uv}
    arrays = {k: np.ascontiguousarray(v) for k, v in arrays.items()}
    nc = bacc.Bacc("TRN2", target_bir_lowering=False, num_devices=1)
    args = [nc.dram_tensor(n, v.shape, mybir.dt.from_np(v.dtype), kind="ExternalInput").ap()
            for n, v in arrays.items()]
    args.append(nc.dram_tensor("out", a["x"].shape, F32, kind="ExternalOutput").ap())
    build(nc, *args)
    return run_bass_kernel_spmd(nc, [arrays], core_ids=[0]).results[0]["out"]
```
